# Optimizing a Trainium2 kernel written in Bass

```python
import jax, jax.numpy as jnp
from jax import lax
import numpy as np

D_MODEL = 1024
BATCH = 1
SEQ = 256
DEPTH = 1
DEC_BATCH = 8
DEC_SEQ = 4
PAST_LEN = 1024
PAGE_SIZE = 128

D_CONV = 512
CONV_WIDTH = 3
N_HEADS = 8
N_KV_HEADS = 2
HEAD_DIM = 64
IDX_HEADS = 8
IDX_DIM = 64
IDX_SCALE = (IDX_DIM ** -0.5) * (IDX_HEADS ** -0.5)
TOPK_MAX = 256
Q_BLOCK = 128
ROPE_THETA = 10000.0
PEER_HEADS = 8
PEER_KEYS = 128
PEER_N_EXPERTS = PEER_KEYS * PEER_KEYS
PEER_QDIM = 256
PEER_TOPK = 16
PEER_BLOCK = 128
N_MOD = 6
NORM_EPS = 1e-6
NEG_INF = -1e30
PROJ_WIDTH = 3 * D_CONV + (N_HEADS + 2 * N_KV_HEADS) * HEAD_DIM + IDX_HEADS * IDX_DIM + IDX_DIM + IDX_HEADS + 2 * D_MODEL

kernel_name = "hybrid_shortconv_dsa_peer_adaln_step"

def _rmsnorm(x, w):
    xf = x.astype(jnp.float32)
    y = xf * lax.rsqrt(jnp.mean(xf * xf, axis=-1, keepdims=True) + NORM_EPS)
    return (y * w.astype(jnp.float32)).astype(x.dtype)

def _modulate(h, shift, scale):
    return h * (1.0 + scale[:, None, :]) + shift[:, None, :]

def _adaln(c, w_ada, b_ada):
    mod = c @ w_ada + b_ada
    return jnp.split(mod, N_MOD, axis=-1)

def _rope(x, pos):
    d = x.shape[-1]
    half = d // 2
    freqs = ROPE_THETA ** (-jnp.arange(half, dtype=jnp.float32) / half)
    ang = pos.astype(jnp.float32)[:, None] * freqs[None, :]
    cos = jnp.cos(ang)[:, None, :]
    sin = jnp.sin(ang)[:, None, :]
    xf = x.astype(jnp.float32)
    x1, x2 = xf[..., :half], xf[..., half:]
    return jnp.concatenate([x1 * cos - x2 * sin, x2 * cos + x1 * sin], axis=-1).astype(x.dtype)

def _split_proj(z):
    sizes = (D_CONV, D_CONV, D_CONV, N_HEADS * HEAD_DIM, N_KV_HEADS * HEAD_DIM, N_KV_HEADS * HEAD_DIM,
             IDX_HEADS * IDX_DIM, IDX_DIM, IDX_HEADS, D_MODEL, D_MODEL)
    parts, start = [], 0
    for s in sizes:
        parts.append(z[..., start:start + s])
        start += s
    return parts

def _mixer_inputs(x, shift, scale, norm_w, w_in, q_norm_w, k_norm_w, pos):
    h = _modulate(_rmsnorm(x, norm_w), shift, scale)
    z = jnp.einsum('btd,dp->btp', h, w_in)
    xin, b_gate, c_gate, q, k, v, qi, ki, wi, g_a, g_b = _split_proj(z)
    bsz, t = x.shape[0], x.shape[1]
    u = c_gate * xin
    q = _rope(_rmsnorm(q.reshape(bsz, t, N_HEADS, HEAD_DIM), q_norm_w), pos)
    k = _rope(_rmsnorm(k.reshape(bsz, t, N_KV_HEADS, HEAD_DIM), k_norm_w), pos)
    v = v.reshape(bsz, t, N_KV_HEADS, HEAD_DIM)
    qi = _rope(qi.reshape(bsz, t, IDX_HEADS, IDX_DIM), pos)
    ki = _rope(ki[:, :, None, :], pos)[:, :, 0, :]
    wi = wi * IDX_SCALE
    return u, b_gate, q, k, v, qi, ki, wi, g_a, g_b

def _causal_conv(u, past, conv_w):
    full = jnp.concatenate([past.astype(u.dtype), u], axis=1)
    t = u.shape[1]
    y = conv_w[CONV_WIDTH - 1] * full[:, CONV_WIDTH - 1:CONV_WIDTH - 1 + t]
    for j in range(CONV_WIDTH - 1):
        y = y + conv_w[j] * full[:, j:j + t]
    return y, full[:, full.shape[1] - (CONV_WIDTH - 1):]

def _index_select(qi, wi, pos_q, ki, pos_k, topk):
    s = jnp.einsum('qhd,ld->qhl', qi.astype(jnp.float32), ki.astype(jnp.float32))
    score = jnp.einsum('qh,qhl->ql', wi.astype(jnp.float32), jax.nn.relu(s))
    score = jnp.where(pos_k[None, :] <= pos_q[:, None], score, NEG_INF)
    _, sel = lax.top_k(score, topk)
    return sel

def _sparse_attend(q, ks, vs, valid):
    nq = q.shape[0]
    qg = q.reshape(nq, N_KV_HEADS, N_HEADS // N_KV_HEADS, HEAD_DIM).astype(jnp.float32)
    logits = jnp.einsum('qngd,qsnd->qngs', qg, ks.astype(jnp.float32)) * (HEAD_DIM ** -0.5)
    logits = jnp.where(valid[:, None, None, :], logits, NEG_INF)
    p = jax.nn.softmax(logits, axis=-1)
    o = jnp.einsum('qngs,qsnd->qngd', p, vs.astype(jnp.float32))
    return o.reshape(nq, N_HEADS * HEAD_DIM).astype(q.dtype)

def _prompt_attention(q, k, v, qi, ki, wi, pos):
    bsz, t = q.shape[0], q.shape[1]
    nb = t // Q_BLOCK
    topk = min(TOPK_MAX, t // 4)

    def one_block(idx):
        b = idx // nb
        start = (idx % nb) * Q_BLOCK
        row = lambda a: lax.dynamic_index_in_dim(a, b, 0, keepdims=False)
        blk = lambda a: lax.dynamic_slice_in_dim(row(a), start, Q_BLOCK, 0)
        qb, qib, wib = blk(q), blk(qi), blk(wi)
        pos_q = lax.dynamic_slice_in_dim(pos, start, Q_BLOCK, 0)
        kb, vb, kib = row(k), row(v), row(ki)
        sel = _index_select(qib, wib, pos_q, kib, pos, topk)
        valid = pos[sel] <= pos_q[:, None]
        return _sparse_attend(qb, kb[sel], vb[sel], valid)

    out = lax.map(one_block, jnp.arange(bsz * nb, dtype=jnp.int32))
    return out.reshape(bsz, t, N_HEADS * HEAD_DIM)

def _sample_attention(q, k_new, v_new, qi, ki_new, wi, pos_q, pool_k, pool_v, pool_ki, page_table):
    db, ds = q.shape[0], q.shape[1]
    past = page_table.shape[1] * PAGE_SIZE
    total = past + ds
    topk = min(TOPK_MAX, total // 4)
    ki_past = pool_ki[page_table].reshape(db, past, IDX_DIM)
    ki_all = jnp.concatenate([ki_past, ki_new.astype(ki_past.dtype)], axis=1)
    pos_k = jnp.arange(total, dtype=jnp.int32)
    sel = jax.vmap(lambda a, w, kk: _index_select(a, w, pos_q, kk, pos_k, topk))(qi, wi, ki_all)
    in_past = sel < past
    ps = jnp.minimum(sel, past - 1)
    phys = jnp.take_along_axis(page_table, (ps // PAGE_SIZE).reshape(db, -1), axis=1).reshape(sel.shape)
    rows = phys * PAGE_SIZE + ps % PAGE_SIZE
    ns = jnp.clip(sel - past, 0, ds - 1)
    take_new = jax.vmap(lambda arr, idx: arr[idx])
    ks = jnp.where(in_past[..., None, None], pool_k.reshape(-1, N_KV_HEADS, HEAD_DIM)[rows], take_new(k_new, ns))
    vs = jnp.where(in_past[..., None, None], pool_v.reshape(-1, N_KV_HEADS, HEAD_DIM)[rows], take_new(v_new, ns))
    valid = sel <= pos_q[None, :, None]
    return jax.vmap(_sparse_attend)(q, ks, vs, valid)

def _peer(h, w_q, sub_keys, u_tab, v_tab):
    t = h.shape[0]
    pad = (-t) % PEER_BLOCK
    blocks = jnp.pad(h, ((0, pad), (0, 0))).reshape(-1, PEER_BLOCK, D_MODEL)

    def block_fn(hb):
        q = (hb @ w_q).reshape(PEER_BLOCK, PEER_HEADS, 2, PEER_QDIM // 2).astype(jnp.float32)
        s = jnp.einsum('thpd,phkd->thpk', q, sub_keys.astype(jnp.float32))
        s1, i1 = lax.top_k(s[:, :, 0], PEER_TOPK)
        s2, i2 = lax.top_k(s[:, :, 1], PEER_TOPK)
        cand = (s1[..., :, None] + s2[..., None, :]).reshape(PEER_BLOCK, PEER_HEADS, PEER_TOPK * PEER_TOPK)
        cidx = (i1[..., :, None] * PEER_KEYS + i2[..., None, :]).reshape(PEER_BLOCK, PEER_HEADS, PEER_TOPK * PEER_TOPK)
        top_s, top_pos = lax.top_k(cand, PEER_TOPK)
        e = jnp.take_along_axis(cidx, top_pos, axis=-1)
        g = jax.nn.softmax(top_s, axis=-1)
        act = jax.nn.gelu(jnp.einsum('thkd,td->thk', u_tab[e], hb).astype(jnp.float32))
        return jnp.einsum('thk,thkd->td', (g * act).astype(hb.dtype), v_tab[e])

    return lax.map(block_fn, blocks).reshape(-1, D_MODEL)[:t]

def _finish_layer(x, a_pre, attn_o, g_a, g_b, gate1, shift2, scale2, gate2, w_conv_out, w_attn_out, w_out,
                  norm2_w, peer_w_q, peer_sub_keys, peer_u, peer_v):
    y_a = a_pre @ w_conv_out
    y_b = attn_o @ w_attn_out
    mix = jax.nn.sigmoid(g_a) * y_a + jax.nn.sigmoid(g_b) * y_b
    x = x + gate1[:, None, :] * (mix @ w_out)
    h2 = _modulate(_rmsnorm(x, norm2_w), shift2, scale2)
    y = _peer(h2.reshape(-1, D_MODEL), peer_w_q, peer_sub_keys, peer_u, peer_v).reshape(x.shape)
    return x + gate2[:, None, :] * y

def setup_inputs(seed: int = 0) -> dict:
    key = jax.random.key(seed)
    ks = jax.random.split(key, 32)
    f32 = jnp.float32
    n_pages = PAST_LEN // PAGE_SIZE
    n_phys = (DEC_BATCH * n_pages * 5) // 4

    def nrm(k, shape, scale):
        return jax.random.normal(k, shape, f32) * scale

    page_table = jax.random.permutation(ks[8], n_phys)[:DEC_BATCH * n_pages].reshape(DEC_BATCH, n_pages).astype(jnp.int32)
    return {
        "x_prompt": nrm(ks[0], (BATCH, SEQ, D_MODEL), 1.0),
        "x_sample": nrm(ks[1], (DEC_BATCH, DEC_SEQ, D_MODEL), 1.0),
        "cache_k": nrm(ks[4], (DEPTH, n_phys, PAGE_SIZE, N_KV_HEADS, HEAD_DIM), 1.0),
        "cache_v": nrm(ks[5], (DEPTH, n_phys, PAGE_SIZE, N_KV_HEADS, HEAD_DIM), 1.0),
        "cache_kidx": nrm(ks[6], (DEPTH, n_phys, PAGE_SIZE, IDX_DIM), 1.0),
        "state_conv": nrm(ks[7], (DEPTH, DEC_BATCH, CONV_WIDTH - 1, D_CONV), 1.0),
        "page_table": page_table,
        "c_prompt": nrm(ks[2], (BATCH, D_MODEL), 1.0),
        "c_sample": nrm(ks[3], (DEC_BATCH, D_MODEL), 1.0),
        "w_ada": nrm(ks[9], (DEPTH, D_MODEL, N_MOD * D_MODEL), 0.1 * D_MODEL ** -0.5),
        "b_ada": nrm(ks[10], (DEPTH, N_MOD * D_MODEL), 0.01),
        "norm1_w": 1.0 + nrm(ks[11], (DEPTH, D_MODEL), 0.01),
        "w_in": nrm(ks[12], (DEPTH, D_MODEL, PROJ_WIDTH), D_MODEL ** -0.5),
        "conv_w": nrm(ks[13], (DEPTH, CONV_WIDTH, D_CONV), CONV_WIDTH ** -0.5),
        "q_norm_w": 1.0 + nrm(ks[14], (DEPTH, HEAD_DIM), 0.01),
        "k_norm_w": 1.0 + nrm(ks[15], (DEPTH, HEAD_DIM), 0.01),
        "w_conv_out": nrm(ks[16], (DEPTH, D_CONV, D_MODEL), D_CONV ** -0.5),
        "w_attn_out": nrm(ks[17], (DEPTH, N_HEADS * HEAD_DIM, D_MODEL), (N_HEADS * HEAD_DIM) ** -0.5),
        "w_out": nrm(ks[18], (DEPTH, D_MODEL, D_MODEL), D_MODEL ** -0.5),
        "norm2_w": 1.0 + nrm(ks[19], (DEPTH, D_MODEL), 0.01),
        "peer_w_q": nrm(ks[20], (DEPTH, D_MODEL, PEER_HEADS * PEER_QDIM), D_MODEL ** -0.5),
        "peer_sub_keys": nrm(ks[21], (DEPTH, 2, PEER_HEADS, PEER_KEYS, PEER_QDIM // 2), (PEER_QDIM // 2) ** -0.5),
        "peer_u": nrm(ks[22], (DEPTH, PEER_N_EXPERTS, D_MODEL), D_MODEL ** -0.5),
        "peer_v": nrm(ks[23], (DEPTH, PEER_N_EXPERTS, D_MODEL), PEER_HEADS ** -0.5),
    }

def reference(x_prompt, x_sample, cache_k, cache_v, cache_kidx, state_conv, page_table, c_prompt, c_sample,
              w_ada, b_ada, norm1_w, w_in, conv_w, q_norm_w, k_norm_w, w_conv_out, w_attn_out, w_out,
              norm2_w, peer_w_q, peer_sub_keys, peer_u, peer_v):
    pos_p = jnp.arange(SEQ, dtype=jnp.int32)
    pos_s = PAST_LEN + jnp.arange(DEC_SEQ, dtype=jnp.int32)
    xp, xs = x_prompt, x_sample
    kp_l, vp_l, kip_l, cp_l = [], [], [], []
    ks_l, vs_l, kis_l, cs_l = [], [], [], []
    for layer in range(DEPTH):
        sh1, sc1, g1, sh2, sc2, g2 = _adaln(c_prompt, w_ada[layer], b_ada[layer])
        u, bg, q, k, v, qi, ki, wi, ga, gb = _mixer_inputs(xp, sh1, sc1, norm1_w[layer], w_in[layer],
                                                           q_norm_w[layer], k_norm_w[layer], pos_p)
        y_conv, conv_p = _causal_conv(u, jnp.zeros((xp.shape[0], CONV_WIDTH - 1, D_CONV), u.dtype), conv_w[layer])
        attn = _prompt_attention(q, k, v, qi, ki, wi, pos_p)
        xp = _finish_layer(xp, bg * y_conv, attn, ga, gb, g1, sh2, sc2, g2, w_conv_out[layer], w_attn_out[layer],
                           w_out[layer], norm2_w[layer], peer_w_q[layer], peer_sub_keys[layer], peer_u[layer], peer_v[layer])
        kp_l.append(k); vp_l.append(v); kip_l.append(ki); cp_l.append(conv_p)
        sh1, sc1, g1, sh2, sc2, g2 = _adaln(c_sample, w_ada[layer], b_ada[layer])
        u, bg, q, k, v, qi, ki, wi, ga, gb = _mixer_inputs(xs, sh1, sc1, norm1_w[layer], w_in[layer],
                                                           q_norm_w[layer], k_norm_w[layer], pos_s)
        y_conv, conv_s = _causal_conv(u, state_conv[layer], conv_w[layer])
        attn = _sample_attention(q, k, v, qi, ki, wi, pos_s, cache_k[layer], cache_v[layer], cache_kidx[layer], page_table)
        xs = _finish_layer(xs, bg * y_conv, attn, ga, gb, g1, sh2, sc2, g2, w_conv_out[layer], w_attn_out[layer],
                           w_out[layer], norm2_w[layer], peer_w_q[layer], peer_sub_keys[layer], peer_u[layer], peer_v[layer])
        ks_l.append(k); vs_l.append(v); kis_l.append(ki); cs_l.append(conv_s)
    k_prompt, v_prompt = jnp.stack(kp_l), jnp.stack(vp_l)
    kidx_prompt, conv_prompt = jnp.stack(kip_l), jnp.stack(cp_l)
    k_sample, v_sample = jnp.stack(ks_l), jnp.stack(vs_l)
    kidx_sample, conv_sample = jnp.stack(kis_l), jnp.stack(cs_l)
    return (xp, xs, k_prompt, v_prompt, kidx_prompt, conv_prompt, k_sample, v_sample, kidx_sample, conv_sample)


_drawn_inputs = setup_inputs


def setup_inputs(seed=0):
    import zlib

    import numpy as np

    out = dict(_drawn_inputs(seed))
    spreads = {}
    factors = {'cache_k': 8.0,
     'cache_v': 8.0,
     'cache_kidx': 8.0,
     'b_ada': 2.803,
     'norm1_w': 3.943,
     'q_norm_w': 8.0,
     'k_norm_w': 5.915,
     'w_attn_out': 3.851,
     'norm2_w': 8.0,
     'peer_w_q': 3.21,
     'peer_sub_keys': 3.211,
     'peer_u': 3.572,
     'peer_v': 3.212}
    for name, (base, spread) in spreads.items():
        noise = np.random.default_rng([zlib.crc32(name.encode()), seed]).standard_normal(out[name].shape)
        drawn = base * np.exp(spread * noise) if base else spread * noise
        out[name] = __import__('jax').numpy.asarray(drawn.astype(out[name].dtype))
    for name, factor in factors.items():
        out[name] = (out[name] * factor).astype(out[name].dtype)
    return out
```

```python
from contextlib import ExitStack

import numpy as np

import concourse.bass as bass
from concourse import mybir

F32 = mybir.dt.float32
BF16 = mybir.dt.bfloat16
I32 = mybir.dt.int32
U32 = mybir.dt.uint32
ALU = mybir.AluOpType
ACT = mybir.ActivationFunctionType
AX = mybir.AxisListType.X

P = 128
D = 1024
DC = D // P
SEQ = 256
NB, NS = 8, 4
NSM = NB * NS
TOK = SEQ + NSM
PAST, PAGE = 1024, 128
NPG = PAST // PAGE
NPHYS = 80
CONV = 512
CC = CONV // P
NH, NKV, HD = 8, 2, 64
NG = NH // NKV
TOPK_P, TOPK_S = SEQ // 4, 256
IDX_SCALE = (64 ** -0.5) * (8 ** -0.5)
QSCALE = HD ** -0.5
EPS = 1e-6
NEG = -1e30
TAKEN = -3e38
NKEY = PAST + NSM
PH, PK, PTOP = 8, 128, 16
ROWS = [P, P, NSM]
COLS = [0, P, SEQ]
SLOTS = [PH * PTOP, PH * PTOP, PH * PTOP // 4]

C_XIN, C_ATT, C_Q, C_K, C_V, C_QI, C_KI, C_WI, C_GA = 0, 1536, 1536, 2048, 2176, 2304, 2816, 2880, 2888
ZW = C_GA - C_ATT
Z_K, Z_V, Z_QI, Z_KI, Z_WI = C_K - C_ATT, C_V - C_ATT, C_QI - C_ATT, C_KI - C_ATT, C_WI - C_ATT

CONST_PARTS = [("ident", P), ("cos", 3 * 32), ("sin", 3 * 32), ("causal0", P), ("causal1", 2 * P), ("newbias", NSM),
               ("rep", 2 * P), ("repT", 2 * NSM), ("headsel", NH), ("sum4", NSM), ("iota", PTOP)]


def const_table():
    t = {n: np.zeros((P, w), np.float32) for n, w in CONST_PARTS}
    t["ident"][:] = np.eye(P, dtype=np.float32)
    freq = (np.float32(10000.0) ** (-np.arange(32, dtype=np.float32) / np.float32(32))).astype(np.float32)
    row = np.arange(P)
    for tile, pos in enumerate([row, row + P, PAST + row % NS]):
        ang = pos.astype(np.float32)[:, None] * freq[None, :]
        t["cos"][:, 32 * tile:32 * tile + 32] = np.cos(ang)
        t["sin"][:, 32 * tile:32 * tile + 32] = np.sin(ang)
    key = np.arange(2 * P)
    t["causal0"][:] = np.where(key[None, :P] <= row[:, None], 0.0, NEG)
    t["causal1"][:] = np.where(key[None, :] <= row[:, None] + P, 0.0, NEG)
    tok = np.arange(NSM)
    t["newbias"][:NSM] = np.where((tok[None, :] // NS == tok[:, None] // NS) & (tok[None, :] <= tok[:, None]), 0.0, NEG)
    for g in range(2):
        src = (4 * g + row // 32) * NS + row % NS
        t["rep"][src, P * g + row] = 1.0
        t["repT"][row, NSM * g + src] = 1.0
    t["headsel"][row, (row // NS) % NH] = 1.0
    t["sum4"][row, row % NSM] = 1.0
    t["iota"][:] = np.arange(PTOP)[None, :]
    return np.concatenate([t[n] for n, _ in CONST_PARTS], axis=1)


INPUTS = ["x_prompt", "x_sample", "cache_k", "cache_v", "cache_kidx", "state_conv", "page_table", "c_prompt", "c_sample",
          "w_ada", "b_ada", "norm1_w", "w_in", "conv_w", "q_norm_w", "k_norm_w", "w_conv_out", "w_attn_out", "w_out",
          "norm2_w", "peer_w_q", "peer_sub_keys", "peer_u", "peer_v"]
LAYERED = set(INPUTS) - {"x_prompt", "x_sample", "page_table", "c_prompt", "c_sample"}
OUTPUTS = [("y_prompt", (1, SEQ, D), ("a t d -> (a t) d", False)), ("y_sample", (NB, NS, D), ("b s d -> (b s) d", False)),
           ("k_prompt", (1, 1, SEQ, NKV, HD), ("l b t n d -> (l b t) (n d)", False)),
           ("v_prompt", (1, 1, SEQ, NKV, HD), ("l b t n d -> (l b t) (n d)", False)),
           ("kidx_prompt", (1, 1, SEQ, HD), ("l b t d -> (l b t) d", False)),
           ("conv_prompt", (1, 1, 2, CONV), ("l b t d -> (l b t) d", False)),
           ("k_sample", (1, NB, NS, NKV, HD), ("l b t n d -> (l b t) (n d)", False)),
           ("v_sample", (1, NB, NS, NKV, HD), ("l b t n d -> (l b t) (n d)", False)),
           ("kidx_sample", (1, NB, NS, HD), ("l b t d -> (l b t) d", False)),
           ("conv_sample", (1, NB, 2, CONV), (None, True))]


class Lane:

    def __init__(self, eng, own):
        self.eng, self.own, self.count = eng, own, {}

    def tell(self, ins, sem=None, wait=True):
        sem = self.own if sem is None else sem
        self.count[id(sem)] = self.count.get(id(sem), 0) + 1
        ins.then_inc(sem, 1)
        if wait:
            self.eng.wait_ge(sem, self.count[id(sem)])


class Banks:

    def __init__(self, banks, full, free):
        self.banks, self.full, self.free, self.n = banks, full, free, 0

    def open(self, pe):
        if self.n >= len(self.banks):
            pe.wait_ge(self.free, self.n - len(self.banks) + 1)
        self.n += 1
        return self.banks[(self.n - 1) % len(self.banks)]

    def close(self, mm, n=1):
        mm.then_inc(self.full, n)

    def take(self, eng):
        eng.wait_ge(self.full, self.n + 1)
        self.n += 1
        return self.banks[(self.n - 1) % len(self.banks)]


def layer_program(nc, x_prompt, x_sample, cache_k, cache_v, cache_kidx, state_conv, page_table, c_prompt, c_sample,
                  w_ada, b_ada, norm1_w, w_in, conv_w, q_norm_w, k_norm_w, w_conv_out, w_attn_out, w_out, norm2_w,
                  peer_w_q, peer_sub_keys, peer_u, peer_v, consts,
                  y_prompt, y_sample, k_prompt, v_prompt, kidx_prompt, conv_prompt, k_sample, v_sample, kidx_sample,
                  conv_sample):
    with ExitStack() as ctx:
        def sb(name, shape, dt=F32):
            return ctx.enter_context(nc.sbuf_tensor(name, shape, dt))

        def sem(name):
            return ctx.enter_context(nc.semaphore(name))

        WSLOT = DC * 512
        NW = 2
        UR = 8
        ctab = sb("ctab", [P, sum(w for _, w in CONST_PARTS)])
        cv, at = {}, 0
        for n, w in CONST_PARTS:
            cv[n] = ctab[:, at:at + w]
            at += w
        ident = cv["ident"]
        ident_bf = sb("ident_bf", [P, P], BF16)
        rep_bf = sb("rep_bf", [NSM, 2 * P], BF16)
        ones = sb("ones", [P, P])
        smallT = sb("smallT", [P, 76])
        qkw = sb("qkw", [P, P])
        cT = sb("cT", [P, DC, 9])
        modT = sb("modT", [P, 48, 9])
        ab = sb("ab", [P, DC, 9])
        xT = sb("xT", [P, DC, TOK])
        hT = sb("hT", [P, DC, 3 * P])
        oT = sb("oT", [P, NG, TOK])
        rstd = sb("rstd", [P, TOK])
        stateT = sb("stateT", [P, CC, NB * 2])
        pages = sb("pages", [1, NB * NPG], I32)

        big = sb("big", [P, NB * NPG * P + 2 * NPG * P + 2 * NPG * 64 + NW * WSLOT])
        o = NB * NPG * P
        vpages = big[:, 0:o].rearrange("p (g d) -> p g d", d=P)
        kpages = big[:, o:o + 2 * NPG * P].rearrange("p (r g d) -> p r g d", r=2, d=P)
        o += 2 * NPG * P
        ipages = big[:, o:o + 2 * NPG * 64].rearrange("p (r g d) -> p r g d", r=2, d=64)
        o += 2 * NPG * 64
        wring = [big[:, o + i * WSLOT:o + (i + 1) * WSLOT] for i in range(NW)]
        urows = [big[:, i * D:(i + 1) * D] for i in range(UR)]
        vrows = [big[:, (UR + i) * D:(UR + i + 1) * D] for i in range(UR)]
        cand = big[:, 2 * UR * D:2 * UR * D + PH * 256].rearrange("p (h i j) -> p h i j", h=PH, i=PTOP)
        assert 2 * UR * D + PH * 256 <= o + NW * WSLOT
        onehot = hT[:, :, :].rearrange("p c t -> p (c t)")[:, 0:PH * 256].rearrange("p (h i j) -> p h i j", h=PH, i=PTOP)

        zall = sb("zall", [P, 32 * P])
        zbuf = zall[:, 0:3 * ZW].rearrange("p (t z) -> p t z", z=ZW)
        subraw = zall[:, 0:16 * P].rearrange("p (j d) -> p j d", d=P)
        subT = zall[:, 16 * P:32 * P].rearrange("p (j k) -> p j k", k=P)

        r5 = sb("r5", [P, 16 * TOK + 12 * TOK + CC * (SEQ + 2) + CC * NB * 6])
        sig = r5[:, 0:16 * TOK].rearrange("p (j t) -> p j t", t=TOK)
        o = 16 * TOK
        bufX = r5[:, o:o + 4 * TOK].rearrange("p (j t) -> p j t", t=TOK)
        bufB = r5[:, o + 4 * TOK:o + 8 * TOK].rearrange("p (j t) -> p j t", t=TOK)
        bufC = r5[:, o + 8 * TOK:o + 12 * TOK].rearrange("p (j t) -> p j t", t=TOK)
        mixT = r5[:, o + 8 * TOK:o + 16 * TOK].rearrange("p (j t) -> p j t", t=TOK)
        o += 12 * TOK
        uP = r5[:, o:o + CC * (SEQ + 2)].rearrange("p (j t) -> p j t", t=SEQ + 2)
        o += CC * (SEQ + 2)
        uS = r5[:, o:o + CC * NB * 6].rearrange("p (j b t) -> p j b t", b=NB, t=6)
        aT = bufB
        qpT = r5[:, 0:16 * 3 * P].rearrange("p (j t) -> p j t", t=3 * P)
        ssb = r5[:, 48 * P:64 * P].rearrange("p (j k) -> p j k", k=P)
        gspread = r5[:, 9288 - 16 * P:9288]
        QIs = r5[:, 0:2 * NB * 32].rearrange("p (v r) -> p v r", v=2)
        dots = r5[:, 64 * P:67 * P].rearrange("p (t s) -> p t s", t=3)
        eidx = r5[:, 67 * P:70 * P].bitcast(I32).rearrange("p (t s) -> p t s", t=3)
        tails = sb("tails", [P, CC, 2 + NB * 2])

        R6 = 9 * D
        r6 = sb("r6", [P, R6])
        cut = [0]

        def part(n, start=None):
            if start is not None:
                cut[0] = start
            v = r6[:, cut[0]:cut[0] + n]
            cut[0] += n
            assert cut[0] <= R6, cut[0]
            return v
        xin = part(3 * D, 0).rearrange("p (t d) -> p t d", d=D)
        crow = part(D)
        srow = part(CONV)
        sq = part(DC * TOK)
        smallrows = part(P)[0:76]
        qkrow = part(P)
        qTz = part(NH * P, 0).rearrange("p (h t) -> p h t", t=P)
        qiTz = part(NH * P).rearrange("p (h t) -> p h t", t=P)
        probs = part(NH * 2 * P)
        probsT = part(NH * 2 * P)
        relu = part(2 * 2 * P)
        rope = [part(10 * 32) for _ in range(2)]
        scP = part(2 * P)
        workP = part(2 * P)
        orow = part(4 * P)
        kidup = part(P)
        mbP = part(P).bitcast(BF16)
        reluS = part(2 * NKEY, 0).rearrange("p (g k) -> p g k", k=NKEY)
        kbT = part(2 * PAST).rearrange("p (r k) -> p r k", k=PAST)
        ibT = part(2 * 4 * P).rearrange("p (r k) -> p r k", k=4 * P)
        scS = part(NKEY)
        workS = part(NKEY)
        probsST = part(NPG * P + P)
        mbS = part(NKEY // 2).bitcast(BF16)[0:NSM]
        probsS = part(NKEY, 0)
        tailrows = part(CONV, 0)[0:2 + NB * 2]
        x1tok = part(3 * D, 0).rearrange("p (t d) -> p t d", d=D)
        h2tok = part(3 * D).rearrange("p (t d) -> p t d", d=D)
        g2tok = part(2 * D).rearrange("p (t d) -> p t d", d=D)
        yout = part(D)
        kT = sb("kT", [P, TOK])
        kiT = sb("kiT", [P, TOK])
        wis = sb("wis", [P, 3, NH])
        stat = sb("stat", [P, 64])
        best = sb("best", [P, 8])
        nmax = sb("nmax", [P, NH])
        rsum = sb("rsum", [P, 3, NH])
        rinv = sb("rinv", [P, NH])
        Qs = sb("Qs", [P, NB * 32])
        wrow = sb("wrow", [P, 2])
        wsel = sb("wsel", [P, 2, NSM])
        cuts = [0]

        def small(n):
            cuts[0] += n
            return zall[:, cuts[0] - n:cuts[0]]
        topv = small(16 * PTOP).rearrange("p (j k) -> p j k", k=PTOP)
        topi = small(16 * PTOP).bitcast(U32).rearrange("p (j k) -> p j k", k=PTOP)
        topf = small(16 * PTOP).rearrange("p (j k) -> p j k", k=PTOP)
        tops = small(P).rearrange("p (h k) -> p h k", k=PTOP)
        posu = small(P).bitcast(U32).rearrange("p (h k) -> p h k", k=PTOP)
        posq = small(P).bitcast(U32).rearrange("p (h k) -> p h k", k=PTOP)
        posf = small(P).rearrange("p (h k) -> p h k", k=PTOP)
        pick = small(2 * P).rearrange("p (q h k) -> p q h k", q=2, k=PTOP)
        gate = small(3 * P).rearrange("p (t s) -> p t s", t=3)
        gsm = sb("gsm", [P, 2, PH])
        dcur = sb("dcur", [P, 2, UR])
        ucur = sb("ucur", [P, 2, UR], I32)
        vcur = sb("vcur", [P, 2, UR], I32)
        NDG = 4
        o = 2 * UR * D + PH * 256
        diag = big[:, o:o + NDG * P].rearrange("p (n k) -> p n k", k=P)
        zeros = big[:, o + NDG * P:o + NDG * P + 512]

        bankA = [ctx.enter_context(nc.psum_tensor(f"bankA{i}", [P, 512], F32)) for i in range(4)]
        bankD = [ctx.enter_context(nc.psum_tensor(f"bankD{i}", [P, 512], F32)) for i in range(4)]

        span = ((0, 512), (512, 512), (1024, NSM))

        in_small, in_x, in_pages, in_const = sem("in_small"), sem("in_x"), sem("in_pages"), sem("in_const")
        w_landed = [sem(f"w_landed{i}") for i in range(NW)]
        kv_out, y_out, conv_out_done = sem("kv_out"), sem("y_out"), sem("conv_out_done")
        gelu_done, row_asked, round_begun = sem("gelu_done"), sem("row_asked"), sem("round_begun")
        sub_landed = sem("sub_landed")
        v_landed = sem("v_landed")
        k_landed = [sem(f"k_landed{i}") for i in range(2)]
        i_landed = [sem(f"i_landed{i}") for i in range(2)]
        a_full, a_free, d_full, d_free = sem("a_full"), sem("a_free"), sem("d_full"), sem("d_free")
        act_seq, dve_seq, pool_seq = sem("act_seq"), sem("dve_seq"), sem("pool_seq")
        consts_ready = sem("consts_ready")
        xT_ready, cT_ready, sq_ready, var_ready, sd_ready, h_ready = (
            sem("xT_ready"), sem("cT_ready"), sem("sq_ready"), sem("var_ready"), sem("sd_ready"), sem("h_ready"))
        z_ready, qk_var, qk_sd, rope_done = sem("z_ready"), sem("qk_var"), sem("qk_sd"), sem("rope_done")
        qT_ready, qT_used = sem("qT_ready"), sem("qT_used")
        mb_ready = sem("mb_ready")
        nmax_ready, probs_ready, probsT_ready, probs_used, probsT_used, orow_ready = (
            sem("nmax_ready"), sem("probs_ready"), sem("probsT_ready"), sem("probs_used"), sem("probsT_used"),
            sem("orow_ready"))
        relu_ready, relu_used, orow_used = sem("relu_ready"), sem("relu_used"), sem("orow_used")
        sq_pre = sem("sq_pre")
        Qs_ready, wsel_ready, ib_ready, ib_used, kb_ready, kb_used, reluS_ready, reluS_used = (
            sem("Qs_ready"), sem("wsel_ready"), sem("ib_ready"), sem("ib_used"), sem("kb_ready"), sem("kb_used"),
            sem("reluS_ready"), sem("reluS_used"))
        mbS_ready, oT_ready, gates_ready, conv_in, a_ready, tail_ready, tail_row = (
            sem("mbS_ready"), sem("oT_ready"), sem("gates_ready"), sem("conv_in"), sem("a_ready"), sem("tail_ready"),
            sem("tail_row"))
        mix_ready, x1_ready, rows_ready, subT_ready, qp_ready, s_ready, s_used = (
            sem("mix_ready"), sem("x1_ready"), sem("rows_ready"), sem("subT_ready"), sem("qp_ready"), sem("s_ready"),
            sem("s_used"))
        routed, zeros_ready = sem("routed"), sem("zeros_ready")
        u_in = [sem(f"u_in{i}") for i in range(UR)]
        v_in = [sem(f"v_in{i}") for i in range(UR)]
        u_used, v_used, dots_ready, w_ready, diag_ready, cur_done, acc_done, acc_taken, y_ready = (
            sem("u_used"), sem("v_used"), sem("dots_ready"), sem("w_ready"), sem("diag_ready"), sem("cur_done"),
            sem("acc_done"), sem("acc_taken"), sem("y_ready"))
        dcur_copied = sem("dcur_copied")

        def cols(w, a, n):
            k = w.shape[0] // P
            return w[:, a:a + n].rearrange("(k p) n -> p k n", p=P), k, n

        attn_rows = w_attn_out.rearrange("(n g d) m -> n g d m", n=NKV, g=NG)
        groups = ([("ada", cols(w_ada, 512 * i, 512)) for i in range(4)]
                  + [("q", cols(w_in, C_Q, 512)), ("kv", cols(w_in, C_K, 256)), ("qi", cols(w_in, C_QI, 512)),
                     ("kw", cols(w_in, C_KI, 72))]
                  + [("conv", cols(w_in, 512 * i, 512)) for i in range(3)]
                  + [("gate", cols(w_in, C_GA + 512 * i, 512)) for i in range(4)]
                  + [("ada", cols(w_ada, 512 * i, 512)) for i in range(4, 12)]
                  + [("convout", cols(w_conv_out, 0, D)), ("attnout", None)]
                  + [("out", cols(w_out, 512 * i, 512)) for i in range(2)]
                  + [("peerq", cols(peer_w_q, 512 * i, 512)) for i in range(4)])
        names = [n for n, _ in groups]

        def weights(eng, g):
            eng.wait_ge(w_landed[g % NW], 16 * (2 if names[g] == "attnout" else 1) * 1 + 16 * landed_before(g))
            k, n = (4, D) if names[g] == "attnout" else groups[g][1][1:]
            return wring[g % NW][:, 0:k * n].rearrange("p (k n) -> p k n", n=n)

        def landed_before(g):
            return sum(2 if names[j] == "attnout" else 1 for j in range(g % NW, g, NW))

        block = ctx.enter_context(nc.Block())

        released = {}
        turned_i, turned_k = {}, {}
        v_done = {}
        logit_bank = {}

        @block.tensor
        def _(pe):
            A, V = Banks(bankA, a_full, a_free), Banks(bankD, d_full, d_free)
            pe.wait_ge(in_const, 16)
            pe.wait_ge(consts_ready, 4)
            pe.wait_ge(in_small, 16 * 9)
            b = V.open(pe)
            V.close(pe.transpose(b[:, 0:76], smallrows[:, :], ident[0:76, 0:76]))
            b = V.open(pe)
            for c in range(DC):
                mm = pe.transpose(b[:, 9 * c:9 * c + 9], crow[0:9, c * P:(c + 1) * P], ident[0:9, 0:9])
            V.close(mm)
            b = V.open(pe)
            for c in range(CC):
                mm = pe.transpose(b[:, 16 * c:16 * c + 16], srow[0:16, c * P:(c + 1) * P], ident[0:16, 0:16])
            V.close(mm)
            b = V.open(pe)
            V.close(pe.matmul(b[:, 0:P], ones[0:1, :], qkrow[0:1, :], start=True, stop=True))
            pe.wait_ge(in_x, 48)
            for c in range(DC):
                b = V.open(pe)
                for t in range(3):
                    mm = pe.transpose(b[:, COLS[t]:COLS[t] + ROWS[t]], xin[0:ROWS[t], t, c * P:(c + 1) * P],
                                      ident[0:ROWS[t], 0:ROWS[t]])
                V.close(mm)

            g = 0

            def ada(g):
                w = weights(pe, g)
                b = V.open(pe)
                for j in range(4):
                    for k in range(DC):
                        mm = pe.matmul(b[:, 9 * j:9 * j + 9], w[:, k, j * P:(j + 1) * P], cT[:, k, :],
                                       start=(k == 0), stop=(k == DC - 1))
                V.close(mm)
                released[g] = (d_full, V.n)

            def norm_sum(n):
                pe.wait_ge(sq_ready, n)
                b = V.open(pe)
                for c in range(DC):
                    mm = pe.matmul(b[:, 0:TOK], ones[:, :], sq[:, c * TOK:(c + 1) * TOK], start=(c == 0), stop=(c == DC - 1))
                V.close(mm)

            pe.wait_ge(cT_ready, 1)
            for _ in range(4):
                ada(g)
                g += 1
            norm_sum(1)
            pe.wait_ge(h_ready, 1)

            for name, width in (("q", 512), ("kv", 256), ("qi", 512), ("kw", 72)):
                w = weights(pe, g)
                for t in range(3):
                    b = A.open(pe)
                    for k in range(DC):
                        mm = pe.matmul(b[0:ROWS[t], 0:width], hT[:, k, COLS[t]:COLS[t] + ROWS[t]], w[:, k, :],
                                       start=(k == 0), stop=(k == DC - 1))
                    A.close(mm)
                released[g] = (a_full, A.n)
                g += 1

            def turn_tile(t, n):
                r, z = ROWS[t], zbuf[0:ROWS[t], t, :]
                idt = ident[0:r, 0:r]
                pe.wait_ge(rope_done, n)
                b = V.open(pe)
                for gg in range(NG):
                    mm = pe.transpose(b[:, gg * r:gg * r + r], orow[0:r, gg * P:(gg + 1) * P], idt)
                V.close(mm)
                b = V.open(pe)
                for c in range(4):
                    mm = pe.transpose(b[:, c * r:c * r + r], z[:, Z_QI + c * P:Z_QI + (c + 1) * P], idt)
                V.close(mm)
                b = V.open(pe)
                pe.transpose(b[:, 0:r], z[:, Z_K:Z_K + P], idt)
                V.close(pe.transpose(b[:, P:P + r], kidup[0:r, :], idt))

            turn_tile(2, 1)
            b = V.open(pe)
            for gg in range(2):
                mm = pe.matmul(b[:, NH * gg:NH * gg + NH], cv["rep"][0:NSM, gg * P:(gg + 1) * P], wis[0:NSM, 2, :],
                               start=True, stop=True)
            V.close(mm)

            for t in range(2):
                W = P * (t + 1)
                turn_tile(t, 2 + t)
                pe.wait_ge(qT_ready, t + 2)
                for hp in range(NH // 2):
                    b = A.open(pe)
                    for j in range(2):
                        mm = pe.matmul(b[:, j * W:(j + 1) * W], qiTz[:, 2 * hp + j, :], kiT[:, 0:W], start=True, stop=True)
                    A.close(mm)
                pe.wait_ge(mb_ready, t + 1)
                for hp in range(NH // 2):
                    b = V.open(pe)
                    logit_bank[t, hp] = b
                    for j in range(2):
                        pe.matmul(b[:, j * W:(j + 1) * W], qTz[:, 2 * hp + j, :], kT[:, 0:W], start=True, stop=False)
                        mm = pe.matmul(b[:, j * W:(j + 1) * W], ident_bf[:, :], mbP[:, 0:W], start=False, stop=True)
                    V.close(mm)
                pe.wait_ge(probs_ready, NH * (t + 1))
                per = t + 1
                for q in range(NH * per // 4):
                    b = A.open(pe)
                    for j in range(4):
                        mm = pe.transpose(b[:, j * P:(j + 1) * P], probs[:, (4 * q + j) * P:(4 * q + j + 1) * P], ident)
                    A.close(mm)
                pe.wait_ge(probsT_ready, 2 if t == 0 else 6)
                b = V.open(pe)
                for h in range(NH):
                    for c in range(per):
                        kv = zbuf[:, c, Z_V + (h // NG) * HD:Z_V + (h // NG + 1) * HD]
                        mm = pe.matmul(b[:, h * HD:(h + 1) * HD], probsT[:, (h * per + c) * P:(h * per + c + 1) * P], kv,
                                       start=(c == 0), stop=(c == per - 1))
                V.close(mm)
                pe.wait_ge(orow_ready, t + 1)
                b = V.open(pe)
                for gg in range(NG):
                    mm = pe.transpose(b[:, gg * P:(gg + 1) * P], orow[:, gg * P:(gg + 1) * P], ident)
                V.close(mm)
            pe.wait_ge(oT_ready, 2)
            for G in range(2):
                sbank = [V.open(pe) for _ in range(3)]
                for b4 in range(4):
                    bb = 4 * G + b4
                    pe.wait_ge(i_landed[bb % 2], 16 * NPG * (bb // 2 + 1))
                    b = A.open(pe)
                    for q in range(4):
                        mm = pe.transpose(b[:, q * P:(q + 1) * P],
                                          ipages[:, bb % 2, 2 * q:2 * q + 2, :].rearrange("p g d -> p (g d)"), ident)
                    A.close(mm)
                    turned_i[bb] = A.n
                    pe.wait_ge(ib_ready, bb + 1)
                    for pg in range(NPG):
                        mm = pe.matmul(sbank[pg // 4][32 * b4:32 * b4 + 32, (pg % 4) * P:(pg % 4 + 1) * P],
                                       QIs[:, pg % 2, bb * 32:(bb + 1) * 32], ibT[:, bb % 2, (pg // 2) * P:(pg // 2 + 1) * P],
                                       start=True, stop=True)
                    mm.then_inc(ib_used, 1)
                mm = pe.matmul(sbank[2][:, 0:NSM], QIs[:, 0, G * P:(G + 1) * P], kiT[:, SEQ:TOK], start=True, stop=True)
                V.close(mm, 3)
            pe.wait_ge(reluS_ready, 6)
            pe.wait_ge(wsel_ready, 1)
            for a, n in span:
                b = V.open(pe)
                for G in range(2):
                    mm = pe.matmul(b[0:NSM, 0:n], wsel[:, G, :], reluS[:, G, a:a + n], start=(G == 0), stop=(G == 1))
                V.close(mm)

            for _ in range(7):
                w = weights(pe, g)
                for j in range(4):
                    b = A.open(pe)
                    for k in range(DC):
                        mm = pe.matmul(b[:, 0:TOK], w[:, k, j * P:(j + 1) * P], hT[:, k, 0:TOK], start=(k == 0), stop=(k == DC - 1))
                    A.close(mm)
                released[g] = (a_full, A.n)
                g += 1
            pe.wait_ge(mbS_ready, 1)
            for G in range(2):
                sbank = [V.open(pe) for _ in range(3)]
                logit_bank[2, G] = sbank
                for i, (a, n) in enumerate(span):
                    pe.matmul(sbank[i][:, 0:n], rep_bf[:, G * P:(G + 1) * P], mbS[:, a:a + n], start=True, stop=False,
                              skip_group_check=True)
                for b4 in range(4):
                    bb = 4 * G + b4
                    pe.wait_ge(k_landed[bb % 2], 16 * NPG * (bb // 2 + 1))
                    for half in range(2):
                        b = A.open(pe)
                        for q in range(4):
                            mm = pe.transpose(b[:, q * P:(q + 1) * P], kpages[:, bb % 2, 4 * half + q, :], ident)
                        A.close(mm)
                    turned_k[bb] = A.n
                    pe.wait_ge(kb_ready, 2 * bb + 2)
                    for half in range(2):
                        mm = pe.matmul(sbank[half][32 * b4:32 * b4 + 32, :], Qs[:, bb * 32:(bb + 1) * 32],
                                       kbT[:, bb % 2, half * 512:(half + 1) * 512], start=False, stop=(b4 == 3),
                                       skip_group_check=True)
                    mm.then_inc(kb_used, 1)
                mm = pe.matmul(sbank[2][:, 0:NSM], Qs[:, G * P:(G + 1) * P], kT[:, SEQ:TOK], start=False, stop=True,
                               skip_group_check=True)
                V.close(mm, 3)
                pe.wait_ge(probs_ready, 2 * NH + 3 * (G + 1))
                for half in range(2):
                    b = A.open(pe)
                    for q in range(4):
                        pg = 4 * half + q
                        mm = pe.transpose(b[:, q * P:(q + 1) * P], probsS[:, pg * P:(pg + 1) * P], ident)
                    A.close(mm)
                b = A.open(pe)
                A.close(pe.transpose(b[0:NSM, 0:P], probsS[:, PAST:NKEY], ident))
                pe.wait_ge(probsT_ready, 6 + 3 * (G + 1))
                pe.wait_ge(v_landed, 16 * NB * NPG)
                b = V.open(pe)
                for b4 in range(4):
                    bb = 4 * G + b4
                    for pg in range(NPG):
                        pe.matmul(b[32 * b4:32 * b4 + 32, 0:P], probsST[:, pg * P + 32 * b4:pg * P + 32 * b4 + 32],
                                  vpages[:, bb * NPG + pg, :], start=(pg == 0), stop=False)
                    mm = pe.matmul(b[32 * b4:32 * b4 + 32, 0:P], probsST[0:NSM, NPG * P + 32 * b4:NPG * P + 32 * b4 + 32],
                                   zbuf[0:NSM, 2, Z_V:Z_V + P], start=False, stop=True)
                V.close(mm)
                v_done[0] = (d_full, V.n)
                pe.wait_ge(orow_ready, 3 + G)
                b = V.open(pe)
                V.close(pe.transpose(b[:, 0:P], orow[:, 0:P], ident))

            for _ in range(8):
                ada(g)
                g += 1
            pe.wait_ge(tail_ready, 1)
            b = V.open(pe)
            for c in range(CC):
                mm = pe.transpose(b[0:18, c * P:(c + 1) * P], tails[:, c, :], ident)
            V.close(mm)
            pe.wait_ge(a_ready, 1)
            pe.wait_ge(oT_ready, 4)
            for src in (aT, oT):
                w = weights(pe, g)
                for j in range(DC):
                    b = V.open(pe)
                    for k in range(4):
                        mm = pe.matmul(b[:, 0:TOK], w[:, k, j * P:(j + 1) * P], src[:, k, 0:TOK], start=(k == 0), stop=(k == 3))
                    V.close(mm)
                released[g] = (d_full, V.n)
                g += 1
            pe.wait_ge(mix_ready, 1)
            for _ in range(2):
                w = weights(pe, g)
                for j in range(4):
                    b = V.open(pe)
                    for k in range(DC):
                        mm = pe.matmul(b[:, 0:TOK], w[:, k, j * P:(j + 1) * P], mixT[:, k, :], start=(k == 0), stop=(k == DC - 1))
                    V.close(mm)
                released[g] = (d_full, V.n)
                g += 1
            pe.wait_ge(sub_landed, 16)
            for q in range(4):
                b = A.open(pe)
                for j in range(4):
                    mm = pe.transpose(b[:, j * P:(j + 1) * P], subraw[:, 4 * q + j, :], ident)
                A.close(mm)
            norm_sum(2)
            pe.wait_ge(h_ready, 2)
            for _ in range(4):
                w = weights(pe, g)
                for j in range(4):
                    b = A.open(pe)
                    for k in range(DC):
                        mm = pe.matmul(b[:, 0:TOK], w[:, k, j * P:(j + 1) * P], hT[:, k, 0:TOK], start=(k == 0), stop=(k == DC - 1))
                    A.close(mm)
                released[g] = (a_full, A.n)
                g += 1
            for t in range(3):
                for half in range(2):
                    b = A.open(pe)
                    for q in range(4):
                        mm = pe.transpose(b[:, q * P:(q + 1) * P], hT[:, 4 * half + q, t * P:(t + 1) * P], ident)
                    A.close(mm)
            for t in range(3):
                for half in range(2):
                    b = A.open(pe)
                    for q in range(4):
                        mm = pe.transpose(b[0:ROWS[t], q * P:(q + 1) * P], xT[:, 4 * half + q, COLS[t]:COLS[t] + ROWS[t]], ident)
                    A.close(mm)
            for s in range(2):
                for half in range(2):
                    b = A.open(pe)
                    for q in range(4):
                        mm = pe.transpose(b[:, q * P:(q + 1) * P], gspread[:, ((4 * half + q) * 2 + s) * P:((4 * half + q) * 2 + s + 1) * P], ident)
                    A.close(mm)
            pe.wait_ge(qp_ready, 1)
            pe.wait_ge(subT_ready, 4)
            for t in range(3):
                for q in range(4):
                    b = A.open(pe)
                    for j in range(4):
                        hp = 4 * q + j
                        mm = pe.matmul(b[:, j * P:(j + 1) * P], qpT[:, hp, t * P:(t + 1) * P],
                                       subT[:, (hp % 2) * PH + hp // 2, :], start=True, stop=True)
                    A.close(mm)
            pe.wait_ge(d_free, V.n)

            pe.wait_ge(zeros_ready, 1)
            pe.sem_inc(v_used, UR)
            v_round = 0
            for t in range(3):
                acc = bankD[2 * (t % 2):2 * (t % 2) + 2]
                if t == 2:
                    pe.wait_ge(acc_taken, 1)
                for half in range(2):
                    pe.matmul(acc[half][:, :], zeros[:, 0:P], zeros, start=True, stop=False, skip_group_check=True)
                rounds = SLOTS[t] // UR
                with pe.Fori(0, rounds) as i:
                    for r in range(UR):
                        pe.wait_ge(v_in[r], (i + (v_round + 1)) * 16)
                        pe.wait_ge(diag_ready, (i + v_round) * UR + (r + 1))
                        pe.matmul(acc[0][:, :], diag[:, r % NDG, :], vrows[r][:, 0:512], start=False, stop=False,
                                  skip_group_check=True)
                        pe.matmul(acc[1][:, :], diag[:, r % NDG, :], vrows[r][:, 512:D], start=False, stop=False,
                                  skip_group_check=True).then_inc(v_used, 1)
                v_round += rounds
                for half in range(2):
                    mm = pe.matmul(acc[half][:, :], zeros[:, 0:P], zeros, start=False, stop=True, skip_group_check=True)
                mm.then_inc(acc_done, 1)
            pe.wait_ge(y_ready, 3)
            pe.wait_ge(acc_taken, 2)
            for half in range(2):
                mm = pe.matmul(bankD[2 + half][0:NSM, :], cv["sum4"], yout[:, half * 512:(half + 1) * 512],
                               start=True, stop=True)
            mm.then_inc(acc_done, 1)

        @block.sync
        def _(sp):
            small = [(b_ada.rearrange("(j p) -> j p", p=P), 0, 48), (norm1_w.rearrange("(j p) -> j p", p=P), 48, 8),
                     (norm2_w.rearrange("(j p) -> j p", p=P), 56, 8), (conv_w.rearrange("w (j p) -> (w j) p", p=P), 64, 12)]
            sp.dma_start(crow[0:1, :], c_prompt).then_inc(in_small, 16)
            sp.dma_start(crow[1:9, :], c_sample).then_inc(in_small, 16)
            sp.dma_start(ctab[:, :], consts).then_inc(in_const, 16)
            for src, a, n in small:
                sp.dma_start(smallrows[a:a + n, :], src).then_inc(in_small, 16)
            sp.dma_start(qkrow[0:1, 0:HD], q_norm_w.rearrange("(a d) -> a d", a=1)).then_inc(in_small, 16)
            sp.dma_start(qkrow[0:1, HD:P], k_norm_w.rearrange("(a d) -> a d", a=1)).then_inc(in_small, 16)
            sp.dma_start(srow[0:16, :], state_conv.rearrange("b j c -> (b j) c")).then_inc(in_small, 16)
            for t in range(2):
                sp.dma_start(xin[:, t, :], x_prompt[t * P:(t + 1) * P, :]).then_inc(in_x, 16)
            sp.dma_start(xin[0:NSM, 2, :], x_sample).then_inc(in_x, 16)

            for g, (name, what) in enumerate(groups):
                if g >= NW:
                    sp.wait_ge(*released[g - NW])
                if name == "attnout":
                    dst = wring[g % NW].rearrange("p (k n) -> p k n", n=D)
                    for n in range(NKV):
                        sp.dma_start(dst[n * HD:(n + 1) * HD, :, :],
                                     attn_rows[n].rearrange("g d m -> d g m")).then_inc(w_landed[g % NW], 16)
                else:
                    src, k, n = what
                    sp.dma_start(wring[g % NW][:, 0:k * n].rearrange("p (k n) -> p k n", n=n), src)\
                      .then_inc(w_landed[g % NW], 16)
                if name == "attnout":
                    sp.wait_ge(oT_ready, 4)
                    sp.wait_ge(kv_out, 16 * 9)
                    sp.dma_start(subraw, peer_sub_keys.rearrange("q h k d -> k (q h) d")).then_inc(sub_landed, 16)
            sp.wait_ge(tail_row, 1)
            sp.dma_start(conv_prompt, tailrows[0:2, :]).then_inc(conv_out_done, 16)
            sp.dma_start(conv_sample.rearrange("b j c -> (b j) c"), tailrows[2:18, :]).then_inc(conv_out_done, 16)
            for t in range(2):
                sp.wait_ge(y_ready, t + 1)
                sp.dma_start(y_prompt[t * P:(t + 1) * P, :], yout[:, :]).then_inc(y_out, 16)
            sp.wait_ge(y_ready, 4)
            sp.dma_start(y_sample, yout[0:NSM, :]).then_inc(y_out, 16)
            sp.wait_ge(y_out, 16 * 3)
            sp.wait_ge(conv_out_done, 16 * 2)

        @block.gpsimd
        def _(pool):
            lane = Lane(pool, pool_seq)
            pool.dma_start(pages[:, :], page_table.rearrange("(a b) g -> a (b g)", a=1)).then_inc(in_pages, 16)
            pool.memset(ones[:, :], 1.0).then_inc(consts_ready, 1)
            pool.memset(Qs[:, :], 0.0).then_inc(consts_ready, 1)
            pool.memset(QIs[:, :, :], 0.0).then_inc(consts_ready, 1)
            pool.memset(uP[:, :, 0:2], 0.0).then_inc(consts_ready, 1)
            pool.wait_ge(in_pages, 16)

            def fetch(dst, src, done, b):
                with pool.Fori(0, NPG) as g:
                    page = pool.value_load(pages[0:1, bass.ds(g + b * NPG, 1)], min_val=0, max_val=NPHYS - 1)
                    pool.dma_start(dst[:, bass.ds(g, 1), :].rearrange("p a d -> p (a d)"),
                                   src[bass.ds(page * PAGE, PAGE), :]).then_inc(done, 16)
            for b in range(2):
                fetch(ipages[:, b], cache_kidx, i_landed[b], b)
            for b in range(2):
                fetch(kpages[:, b], cache_k, k_landed[b], b)
            for b in range(NB):
                fetch(vpages[:, b * NPG:(b + 1) * NPG], cache_v, v_landed, b)
            for b in range(2, NB):
                pool.wait_ge(a_full, turned_i[b - 2])
                fetch(ipages[:, b % 2], cache_kidx, i_landed[b % 2], b)
            for b in range(2, NB):
                pool.wait_ge(a_full, turned_k[b - 2])
                fetch(kpages[:, b % 2], cache_k, k_landed[b % 2], b)

            for full, n in released[len(groups) - 1], released[len(groups) - 2], v_done[0]:
                pool.wait_ge(full, n)
            done = {"u": 0, "v": 0, "cur": 0}

            def gather(kind, t, ring, cur, table, landed, used):
                rounds = SLOTS[t] // UR
                with pool.Fori(0, rounds // 2) as i:
                    for par in range(2):
                        pool.tensor_copy(cur[:, par, :], eidx[:, t, bass.ds(i * (2 * UR) + par * UR, UR)]).then_inc(cur_done, 1)
                        pool.wait_ge(cur_done, i * 2 + (done["cur"] + par + 1))
                        for r in range(UR):
                            pool.wait_ge(used, i * (2 * UR) + ((done[kind] + par) * UR + r + 1))
                            pool.sem_inc(row_asked, 1)
                            pool.indirect_dma_start(ring[r], None, table, bass.IndirectOffsetOnAxis(
                                ap=cur[:, par, r:r + 1], axis=0)).then_inc(landed[r], 16)
                done[kind] += rounds
                done["cur"] += rounds

            for t in range(3):
                pool.wait_ge(routed, t + 1)
                gather("u", t, urows, ucur, peer_u, u_in, u_used)
                gather("v", t, vrows, vcur, peer_v, v_in, v_used)

        @block.scalar
        def _(act):
            A = Banks(bankA, a_full, a_free)
            L = Lane(act, act_seq)
            act.wait_ge(xT_ready, DC)
            L.tell(act.activation(sq, xT[:, :, :].rearrange("p c t -> p (c t)"), ACT.Square), sq_ready)
            act.wait_ge(var_ready, 1)
            L.tell(act.activation(rstd[:, :], rstd[:, :], ACT.Sqrt), sd_ready)
            for a, n in ((0, 512), (Z_K, 256), (Z_QI, 512), (Z_KI, 72)):
                for t in range(3):
                    b = A.take(act)
                    act.activation(zbuf[0:ROWS[t], t, a:a + n], b[0:ROWS[t], 0:n], ACT.Copy).then_inc(a_free, 1)
                    act.wait_ge(a_free, A.n)
            act.sem_inc(z_ready, 1)

            def head_norm(n, t, k_out, v_out, i_out):
                act.wait_ge(qk_var, n)
                r = ROWS[t]
                L.tell(act.activation(stat[0:r, 0:10], stat[0:r, 0:10], ACT.Sqrt), qk_sd)
                act.wait_ge(rope_done, n)
                act.dma_start(k_out, zbuf[0:r, t, Z_K:Z_K + P]).then_inc(kv_out, 16)
                act.dma_start(v_out, zbuf[0:r, t, Z_V:Z_V + P]).then_inc(kv_out, 16)
                act.dma_start(i_out, zbuf[0:r, t, Z_KI:Z_KI + HD]).then_inc(kv_out, 16)

            head_norm(1, 2, k_sample, v_sample, kidx_sample)
            for t in range(2):
                W = P * (t + 1)
                head_norm(2 + t, t, k_prompt[t * P:(t + 1) * P, :], v_prompt[t * P:(t + 1) * P, :],
                          kidx_prompt[t * P:(t + 1) * P, :])
                for hp in range(4):
                    b = A.take(act)
                    if 4 * t + hp >= 2:
                        act.wait_ge(relu_used, 4 * t + hp - 1)
                    dst = relu[:, 0:2 * W] if hp % 2 == 0 else probs[:, 0:2 * W]
                    ins = act.activation(dst, b[:, 0:2 * W], ACT.Relu)
                    ins.then_inc(relu_ready, 1)
                    act.wait_ge(relu_ready, 4 * t + hp + 1)
                    act.sem_inc(a_free, 1)
                for h in range(NH):
                    act.wait_ge(nmax_ready, NH // 2 * t + h // 2 + 1)
                    src = logit_bank[t, h // 2][:, (h % 2) * W:(h % 2 + 1) * W]
                    L.tell(act.activation(probs[:, h * W:(h + 1) * W], src, ACT.Exp, bias=nmax[:, h:h + 1], scale=QSCALE,
                                          accum_out=rsum[:, t, h:h + 1]), probs_ready)
                for q in range(2 * (t + 1)):
                    b = A.take(act)
                    L.tell(act.activation(probsT[:, q * 512:(q + 1) * 512], b[:, :], ACT.Copy), probsT_ready)
                    act.sem_inc(a_free, 1)
            act.wait_ge(oT_ready, 2)
            for G in range(2):
                for b4 in range(4):
                    bb = 4 * G + b4
                    b = A.take(act)
                    if bb >= 2:
                        act.wait_ge(ib_used, bb - 1)
                    L.tell(act.activation(ibT[:, bb % 2, :], b[:, :], ACT.Copy), ib_ready)
                    act.sem_inc(a_free, 1)
            for j in range(12):
                b = A.take(act)
                L.tell(act.activation((bufX, bufB, bufC)[j // 4][:, j % 4, :], b[:, 0:TOK], ACT.Copy), conv_in)
                act.sem_inc(a_free, 1)
            for j in range(16):
                b = A.take(act)
                L.tell(act.activation(sig[:, j, :], b[:, 0:TOK], ACT.Sigmoid), gates_ready)
                act.sem_inc(a_free, 1)
            for G in range(2):
                for b4 in range(4):
                    bb = 4 * G + b4
                    for half in range(2):
                        b = A.take(act)
                        if bb >= 2:
                            act.wait_ge(kb_used, bb - 1)
                        L.tell(act.activation(kbT[:, bb % 2, half * 512:(half + 1) * 512], b[:, :], ACT.Copy), kb_ready)
                        act.sem_inc(a_free, 1)
                act.wait_ge(nmax_ready, NH + G + 1)
                for i, (a, n) in enumerate(span):
                    src = logit_bank[2, G][i][:, 0:n]
                    L.tell(act.activation(probsS[:, a:a + n], src, ACT.Exp, bias=nmax[:, 0:1], scale=QSCALE,
                                          accum_out=rsum[:, 2, 4 * G + i:4 * G + i + 1]), probs_ready)
                for half in range(2):
                    b = A.take(act)
                    if G == 1:
                        act.wait_ge(orow_ready, 3)
                    L.tell(act.activation(probsST[:, half * 512:(half + 1) * 512], b[:, :], ACT.Copy), probsT_ready)
                    act.sem_inc(a_free, 1)
                b = A.take(act)
                L.tell(act.activation(probsST[0:NSM, NPG * P:NPG * P + P], b[0:NSM, 0:P], ACT.Copy), probsT_ready)
                act.sem_inc(a_free, 1)
            act.wait_ge(sub_landed, 16)
            for q in range(4):
                b = A.take(act)
                L.tell(act.activation(subT[:, 4 * q:4 * q + 4, :].rearrange("p j k -> p (j k)"), b[:, :], ACT.Copy), subT_ready)
                act.sem_inc(a_free, 1)
            act.wait_ge(x1_ready, DC)
            L.tell(act.activation(sq, xT[:, :, :].rearrange("p c t -> p (c t)"), ACT.Square), sq_ready)
            act.wait_ge(var_ready, 2)
            L.tell(act.activation(rstd[:, :], rstd[:, :], ACT.Sqrt), sd_ready)
            act.wait_ge(h_ready, 2)
            for j in range(16):
                b = A.take(act)
                L.tell(act.activation(qpT[:, j, 0:SEQ], b[:, 0:SEQ], ACT.Copy), wait=False)
                L.tell(act.activation(qpT[:, j, SEQ:3 * P].rearrange("p (r t) -> p r t", r=4),
                                      b[:, SEQ:TOK].unsqueeze(1).broadcast_to([P, 4, NSM]), ACT.Copy))
                act.sem_inc(a_free, 1)
            act.sem_inc(qp_ready, 1)
            act.wait_ge(sq_pre, 1)
            act.wait_ge(conv_out_done, 32)
            for t in range(3):
                for half in range(2):
                    b = A.take(act)
                    L.tell(act.activation(h2tok[:, t, half * 512:(half + 1) * 512], b[:, :], ACT.Copy))
                    act.sem_inc(a_free, 1)
            for t in range(3):
                for half in range(2):
                    b = A.take(act)
                    L.tell(act.activation(x1tok[0:ROWS[t], t, half * 512:(half + 1) * 512], b[0:ROWS[t], :], ACT.Copy))
                    act.sem_inc(a_free, 1)
            for s in range(2):
                for half in range(2):
                    b = A.take(act)
                    L.tell(act.activation(g2tok[:, s, half * 512:(half + 1) * 512], b[:, :], ACT.Copy))
                    act.sem_inc(a_free, 1)
            act.sem_inc(rows_ready, 1)
            def scores(t):
                if t:
                    act.wait_ge(s_used, t)
                for q in range(4):
                    b = A.take(act)
                    L.tell(act.activation(ssb[:, 4 * q:4 * q + 4, :].rearrange("p j k -> p (j k)"), b[:, :], ACT.Copy), s_ready)
                    act.sem_inc(a_free, 1)

            scores(0)
            scores(1)
            v_round = 0
            for t in range(3):
                n = SLOTS[t]
                act.wait_ge(dots_ready, t + 1)
                L.tell(act.activation(dots[:, t, 0:n], dots[:, t, 0:n], ACT.Gelu_apprx_tanh), gelu_done)
                L.tell(act.activation(gate[:, t, 0:n], gate[:, t, 0:n], ACT.Exp), gelu_done)
                act.wait_ge(w_ready, t + 1)
                with act.Fori(0, n // UR) as i:
                    for r in range(UR):
                        act.wait_ge(v_used, (i + v_round) * UR + (r + 1 + UR - NDG))
                        act.activation(diag[:, r % NDG, :], ident, ACT.Copy, scale=dots[:, t, bass.ds(i * UR + r, 1)])\
                           .then_inc(diag_ready, 1)
                v_round += n // UR
                if t == 0:
                    scores(2)

        @block.vector
        def _(dve):
            V = Banks(bankD, d_full, d_free)
            L = Lane(dve, dve_seq)
            tt, ts, cp = dve.tensor_tensor, dve.tensor_scalar, dve.tensor_copy

            def free():
                dve.sem_inc(d_free, 1)

            dve.wait_ge(in_const, 16)
            L.tell(cp(ident_bf[:, :], ident))
            L.tell(cp(rep_bf[:, :], cv["rep"][0:NSM, :]))
            dve.wait_ge(consts_ready, 4)
            L.tell(cp(smallT[:, :], V.take(dve)[:, 0:76])); free()
            L.tell(cp(cT[:, :, :].rearrange("p c b -> p (c b)"), V.take(dve)[:, 0:72]), cT_ready); free()
            L.tell(cp(stateT[:, :, :].rearrange("p c b -> p (c b)"), V.take(dve)[:, 0:64])); free()
            L.tell(cp(qkw[:, :], V.take(dve)[:, 0:P])); free()
            for c in range(DC):
                L.tell(cp(xT[:, c, :], V.take(dve)[:, 0:TOK]), xT_ready); free()

            def ada(g):
                b = V.take(dve)
                L.tell(tt(modT[:, 4 * g:4 * g + 4, :], b[:, 0:36].rearrange("p (j b) -> p j b", b=9),
                          smallT[:, 4 * g:4 * g + 4].unsqueeze(2).broadcast_to([P, 4, 9]), ALU.add)); free()

            def norm(n, scale, shift, w):
                L.tell(ts(ab[:, :, :], modT[:, scale:scale + DC, :], 1.0, None, ALU.add))
                L.tell(tt(ab[:, :, :], ab[:, :, :], smallT[:, w:w + DC].unsqueeze(2).broadcast_to([P, DC, 9]), ALU.mult))
                b = V.take(dve)
                L.tell(ts(rstd[:, :], b[:, 0:TOK], 1.0 / D, EPS, ALU.mult, ALU.add), var_ready); free()
                dve.wait_ge(sd_ready, n)
                L.tell(dve.reciprocal(rstd[:, :], rstd[:, :]))
                h = hT[:, :, 0:TOK]
                L.tell(tt(h, xT[:, :, :], rstd[:, :].unsqueeze(1).broadcast_to([P, DC, TOK]), ALU.mult))
                for c in range(DC):
                    L.tell(ts(hT[:, c, 0:SEQ], hT[:, c, 0:SEQ], ab[:, c, 0:1], modT[:, shift + c, 0:1], ALU.mult, ALU.add),
                           wait=False)
                    hs = hT[:, c, SEQ:TOK].rearrange("p (b s) -> p b s", s=NS)
                    L.tell(tt(hs, hs, ab[:, c, 1:9].unsqueeze(2).broadcast_to([P, NB, NS]), ALU.mult))
                    L.tell(tt(hs, hs, modT[:, shift + c, 1:9].unsqueeze(2).broadcast_to([P, NB, NS]), ALU.add))

            for g in range(4):
                ada(g)
            norm(1, 8, 0, 48)
            dve.sem_inc(h_ready, 1)

            dve.wait_ge(z_ready, 1)

            def rotate(z, a, nh, t, r):
                x1 = z[:, a:a + nh * HD].rearrange("p (h d) -> p h d", d=HD)[:, :, 0:32]
                x2 = z[:, a:a + nh * HD].rearrange("p (h d) -> p h d", d=HD)[:, :, 32:64]
                cs = cv["cos"][0:r, 32 * t:32 * t + 32].unsqueeze(1).broadcast_to([r, nh, 32])
                sn = cv["sin"][0:r, 32 * t:32 * t + 32].unsqueeze(1).broadcast_to([r, nh, 32])
                t1, t2 = (rope[i][0:r, 0:nh * 32].rearrange("p (h d) -> p h d", d=32) for i in range(2))
                L.tell(tt(t1, x2, sn, ALU.mult), wait=False)
                L.tell(tt(t2, x1, sn, ALU.mult))
                L.tell(tt(x1, x1, cs, ALU.mult), wait=False)
                L.tell(tt(x2, x2, cs, ALU.mult))
                L.tell(tt(x1, x1, t1, ALU.subtract), wait=False)
                L.tell(tt(x2, x2, t2, ALU.add))

            for n, t in enumerate((2, 0, 1)):
                r, z = ROWS[t], zbuf[0:ROWS[t], t, :]
                st = stat[0:r, 0:10]
                zq = z[:, 0:10 * HD].rearrange("p (h d) -> p h d", d=HD)
                sqv = probs[0:r, 0:10 * HD].rearrange("p (h d) -> p h d", d=HD)
                L.tell(tt(sqv, zq, zq, ALU.mult))
                L.tell(dve.tensor_reduce(st, sqv, AX, ALU.add))
                L.tell(ts(st, st, 1.0 / HD, EPS, ALU.mult, ALU.add), qk_var)
                dve.wait_ge(qk_sd, n + 1)
                L.tell(dve.reciprocal(st, st))
                L.tell(tt(zq, zq, st.unsqueeze(2).broadcast_to([r, 10, HD]), ALU.mult))
                L.tell(tt(zq[:, 0:8], zq[:, 0:8], qkw[0:r, 0:HD].unsqueeze(1).broadcast_to([r, 8, HD]), ALU.mult), wait=False)
                L.tell(tt(zq[:, 8:10], zq[:, 8:10], qkw[0:r, HD:P].unsqueeze(1).broadcast_to([r, 2, HD]), ALU.mult))
                rotate(z, 0, 10, t, r)
                rotate(z, Z_QI, 9, t, r)
                L.tell(cp(orow[0:r, :].rearrange("p (g n d) -> p n g d", g=NG, n=NKV),
                          z[:, 0:512].rearrange("p (n g d) -> p n g d", n=NKV, g=NG)), wait=False)
                L.tell(cp(kidup[0:r, 0:HD], z[:, Z_KI:Z_KI + HD]), wait=False)
                L.tell(cp(kidup[0:r, HD:P], z[:, Z_KI:Z_KI + HD]), wait=False)
                L.tell(ts(wis[0:r, t, :], z[:, Z_WI:Z_WI + NH], IDX_SCALE, None, ALU.mult), rope_done)

                b = V.take(dve)
                bq = b[:, 0:NG * r].rearrange("p (g t) -> p g t", t=r)
                if t == 2:
                    for nn in range(NKV):
                        s, e = nn * HD, (nn + 1) * HD
                        dst = Qs[s:e, :].rearrange("p (b h s) -> p b h s", h=NH, s=NS)[:, :, nn * NG:(nn + 1) * NG, :]
                        for gg in range(NG):
                            L.tell(cp(dst[:, :, gg, :], bq[s:e, gg, :].rearrange("p (b s) -> p b s", s=NS)))
                    free()
                else:
                    if t == 0:
                        L.tell(dve.memset(qTz, 0.0), wait=False)
                        L.tell(dve.memset(qiTz, 0.0))
                    for nn in range(NKV):
                        s, e = nn * HD, (nn + 1) * HD
                        L.tell(cp(qTz[s:e, nn * NG:(nn + 1) * NG, :], bq[s:e]))
                    free()
                b = V.take(dve)
                bi = b[:, 0:4 * r].rearrange("p (c t) -> p c t", t=r)
                for par in range(2):
                    s, e = par * HD, (par + 1) * HD
                    if t == 2:
                        for v in range(2):
                            dst = QIs[v * HD:(v + 1) * HD, v, :].rearrange("p (b h s) -> p b h s", h=NH, s=NS)
                            for c in range(4):
                                L.tell(cp(dst[:, :, 2 * c + par, :], bi[s:e, c, :].rearrange("p (b s) -> p b s", s=NS)))
                    else:
                        L.tell(cp(qiTz[s:e].rearrange("p (c q) t -> p c q t", q=2)[:, :, par, :], bi[s:e]))
                free()
                b = V.take(dve)
                L.tell(cp(kT[:, COLS[t]:COLS[t] + r], b[:, 0:r]), wait=False)
                L.tell(cp(kiT[:, COLS[t]:COLS[t] + r], b[:, P:P + r]), qT_ready)
                free()
                if t == 2:
                    b = V.take(dve)
                    for G in range(2):
                        L.tell(tt(stat[:, 16:24], b[:, NH * G:NH * G + NH], cv["headsel"], ALU.mult))
                        L.tell(dve.tensor_reduce(wrow[:, G:G + 1], stat[:, 16:24], AX, ALU.add))
                        L.tell(ts(wsel[:, G, :], cv["repT"][:, G * NSM:(G + 1) * NSM], wrow[:, G:G + 1], None, ALU.mult))
                    dve.sem_inc(wsel_ready, 1)
                    free()
                    continue

                W = P * (t + 1)
                L.tell(cp(scP[:, 0:W], cv["causal0"] if t == 0 else cv["causal1"]))
                for hp in range(4):
                    dve.wait_ge(relu_ready, 4 * t + hp + 1)
                    src = relu if hp % 2 == 0 else probs
                    for j in range(2):
                        L.tell(dve.scalar_tensor_tensor(scP[:, 0:W], src[:, j * W:(j + 1) * W],
                                                        wis[:, t, 2 * hp + j:2 * hp + j + 1], scP[:, 0:W], ALU.mult, ALU.add))
                    dve.sem_inc(relu_used, 1)
                src = scP
                for _ in range(TOPK_P // 8):
                    L.tell(dve.max(best[:, :], src[:, 0:W]))
                    L.tell(dve.match_replace(workP[:, 0:W], best[:, :], src[:, 0:W], TAKEN))
                    src = workP
                L.tell(ts(workP[:, 0:W], workP[:, 0:W], -1e35, NEG, ALU.is_gt, ALU.mult))
                L.tell(tt(mbP[:, 0:W], workP[:, 0:W], cv["causal0"] if t == 0 else cv["causal1"], ALU.add), mb_ready)
                for hp in range(4):
                    b = V.take(dve)
                    L.tell(dve.tensor_reduce(stat[:, 32 + 2 * hp:34 + 2 * hp], b[:, 0:2 * W].rearrange("p (h k) -> p h k", k=W),
                                             AX, ALU.max))
                    L.tell(ts(nmax[:, 2 * hp:2 * hp + 2], stat[:, 32 + 2 * hp:34 + 2 * hp], -QSCALE, None, ALU.mult), nmax_ready)
                dve.wait_ge(probs_ready, NH * (t + 1))
                dve.sem_inc(d_free, 4)
                L.tell(dve.reciprocal(rinv[:, :], rsum[:, t, :]))
                b = V.take(dve)
                L.tell(tt(orow.rearrange("p (g n d) -> p n g d", g=NG, n=NKV),
                          b[:, :].rearrange("p (n g d) -> p n g d", n=NKV, g=NG),
                          rinv[:, :].rearrange("p (n g) -> p n g", n=NKV).unsqueeze(3).broadcast_to([P, NKV, NG, HD]), ALU.mult),
                       orow_ready)
                free()
                b = V.take(dve)
                L.tell(cp(oT[:, :, COLS[t]:COLS[t] + P], b[:, :].rearrange("p (g t) -> p g t", t=P)), oT_ready)
                free()

            for G in range(2):
                for i, (a, n) in enumerate(span):
                    b = V.take(dve)
                    L.tell(ts(reluS[:, G, a:a + n], b[:, 0:n], 0.0, None, ALU.max), reluS_ready)
                    free()
            for a, n in span:
                b = V.take(dve)
                if a < 1024:
                    L.tell(cp(scS[0:NSM, a:a + n], b[0:NSM, 0:n]))
                else:
                    L.tell(tt(scS[0:NSM, a:a + n], b[0:NSM, 0:n], cv["newbias"][0:NSM, :], ALU.add))
                free()
            L.tell(dve.max(best[0:NSM, :], scS[0:NSM, :]))
            L.tell(dve.match_replace(workS[0:NSM, :], best[0:NSM, :], scS[0:NSM, :], TAKEN))
            seq0 = L.count[id(dve_seq)]
            with dve.Fori(0, TOPK_S // 8 - 1) as i:
                dve.max(best[0:NSM, :], workS[0:NSM, :]).then_inc(dve_seq, 1)
                dve.wait_ge(dve_seq, i * 2 + (seq0 + 1))
                dve.sem_inc(round_begun, 1)
                dve.match_replace(workS[0:NSM, :], best[0:NSM, :], workS[0:NSM, :], TAKEN).then_inc(dve_seq, 1)
                dve.wait_ge(dve_seq, i * 2 + (seq0 + 2))
            L.count[id(dve_seq)] = seq0 + 2 * (TOPK_S // 8 - 1)
            L.tell(ts(mbS[:, :], workS[0:NSM, :], -1e35, NEG, ALU.is_gt, ALU.mult), mbS_ready)

            dve.wait_ge(conv_in, 12)
            for c in range(CC):
                L.tell(tt(uP[:, c, 2:SEQ + 2], bufX[:, c, 0:SEQ], bufC[:, c, 0:SEQ], ALU.mult), wait=False)
                L.tell(cp(uS[:, c, :, 0:2], stateT[:, c, :].rearrange("p (b j) -> p b j", j=2)), wait=False)
                L.tell(tt(uS[:, c, :, 2:6], bufX[:, c, SEQ:TOK].rearrange("p (b s) -> p b s", s=NS),
                          bufC[:, c, SEQ:TOK].rearrange("p (b s) -> p b s", s=NS), ALU.mult))
                L.tell(cp(tails[:, c, 0:2], uP[:, c, SEQ:SEQ + 2]), wait=False)
                L.tell(cp(tails[:, c, 2:18].rearrange("p (b j) -> p b j", j=2), uS[:, c, :, 4:6]), wait=False)
                for u, y, n in ((uP[:, c], bufX[:, c, 0:SEQ], SEQ), (uS[:, c], bufX[:, c, SEQ:TOK].rearrange("p (b s) -> p b s", s=NS), NS)):
                    tap = [u[:, j:j + n] if n == SEQ else u[:, :, j:j + n] for j in range(3)]
                    wc = [smallT[:, 64 + 4 * j + c:65 + 4 * j + c] for j in range(3)]
                    L.tell(ts(y, tap[2], wc[2], None, ALU.mult))
                    L.tell(dve.scalar_tensor_tensor(y, tap[0], wc[0], y, ALU.mult, ALU.add))
                    L.tell(dve.scalar_tensor_tensor(y, tap[1], wc[1], y, ALU.mult, ALU.add))
                L.tell(tt(aT[:, c, :], bufB[:, c, :], bufX[:, c, :], ALU.mult))
            dve.sem_inc(tail_ready, 1)
            dve.sem_inc(a_ready, 1)

            for G in range(2):
                bs = [V.take(dve) for _ in range(3)]
                for i, (a, n) in enumerate(span):
                    L.tell(dve.tensor_reduce(stat[:, 40 + i:41 + i], bs[i][:, 0:n], AX, ALU.max))
                L.tell(dve.tensor_reduce(stat[:, 43:44], stat[:, 40:43], AX, ALU.max))
                L.tell(ts(nmax[:, 0:1], stat[:, 43:44], -QSCALE, None, ALU.mult), nmax_ready)
                dve.wait_ge(probs_ready, 2 * NH + 3 * (G + 1))
                dve.sem_inc(d_free, 3)
                L.tell(dve.tensor_reduce(stat[:, 44:45], rsum[:, 2, 4 * G:4 * G + 3], AX, ALU.add))
                L.tell(dve.reciprocal(rinv[:, 0:1], stat[:, 44:45]))
                b = V.take(dve)
                L.tell(ts(orow[:, 0:P], b[:, 0:P], rinv[:, 0:1], None, ALU.mult), orow_ready)
                free()
                b = V.take(dve)
                for nn in range(NKV):
                    s, e = nn * HD, (nn + 1) * HD
                    src = b[s:e, 0:P].rearrange("p (b h s) -> p b h s", h=NH, s=NS)[:, :, nn * NG:(nn + 1) * NG, :]
                    for gg in range(NG):
                        L.tell(cp(oT[s:e, gg, SEQ + 16 * G:SEQ + 16 * G + 16].rearrange("p (b s) -> p b s", s=NS), src[:, :, gg, :]))
                free()
                dve.sem_inc(oT_ready, 1)

            for g in range(4, 12):
                ada(g)
            b = V.take(dve)
            L.tell(cp(tailrows[:, :], b[0:18, :]), tail_row)
            free()
            dve.wait_ge(gates_ready, 16)
            for j in range(DC):
                b = V.take(dve)
                L.tell(tt(sig[:, j, :], sig[:, j, :], b[:, 0:TOK], ALU.mult))
                free()
            for j in range(DC):
                b = V.take(dve)
                L.tell(tt(sig[:, 8 + j, :], sig[:, 8 + j, :], b[:, 0:TOK], ALU.mult))
                free()
                L.tell(tt(mixT[:, j, :], sig[:, j, :], sig[:, 8 + j, :], ALU.add))
            dve.sem_inc(mix_ready, 1)
            for j in range(DC):
                b = V.take(dve)
                xs = xT[:, j, SEQ:TOK].rearrange("p (b s) -> p b s", s=NS)
                tmp = rstd[:, 0:NSM].rearrange("p (b s) -> p b s", s=NS)
                L.tell(dve.scalar_tensor_tensor(xT[:, j, 0:SEQ], b[:, 0:SEQ], modT[:, 16 + j, 0:1], xT[:, j, 0:SEQ], ALU.mult, ALU.add),
                       wait=False)
                L.tell(tt(tmp, b[:, SEQ:TOK].rearrange("p (b s) -> p b s", s=NS),
                          modT[:, 16 + j, 1:9].unsqueeze(2).broadcast_to([P, NB, NS]), ALU.mult))
                L.tell(tt(xs, xs, tmp, ALU.add), x1_ready)
                free()
            norm(2, 32, 24, 56)
            for c in range(DC):
                for r in range(1, 4):
                    L.tell(cp(hT[:, c, SEQ + 32 * r:SEQ + 32 * r + 32], hT[:, c, SEQ:TOK]), wait=(c == DC - 1))
            for c in range(DC):
                L.tell(cp(gspread[:, 2 * c * P:(2 * c + 1) * P], modT[:, 40 + c, 0:1].broadcast_to([P, P])), wait=False)
                L.tell(cp(gspread[:, (2 * c + 1) * P:(2 * c + 2) * P].rearrange("p (r b s) -> p r b s", r=4, b=NB),
                          modT[:, 40 + c, 1:9].unsqueeze(1).unsqueeze(3).broadcast_to([P, 4, NB, NS])))
            dve.sem_inc(sq_pre, 1)
            dve.sem_inc(h_ready, 1)

            dve.wait_ge(rows_ready, 1)
            L.tell(dve.memset(zeros, 0.0), zeros_ready)

            def route(t):
                dve.wait_ge(s_ready, 4 * (t + 1))
                for hp in range(16):
                    s, v, ix = ssb[:, hp, :], topv[:, hp, :], topi[:, hp, :]
                    L.tell(dve.max(v[:, 0:8], s))
                    L.tell(dve.max_index(ix[:, 0:8], v[:, 0:8], s))
                    L.tell(dve.match_replace(s, v[:, 0:8], s, TAKEN))
                    L.tell(dve.max(v[:, 8:16], s))
                    L.tell(dve.max_index(ix[:, 8:16], v[:, 8:16], s))
                dve.sem_inc(s_used, 1)
                L.tell(cp(topf[:, :, :], topi[:, :, :]))
                tv = topv[:, :, :].rearrange("p (h q) k -> p h q k", q=2)
                tf = topf[:, :, :].rearrange("p (h q) k -> p h q k", q=2)
                for h in range(PH):
                    L.tell(tt(cand[:, h], tv[:, h, 0, :].unsqueeze(2).broadcast_to([P, PTOP, PTOP]),
                              tv[:, h, 1, :].unsqueeze(1).broadcast_to([P, PTOP, PTOP]), ALU.add))
                for h in range(PH):
                    cf = cand[:, h].rearrange("p i j -> p (i j)")
                    L.tell(dve.max(tops[:, h, 0:8], cf))
                    L.tell(dve.max_index(posu[:, h, 0:8], tops[:, h, 0:8], cf))
                    L.tell(dve.match_replace(cf, tops[:, h, 0:8], cf, TAKEN))
                    L.tell(dve.max(tops[:, h, 8:16], cf))
                    L.tell(dve.max_index(posu[:, h, 8:16], tops[:, h, 8:16], cf))
                L.tell(cp(gsm[:, 0, :], tops[:, :, 0:1].rearrange("p h k -> p (h k)")))
                L.tell(tt(tops[:, :, :], tops[:, :, :], gsm[:, 0, :].unsqueeze(2).broadcast_to([P, PH, PTOP]), ALU.subtract))
                for q in range(2):
                    if q == 0:
                        L.tell(ts(posq[:, :, :], posu[:, :, :], 4, None, ALU.logical_shift_right))
                    else:
                        L.tell(ts(posq[:, :, :], posu[:, :, :], 15, None, ALU.bitwise_and))
                    L.tell(cp(posf[:, :, :], posq[:, :, :]))
                    for h in range(PH):
                        L.tell(tt(onehot[:, h], posf[:, h, :].unsqueeze(2).broadcast_to([P, PTOP, PTOP]),
                                  cv["iota"].unsqueeze(1).broadcast_to([P, PTOP, PTOP]), ALU.is_equal))
                        L.tell(tt(onehot[:, h], onehot[:, h], tf[:, h, q, :].unsqueeze(1).broadcast_to([P, PTOP, PTOP]), ALU.mult))
                    L.tell(dve.tensor_reduce(pick[:, q], onehot, AX, ALU.add))
                L.tell(dve.scalar_tensor_tensor(pick[:, 0], pick[:, 0], float(PK), pick[:, 1], ALU.mult, ALU.add))
                ef, gf = pick[:, 0].rearrange("p h k -> p (h k)"), tops[:, :, :].rearrange("p h k -> p (h k)")
                if t < 2:
                    L.tell(cp(eidx[:, t, :], ef))
                    L.tell(cp(gate[:, t, :], gf))
                else:
                    for q in range(4):
                        s, e = 32 * q, 32 * q + 32
                        L.tell(cp(eidx[s:e, t, 0:32], ef[s:e, s:e]))
                        L.tell(cp(gate[s:e, t, 0:32], gf[s:e, s:e]))
                dve.sem_inc(routed, 1)

            dve.sem_inc(u_used, UR)
            u_round = 0

            def output(t):
                dve.wait_ge(acc_done, t + 1)
                if t:
                    dve.wait_ge(y_out, 16 * t)
                acc = bankD[2 * (t % 2):2 * (t % 2) + 2]
                for half in range(2):
                    s, e = half * 512, (half + 1) * 512
                    if t < 2:
                        L.tell(tt(yout[:, s:e], acc[half][:, :], g2tok[:, 0, s:e], ALU.mult))
                    else:
                        L.tell(cp(yout[:, s:e], acc[half][:, :]))
                dve.sem_inc(acc_taken, 1)
                if t < 2:
                    L.tell(tt(yout, yout, x1tok[:, t, :], ALU.add))
                dve.sem_inc(y_ready, 1)

            route(0)
            for t in range(3):
                rounds, n = SLOTS[t] // UR, SLOTS[t]
                with dve.Fori(0, rounds // 2) as i:
                    for par in range(2):
                        for r in range(UR):
                            dve.wait_ge(u_in[r], i * 32 + (u_round + par + 1) * 16)
                            dve.tensor_tensor_reduce(out=urows[r], in0=urows[r], in1=h2tok[:, t, :], scale=1.0, scalar=0.0,
                                                     op0=ALU.mult, op1=ALU.add, accum_out=dcur[:, par, r:r + 1]).then_inc(u_used, 1)
                        dve.wait_ge(u_used, i * (2 * UR) + (u_round + par + 2) * UR)
                        dve.tensor_copy(dots[:, t, bass.ds(i * (2 * UR) + par * UR, UR)], dcur[:, par, :]).then_inc(dcur_copied, 1)
                        dve.wait_ge(dcur_copied, i * 2 + (u_round + par + 1))
                u_round += rounds
                dve.sem_inc(dots_ready, 1)
                dve.wait_ge(gelu_done, 2 * t + 2)
                nh = n // PTOP
                gv = gate[:, t, 0:n].rearrange("p (h k) -> p h k", k=PTOP)
                L.tell(dve.tensor_reduce(gsm[:, 1, 0:nh], gv, AX, ALU.add))
                L.tell(dve.reciprocal(gsm[:, 1, 0:nh], gsm[:, 1, 0:nh]))
                L.tell(tt(gv, gv, gsm[:, 1, 0:nh].unsqueeze(2).broadcast_to([P, nh, PTOP]), ALU.mult))
                L.tell(tt(dots[:, t, 0:n], dots[:, t, 0:n], gate[:, t, 0:n], ALU.mult), w_ready)
                if t < 2:
                    route(t + 1)
                if t == 2:
                    output(0)
            output(1)
            output(2)
            dve.wait_ge(acc_done, 4)
            for half in range(2):
                s, e = half * 512, (half + 1) * 512
                L.tell(tt(yout[0:NSM, s:e], bankD[2 + half][0:NSM, :], g2tok[0:NSM, 1, s:e], ALU.mult))
                L.tell(tt(yout[0:NSM, s:e], yout[0:NSM, s:e], x1tok[0:NSM, 2, s:e], ALU.add))
            dve.sem_inc(y_ready, 1)


def kernel(**inputs):
    import concourse.bacc as bacc
    from concourse.bass_utils import run_bass_kernel_spmd

    nc = bacc.Bacc("TRN2", target_bir_lowering=False, num_devices=1)
    arrays = {name: np.ascontiguousarray(inputs[name]) for name in INPUTS}
    arrays["consts"] = const_table()
    ap = {}
    for name, a in arrays.items():
        t = nc.dram_tensor(name, a.shape, mybir.dt.from_np(a.dtype), kind="ExternalInput").ap()
        if name in LAYERED or name in ("x_prompt",):
            t = t[0]
        if name in ("cache_k", "cache_v"):
            t = t.rearrange("g p n d -> (g p) (n d)")
        if name == "cache_kidx":
            t = t.rearrange("g p d -> (g p) d")
        if name == "x_sample":
            t = t.rearrange("b s d -> (b s) d")
        ap[name] = t
    outs = {}
    for name, shape, view in OUTPUTS:
        t = nc.dram_tensor("out_" + name, shape, F32, kind="ExternalOutput").ap()
        outs[name] = t.rearrange(view[0]) if view[0] else t
        if view[1]:
            outs[name] = outs[name][0]
    layer_program(nc, **ap, **outs)
    r = run_bass_kernel_spmd(nc, [arrays], core_ids=[0])
    return tuple(r.results[0]["out_" + name] for name, _, _ in OUTPUTS)
```

```python
from contextlib import ExitStack

import numpy as np

import concourse.bass as bass
from concourse import mybir

F32 = mybir.dt.float32
BF16 = mybir.dt.bfloat16
I32 = mybir.dt.int32
U32 = mybir.dt.uint32
ALU = mybir.AluOpType
ACT = mybir.ActivationFunctionType
AX = mybir.AxisListType.X

P = 128
D = 1024
DC = D // P
SEQ = 256
NB, NS = 8, 4
NSM = NB * NS
TOK = SEQ + NSM
PAST, PAGE = 1024, 128
NPG = PAST // PAGE
NPHYS = 80
CONV = 512
CC = CONV // P
NH, NKV, HD = 8, 2, 64
NG = NH // NKV
TOPK_P, TOPK_S = SEQ // 4, 256
IDX_SCALE = (64 ** -0.5) * (8 ** -0.5)
QSCALE = HD ** -0.5
EPS = 1e-6
NEG = -1e30
TAKEN = -3e38
NKEY = PAST + NSM
PH, PK, PTOP = 8, 128, 16
ROWS = [P, P, NSM]
COLS = [0, P, SEQ]
SLOTS = [PH * PTOP, PH * PTOP, PH * PTOP // 4]

C_XIN, C_ATT, C_Q, C_K, C_V, C_QI, C_KI, C_WI, C_GA = 0, 1536, 1536, 2048, 2176, 2304, 2816, 2880, 2888
ZW = C_GA - C_ATT
Z_K, Z_V, Z_QI, Z_KI, Z_WI = C_K - C_ATT, C_V - C_ATT, C_QI - C_ATT, C_KI - C_ATT, C_WI - C_ATT

CONST_PARTS = [("ident", P), ("cos", 3 * 32), ("sin", 3 * 32), ("causal0", P), ("causal1", 2 * P), ("newbias", NSM),
               ("rep", 2 * P), ("repT", 2 * NSM), ("headsel", NH), ("sum4", NSM), ("iota", PTOP)]


def const_table():
    t = {n: np.zeros((P, w), np.float32) for n, w in CONST_PARTS}
    t["ident"][:] = np.eye(P, dtype=np.float32)
    freq = (np.float32(10000.0) ** (-np.arange(32, dtype=np.float32) / np.float32(32))).astype(np.float32)
    row = np.arange(P)
    for tile, pos in enumerate([row, row + P, PAST + row % NS]):
        ang = pos.astype(np.float32)[:, None] * freq[None, :]
        t["cos"][:, 32 * tile:32 * tile + 32] = np.cos(ang)
        t["sin"][:, 32 * tile:32 * tile + 32] = np.sin(ang)
    key = np.arange(2 * P)
    t["causal0"][:] = np.where(key[None, :P] <= row[:, None], 0.0, NEG)
    t["causal1"][:] = np.where(key[None, :] <= row[:, None] + P, 0.0, NEG)
    tok = np.arange(NSM)
    t["newbias"][:NSM] = np.where((tok[None, :] // NS == tok[:, None] // NS) & (tok[None, :] <= tok[:, None]), 0.0, NEG)
    for g in range(2):
        src = (4 * g + row // 32) * NS + row % NS
        t["rep"][src, P * g + row] = 1.0
        t["repT"][row, NSM * g + src] = 1.0
    t["headsel"][row, (row // NS) % NH] = 1.0
    t["sum4"][row, row % NSM] = 1.0
    t["iota"][:] = np.arange(PTOP)[None, :]
    return np.concatenate([t[n] for n, _ in CONST_PARTS], axis=1)


INPUTS = ["x_prompt", "x_sample", "cache_k", "cache_v", "cache_kidx", "state_conv", "page_table", "c_prompt", "c_sample",
          "w_ada", "b_ada", "norm1_w", "w_in", "conv_w", "q_norm_w", "k_norm_w", "w_conv_out", "w_attn_out", "w_out",
          "norm2_w", "peer_w_q", "peer_sub_keys", "peer_u", "peer_v"]
LAYERED = set(INPUTS) - {"x_prompt", "x_sample", "page_table", "c_prompt", "c_sample"}
OUTPUTS = [("y_prompt", (1, SEQ, D), ("a t d -> (a t) d", False)), ("y_sample", (NB, NS, D), ("b s d -> (b s) d", False)),
           ("k_prompt", (1, 1, SEQ, NKV, HD), ("l b t n d -> (l b t) (n d)", False)),
           ("v_prompt", (1, 1, SEQ, NKV, HD), ("l b t n d -> (l b t) (n d)", False)),
           ("kidx_prompt", (1, 1, SEQ, HD), ("l b t d -> (l b t) d", False)),
           ("conv_prompt", (1, 1, 2, CONV), ("l b t d -> (l b t) d", False)),
           ("k_sample", (1, NB, NS, NKV, HD), ("l b t n d -> (l b t) (n d)", False)),
           ("v_sample", (1, NB, NS, NKV, HD), ("l b t n d -> (l b t) (n d)", False)),
           ("kidx_sample", (1, NB, NS, HD), ("l b t d -> (l b t) d", False)),
           ("conv_sample", (1, NB, 2, CONV), (None, True))]


class Lane:

    def __init__(self, eng, own):
        self.eng, self.own, self.count = eng, own, {}

    def tell(self, ins, sem=None, wait=True):
        sem = self.own if sem is None else sem
        self.count[id(sem)] = self.count.get(id(sem), 0) + 1
        ins.then_inc(sem, 1)
        if wait:
            self.eng.wait_ge(sem, self.count[id(sem)])


class Banks:

    def __init__(self, banks, full, free):
        self.banks, self.full, self.free, self.n = banks, full, free, 0

    def open(self, pe):
        if self.n >= len(self.banks):
            pe.wait_ge(self.free, self.n - len(self.banks) + 1)
        self.n += 1
        return self.banks[(self.n - 1) % len(self.banks)]

    def close(self, mm, n=1):
        mm.then_inc(self.full, n)

    def take(self, eng):
        eng.wait_ge(self.full, self.n + 1)
        self.n += 1
        return self.banks[(self.n - 1) % len(self.banks)]


def layer_program(nc, x_prompt, x_sample, cache_k, cache_v, cache_kidx, state_conv, page_table, c_prompt, c_sample,
                  w_ada, b_ada, norm1_w, w_in, conv_w, q_norm_w, k_norm_w, w_conv_out, w_attn_out, w_out, norm2_w,
                  peer_w_q, peer_sub_keys, peer_u, peer_v, consts,
                  y_prompt, y_sample, k_prompt, v_prompt, kidx_prompt, conv_prompt, k_sample, v_sample, kidx_sample,
                  conv_sample):
    with ExitStack() as ctx:
        def sb(name, shape, dt=F32):
            return ctx.enter_context(nc.sbuf_tensor(name, shape, dt))

        def sem(name):
            return ctx.enter_context(nc.semaphore(name))

        WSLOT = DC * 512
        NW = 2
        UR = 8
        ctab = sb("ctab", [P, sum(w for _, w in CONST_PARTS)])
        cv, at = {}, 0
        for n, w in CONST_PARTS:
            cv[n] = ctab[:, at:at + w]
            at += w
        ident = cv["ident"]
        ident_bf = sb("ident_bf", [P, P], BF16)
        rep_bf = sb("rep_bf", [NSM, 2 * P], BF16)
        ones = sb("ones", [P, P])
        smallT = sb("smallT", [P, 76])
        qkw = sb("qkw", [P, P])
        cT = sb("cT", [P, DC, 32])
        modT = sb("modT", [P, 48, 9])
        ab = sb("ab", [P, DC, 9])
        xT = sb("xT", [P, DC, TOK])
        hT = sb("hT", [P, DC, 3 * P])
        oT = sb("oT", [P, NG, TOK])
        rstd = sb("rstd", [P, TOK])
        stateT = sb("stateT", [P, CC, NB * 2])
        pages = sb("pages", [1, NB * NPG], I32)

        big = sb("big", [P, NB * NPG * P + 2 * NPG * P + 2 * NPG * 64 + NW * WSLOT])
        o = NB * NPG * P
        vpages = big[:, 0:o].rearrange("p (g d) -> p g d", d=P)
        NI, NK = 6, 3
        ipages = big[:, o:o + NI * NPG * 64].rearrange("p (r g d) -> p r g d", r=NI, d=64)
        kpages = big[:, o:o + NK * NPG * P].rearrange("p (r g d) -> p r g d", r=NK, d=P)
        o += NK * NPG * P
        wring = [big[:, o + i * WSLOT:o + (i + 1) * WSLOT] for i in range(NW)]
        urows = [big[:, i * D:(i + 1) * D] for i in range(UR)]
        vrows = [big[:, (UR + i) * D:(UR + i + 1) * D] for i in range(UR)]
        assert 2 * UR * D + PH * 256 <= o + NW * WSLOT
        gspread = big[:, 0:16 * P]
        route_work = [big[:, a:a + 6 * 256].rearrange("p (w h i j) -> p w h i j", w=3, h=2, i=PTOP) for a in (16 * P, 2 * UR * D)]

        zall = sb("zall", [P, 32 * P])
        zbuf = zall[:, 0:3 * ZW].rearrange("p (t z) -> p t z", z=ZW)
        subraw = zall[:, 0:16 * P].rearrange("p (j d) -> p j d", d=P)
        subT = zall[:, 16 * P:32 * P].rearrange("p (j k) -> p j k", k=P)

        r5 = sb("r5", [P, 16 * TOK + 12 * TOK + CC * (SEQ + 2) + CC * NB * 6])
        sig = r5[:, 0:16 * TOK].rearrange("p (j t) -> p j t", t=TOK)
        o = 16 * TOK
        bufX = r5[:, o:o + 4 * TOK].rearrange("p (j t) -> p j t", t=TOK)
        bufB = r5[:, o + 4 * TOK:o + 8 * TOK].rearrange("p (j t) -> p j t", t=TOK)
        bufC = r5[:, o + 8 * TOK:o + 12 * TOK].rearrange("p (j t) -> p j t", t=TOK)
        mixT = r5[:, o + 8 * TOK:o + 16 * TOK].rearrange("p (j t) -> p j t", t=TOK)
        o += 12 * TOK
        uP = r5[:, o:o + CC * (SEQ + 2)].rearrange("p (j t) -> p j t", t=SEQ + 2)
        o += CC * (SEQ + 2)
        uS = r5[:, o:o + CC * NB * 6].rearrange("p (j b t) -> p j b t", b=NB, t=6)
        aT = bufB
        qpT = r5[:, 0:16 * 3 * P].rearrange("p (j t) -> p j t", t=3 * P)
        ssb = r5[:, 48 * P:64 * P].rearrange("p (j k) -> p j k", k=P)
        dots = r5[:, 64 * P:67 * P].rearrange("p (t s) -> p t s", t=3)
        eidx = r5[:, 67 * P:70 * P].bitcast(I32).rearrange("p (t s) -> p t s", t=3)
        tails = sb("tails", [P, CC, 2 + NB * 2])

        R6 = 9 * D
        r6 = sb("r6", [P, R6])
        cut = [0]

        def part(n, start=None):
            if start is not None:
                cut[0] = start
            v = r6[:, cut[0]:cut[0] + n]
            cut[0] += n
            assert cut[0] <= R6, cut[0]
            return v
        xin = part(3 * D, 0).rearrange("p (t d) -> p t d", d=D)
        crow = part(D)
        srow = part(CONV)
        sq = part(DC * TOK)
        smallrows = part(P)[0:76]
        qkrow = part(P)
        qTz = part(NH * P, 0).rearrange("p (h t) -> p h t", t=P)
        qiTz = part(NH * P).rearrange("p (h t) -> p h t", t=P)
        probs = part(NH * 2 * P)
        probsT = part(NH * 2 * P)
        relu = part(2 * 2 * P)
        rope = [part(10 * 32) for _ in range(2)]
        scP = part(2 * P)
        workP = part(2 * P)
        orow = part(4 * P)
        kidup = part(P)
        mbP = part(P).bitcast(BF16)
        adarow = part(512)
        reluS = part(2 * NKEY, 0).rearrange("p (g k) -> p g k", k=NKEY)
        probsS = part(NKEY, 0)
        KB = 4
        kbT = part(KB * PAST).rearrange("p (r k) -> p r k", k=PAST)
        scS = part(NKEY)
        mbS = part(NKEY // 2).bitcast(BF16)[0:NSM]
        ibT = part(2 * 4 * P, cut[0]).rearrange("p (r k) -> p r k", k=4 * P)
        probsST = part(NPG * P + P, cut[0] - 8 * P)
        tailrows = part(CONV, 0)[0:2 + NB * 2]
        x1tok = part(3 * D, 0).rearrange("p (t d) -> p t d", d=D)
        h2tok = part(3 * D).rearrange("p (t d) -> p t d", d=D)
        g2tok = part(2 * D).rearrange("p (t d) -> p t d", d=D)
        yout = part(D)
        kT = sb("kT", [P, TOK])
        kiT = sb("kiT", [P, TOK])
        wis = sb("wis", [P, 3, NH])
        stat = sb("stat", [P, 64])
        best = sb("best", [P, 8])
        nmax = sb("nmax", [P, NH])
        rsum = sb("rsum", [P, 3, NH])
        rinv = sb("rinv", [P, NH])
        QIs = sb("QIs", [P, 2, NB * 32])
        Qs = sb("Qs", [P, NB * 32])
        wrow = sb("wrow", [P, 2])
        wsel = sb("wsel", [P, 2, NSM])
        cuts = [0]

        def small(n):
            cuts[0] += n
            return zall[:, cuts[0] - n:cuts[0]]
        topv = small(16 * PTOP).rearrange("p (j k) -> p j k", k=PTOP)
        topi = small(16 * PTOP).bitcast(U32).rearrange("p (j k) -> p j k", k=PTOP)
        topf = small(16 * PTOP).rearrange("p (j k) -> p j k", k=PTOP)
        tops = small(P).rearrange("p (h k) -> p h k", k=PTOP)
        posu = small(P).bitcast(U32).rearrange("p (h k) -> p h k", k=PTOP)
        posq = small(P).bitcast(U32).rearrange("p (h k) -> p h k", k=PTOP)
        posf = small(P).rearrange("p (h k) -> p h k", k=PTOP)
        pick = small(2 * P).rearrange("p (q h k) -> p q h k", q=2, k=PTOP)
        gate = small(3 * P).rearrange("p (t s) -> p t s", t=3)
        gsm = sb("gsm", [P, 2, PH])
        dcur = sb("dcur", [P, UR])
        ucur = sb("ucur", [P, 2, UR], I32)
        vcur = sb("vcur", [P, 2, UR], I32)
        NDG = 4
        o = 2 * UR * D + PH * 256
        diag = big[:, o:o + NDG * P].rearrange("p (n k) -> p n k", k=P)
        zeros = big[:, o + NDG * P:o + NDG * P + 512]

        bankA = [ctx.enter_context(nc.psum_tensor(f"bankA{i}", [P, 512], F32)) for i in range(4)]
        bankD = [ctx.enter_context(nc.psum_tensor(f"bankD{i}", [P, 512], F32)) for i in range(4)]

        span = ((0, 512), (512, 512), (1024, NSM))

        in_small, in_x, in_pages, in_const = sem("in_small"), sem("in_x"), sem("in_pages"), sem("in_const")
        w_landed = [sem(f"w_landed{i}") for i in range(NW)]
        kv_out, y_out, conv_out_done = sem("kv_out"), sem("y_out"), sem("conv_out_done")
        gelu_done, row_asked, round_begun = sem("gelu_done"), sem("row_asked"), sem("round_begun")
        sub_landed, exp_done = sem("sub_landed"), sem("exp_done")
        v_landed = sem("v_landed")
        k_landed = [sem(f"k_landed{i}") for i in range(NK)]
        i_landed = [sem(f"i_landed{i}") for i in range(NI)]
        adarow_ready, mod_ready, qk_ready, co_ready = (
            sem("adarow_ready"), sem("mod_ready"), sem("qk_ready"), sem("co_ready"))
        a_full, a_free, d_full, d_free = sem("a_full"), sem("a_free"), sem("d_full"), sem("d_free")
        act_seq, dve_seq, pool_seq = sem("act_seq"), sem("dve_seq"), sem("pool_seq")
        consts_ready = sem("consts_ready")
        xT_ready, cT_ready, sq_ready, var_ready, sd_ready, h_ready = (
            sem("xT_ready"), sem("cT_ready"), sem("sq_ready"), sem("var_ready"), sem("sd_ready"), sem("h_ready"))
        z_ready, qk_var, qk_sd, rope_done = sem("z_ready"), sem("qk_var"), sem("qk_sd"), sem("rope_done")
        qT_ready, qT_used = sem("qT_ready"), sem("qT_used")
        mb_ready = sem("mb_ready")
        nmax_ready, probs_ready, probsT_ready, probs_used, probsT_used, orow_ready = (
            sem("nmax_ready"), sem("probs_ready"), sem("probsT_ready"), sem("probs_used"), sem("probsT_used"),
            sem("orow_ready"))
        relu_ready, relu_used, orow_used = sem("relu_ready"), sem("relu_used"), sem("orow_used")
        gspread_ready = sem("gspread_ready")
        Qs_ready, wsel_ready, ib_ready, ib_used, kb_ready, kb_used, reluS_ready, reluS_used = (
            sem("Qs_ready"), sem("wsel_ready"), sem("ib_ready"), sem("ib_used"), sem("kb_ready"), sem("kb_used"),
            sem("reluS_ready"), sem("reluS_used"))
        mbS_ready, oT_ready, gates_ready, conv_in, a_ready, tail_ready, tail_row = (
            sem("mbS_ready"), sem("oT_ready"), sem("gates_ready"), sem("conv_in"), sem("a_ready"), sem("tail_ready"),
            sem("tail_row"))
        mix_ready, x1_ready, rows_ready, subT_ready, qp_ready, s_ready, s_used = (
            sem("mix_ready"), sem("x1_ready"), sem("rows_ready"), sem("subT_ready"), sem("qp_ready"), sem("s_ready"),
            sem("s_used"))
        routed, zeros_ready = sem("routed"), sem("zeros_ready")
        u_in = [sem(f"u_in{i}") for i in range(UR)]
        v_in = [sem(f"v_in{i}") for i in range(UR)]
        u_used, v_used, dots_ready, w_ready, diag_ready, acc_done, acc_taken, y_ready = (
            sem("u_used"), sem("v_used"), sem("dots_ready"), sem("w_ready"), sem("diag_ready"),
            sem("acc_done"), sem("acc_taken"), sem("y_ready"))
        dcur_copied, ucur_done, vcur_done = sem("dcur_copied"), sem("ucur_done"), sem("vcur_done")

        def cols(w, a, n):
            k = w.shape[0] // P
            return [(w[:, a:a + n].rearrange("(k p) n -> p k n", p=P), k, n)]

        attn_rows = w_attn_out.rearrange("(n g d) m -> n g d m", n=NKV, g=NG)
        groups = ([("ada", cols(w_ada, 512 * i, 512)) for i in range(4)]
                  + [("q", cols(w_in, C_Q, 512)), ("kvw", cols(w_in, C_K, 256) + cols(w_in, C_KI, 72)),
                     ("qi", cols(w_in, C_QI, 512))]
                  + [("conv", cols(w_in, 512 * i, 512)) for i in range(3)]
                  + [("gate", cols(w_in, C_GA + 512 * i, 512)) for i in range(4)]
                  + [("convout", cols(w_conv_out, 0, D))]
                  + [("ada", cols(w_ada, 512 * i, 512)) for i in range(4, 12)]
                  + [("attnout", [(None, 4, D)] * 2)]
                  + [("out", cols(w_out, 512 * i, 512)) for i in range(2)]
                  + [("peerq", cols(peer_w_q, 512 * i, 512)) for i in range(4)])
        names = [n for n, _ in groups]

        def weights(eng, g):
            eng.wait_ge(w_landed[g % NW], 16 * sum(len(groups[j][1]) for j in range(g % NW, g + 1, NW)))
            k, n = groups[g][1][0][1], sum(part[2] for part in groups[g][1])
            n = D if names[g] == "attnout" else n
            return wring[g % NW][:, 0:k * n].rearrange("p (k n) -> p k n", n=n)

        block = ctx.enter_context(nc.Block())

        released = {}
        turned_i, turned_k = {}, {}
        v_done = {}
        FILL = {"start": 1, "T2": 2, "select": (2, 2), "softmax": (2, 3), "next": (1, 0)}
        CHUNK = 32
        CHUNKS = [(t, first) for t in range(3) for first in range(0, SLOTS[t], CHUNK)]
        SCORE_AFTER = [5, 9, 13]
        logit_bank = {}

        @block.tensor
        def _(pe):
            A, V = Banks(bankA, a_full, a_free), Banks(bankD, d_full, d_free)
            pe.wait_ge(in_const, 16)
            pe.wait_ge(consts_ready, 4)
            pe.wait_ge(in_small, 16 * 9)
            b = V.open(pe)
            V.close(pe.transpose(b[:, 0:76], smallrows[:, :], ident[0:76, 0:76]))
            b = V.open(pe)
            for c in range(DC):
                mm = pe.transpose(b[:, 9 * c:9 * c + 9], crow[0:9, c * P:(c + 1) * P], ident[0:9, 0:9])
            V.close(mm)
            b = V.open(pe)
            for c in range(CC):
                mm = pe.transpose(b[:, 16 * c:16 * c + 16], srow[0:16, c * P:(c + 1) * P], ident[0:16, 0:16])
            V.close(mm)
            b = V.open(pe)
            V.close(pe.matmul(b[:, 0:P], ones[0:1, :], qkrow[0:1, :], start=True, stop=True))
            pe.wait_ge(in_x, 48)
            for c in range(DC):
                b = V.open(pe)
                for t in range(3):
                    mm = pe.transpose(b[:, COLS[t]:COLS[t] + ROWS[t]], xin[0:ROWS[t], t, c * P:(c + 1) * P],
                                      ident[0:ROWS[t], 0:ROWS[t]])
                V.close(mm)

            g = 0
            ada_done = [0]

            def ada(g):
                w = weights(pe, g)
                b = A.open(pe)
                for k in range(DC):
                    q = k % 4
                    mm = pe.matmul(b[32 * q:32 * q + 32, :], cT[:, k, :], w[:, k, :], start=(k < 4), stop=(k >= 4),
                                   skip_group_check=True)
                A.close(mm)
                released[g] = (a_full, A.n)
                ada_done[0] += 1
                pe.wait_ge(adarow_ready, ada_done[0])
                b = A.open(pe)
                for j in range(4):
                    mm = pe.matmul(b[:, 9 * j:9 * j + 9], adarow[:, j * P:(j + 1) * P], cv["sum4"][:, 0:9], start=True, stop=True)
                A.close(mm)

            def norm_sum(n):
                b = V.open(pe)
                for c in range(DC):
                    pe.wait_ge(sq_ready, n[c])
                    mm = pe.matmul(b[:, 0:TOK], ones[:, :], sq[:, c * TOK:(c + 1) * TOK], start=(c == 0), stop=(c == DC - 1))
                V.close(mm)

            norm_sum([1] * DC)
            pe.wait_ge(cT_ready, 1)
            for _ in range(4):
                ada(g)
                g += 1
            pe.wait_ge(h_ready, 1)

            for name in ("q", "kvw", "qi"):
                w = weights(pe, g)
                width = w.shape[2]
                b = A.open(pe)
                for k in range(DC):
                    q = k % 4
                    mm = pe.matmul(b[32 * q:32 * q + 32, 0:width], hT[:, k, SEQ:TOK], w[:, k, :], start=(k < 4), stop=(k >= 4),
                                   skip_group_check=True)
                A.close(mm)
                for t in range(2):
                    b = A.open(pe)
                    for k in range(DC):
                        mm = pe.matmul(b[:, 0:width], hT[:, k, COLS[t]:COLS[t] + P], w[:, k, :], start=(k == 0), stop=(k == DC - 1))
                    A.close(mm)
                released[g] = (a_full, A.n)
                g += 1
                ada_done[0] += 1
                pe.wait_ge(adarow_ready, ada_done[0])
                b = A.open(pe)
                A.close(pe.matmul(b[0:NSM, 0:width], cv["sum4"], adarow[:, 0:width], start=True, stop=True))

            blocks = iter([(g + i // 4, i % 4) for i in range(28)])
            g += 7

            def fill(n):
                for _ in range(n):
                    gg, j = next(blocks, (None, None))
                    if gg is None:
                        return
                    if j == 0:
                        slot[0] = weights(pe, gg)
                    w, b = slot[0], A.open(pe)
                    for k in range(DC):
                        mm = pe.matmul(b[:, 0:TOK], w[:, k, j * P:(j + 1) * P], hT[:, k, 0:TOK], start=(k == 0), stop=(k == DC - 1))
                    A.close(mm)
                    released[gg] = (a_full, A.n)

            slot = [None]
            def turn_tile(t, n):
                r, z = ROWS[t], zbuf[0:ROWS[t], t, :]
                idt = ident[0:r, 0:r]
                pe.wait_ge(rope_done, n)
                b = V.open(pe)
                for gg in range(NG):
                    mm = pe.transpose(b[:, gg * r:gg * r + r], orow[0:r, gg * P:(gg + 1) * P], idt)
                V.close(mm)
                b = V.open(pe)
                for c in range(4):
                    mm = pe.transpose(b[:, c * r:c * r + r], z[:, Z_QI + c * P:Z_QI + (c + 1) * P], idt)
                V.close(mm)
                b = V.open(pe)
                pe.transpose(b[:, 0:r], z[:, Z_K:Z_K + P], idt)
                V.close(pe.transpose(b[:, P:P + r], kidup[0:r, :], idt))

            fill(FILL["start"])
            turn_tile(2, 1)
            b = V.open(pe)
            for gg in range(2):
                mm = pe.matmul(b[:, NH * gg:NH * gg + NH], cv["rep"][0:NSM, gg * P:(gg + 1) * P], wis[0:NSM, 2, :],
                               start=True, stop=True)
            V.close(mm)

            fill(FILL["T2"])
            for t in range(2):
                W = P * (t + 1)
                turn_tile(t, 2 + t)
                pe.wait_ge(qT_ready, t + 2)
                for hp in range(NH // 2):
                    b = A.open(pe)
                    for j in range(2):
                        mm = pe.matmul(b[:, j * W:(j + 1) * W], qiTz[:, 2 * hp + j, :], kiT[:, 0:W], start=True, stop=True)
                    A.close(mm)
                fill(FILL["select"][t])
                pe.wait_ge(mb_ready, t + 1)
                for hp in range(NH // 2):
                    b = V.open(pe)
                    logit_bank[t, hp] = b
                    for j in range(2):
                        pe.matmul(b[:, j * W:(j + 1) * W], qTz[:, 2 * hp + j, :], kT[:, 0:W], start=True, stop=False)
                        mm = pe.matmul(b[:, j * W:(j + 1) * W], ident_bf[:, :], mbP[:, 0:W], start=False, stop=True)
                    V.close(mm)
                fill(FILL["softmax"][t])
                pe.wait_ge(probs_ready, NH * (t + 1))
                per = t + 1
                for q in range(NH * per // 4):
                    b = A.open(pe)
                    for j in range(4):
                        mm = pe.transpose(b[:, j * P:(j + 1) * P], probs[:, (4 * q + j) * P:(4 * q + j + 1) * P], ident)
                    A.close(mm)
                pe.wait_ge(probsT_ready, 2 if t == 0 else 6)
                b = V.open(pe)
                for h in range(NH):
                    for c in range(per):
                        kv = zbuf[:, c, Z_V + (h // NG) * HD:Z_V + (h // NG + 1) * HD]
                        mm = pe.matmul(b[:, h * HD:(h + 1) * HD], probsT[:, (h * per + c) * P:(h * per + c + 1) * P], kv,
                                       start=(c == 0), stop=(c == per - 1))
                V.close(mm)
                pe.wait_ge(orow_ready, t + 1)
                b = V.open(pe)
                for gg in range(NG):
                    mm = pe.transpose(b[:, gg * P:(gg + 1) * P], orow[:, gg * P:(gg + 1) * P], ident)
                V.close(mm)
                fill(FILL["next"][t])
            pe.wait_ge(oT_ready, 2)
            def turn_i(bb):
                pe.wait_ge(i_landed[bb % NI], 16 * NPG * (bb // NI + 1))
                b = A.open(pe)
                for q in range(4):
                    mm = pe.transpose(b[:, q * P:(q + 1) * P],
                                      ipages[:, bb % NI, 2 * q:2 * q + 2, :].rearrange("p g d -> p (g d)"), ident)
                A.close(mm)
                turned_i[bb] = A.n

            turn_i(0)
            for G in range(2):
                sbank = [V.open(pe) for _ in range(3)]
                for bb in range(4 * G, 4 * G + 4):
                    b4 = bb % 4
                    if bb + 1 < NB:
                        turn_i(bb + 1)
                    fill(1)
                    pe.wait_ge(ib_ready, bb + 1)
                    for pg in range(NPG):
                        mm = pe.matmul(sbank[pg // 4][32 * b4:32 * b4 + 32, (pg % 4) * P:(pg % 4 + 1) * P],
                                       QIs[:, pg % 2, bb * 32:(bb + 1) * 32], ibT[:, bb % 2, (pg // 2) * P:(pg // 2 + 1) * P],
                                       start=True, stop=True)
                    mm.then_inc(ib_used, 1)
                mm = pe.matmul(sbank[2][:, 0:NSM], QIs[:, 0, G * P:(G + 1) * P], kiT[:, SEQ:TOK], start=True, stop=True)
                V.close(mm, 3)
            pe.wait_ge(reluS_ready, 6)
            pe.wait_ge(wsel_ready, 1)
            for a, n in span:
                b = V.open(pe)
                for G in range(2):
                    mm = pe.matmul(b[0:NSM, 0:n], wsel[:, G, :], reluS[:, G, a:a + n], start=(G == 0), stop=(G == 1))
                V.close(mm)

            def turn_k(bb):
                slot_k = (bb + 1) % NK
                pe.wait_ge(k_landed[slot_k], 16 * NPG * (bb // NK + 1))
                for half in range(2):
                    b = A.open(pe)
                    for q in range(4):
                        mm = pe.transpose(b[:, q * P:(q + 1) * P], kpages[:, slot_k, 4 * half + q, :], ident)
                    A.close(mm)
                turned_k[bb] = A.n

            fill(28)
            pe.wait_ge(a_ready, 1)
            w = weights(pe, g)
            for j in range(DC):
                b = A.open(pe)
                for k in range(4):
                    mm = pe.matmul(b[:, 0:TOK], w[:, k, j * P:(j + 1) * P], aT[:, k, 0:TOK], start=(k == 0), stop=(k == 3))
                A.close(mm)
            released[g] = (a_full, A.n)
            g += 1
            for bb in range(4):
                turn_k(bb)
                ada(g)
                ada(g + 1)
                g += 2
            pe.wait_ge(mbS_ready, 1)
            for G in range(2):
                sbank = [V.open(pe) for _ in range(3)]
                logit_bank[2, G] = sbank
                for i, (a, n) in enumerate(span):
                    pe.matmul(sbank[i][:, 0:n], rep_bf[:, G * P:(G + 1) * P], mbS[:, a:a + n], start=True, stop=False,
                              skip_group_check=True)
                for b4 in range(4):
                    bb = 4 * G + b4
                    pe.wait_ge(kb_ready, 2 * bb + 2)
                    for half in range(2):
                        mm = pe.matmul(sbank[half][32 * b4:32 * b4 + 32, :], Qs[:, bb * 32:(bb + 1) * 32],
                                       kbT[:, bb % KB, half * 512:(half + 1) * 512], start=False, stop=(b4 == 3),
                                       skip_group_check=True)
                    mm.then_inc(kb_used, 1)
                mm = pe.matmul(sbank[2][:, 0:NSM], Qs[:, G * P:(G + 1) * P], kT[:, SEQ:TOK], start=False, stop=True,
                               skip_group_check=True)
                V.close(mm, 3)
                if G == 0:
                    for bb in range(4, NB):
                        turn_k(bb)
                pe.wait_ge(probs_ready, 2 * NH + 3 * (G + 1))
                for half in range(2):
                    b = A.open(pe)
                    for q in range(4):
                        pg = 4 * half + q
                        mm = pe.transpose(b[:, q * P:(q + 1) * P], probsS[:, pg * P:(pg + 1) * P], ident)
                    A.close(mm)
                b = A.open(pe)
                A.close(pe.transpose(b[0:NSM, 0:P], probsS[:, PAST:NKEY], ident))
                pe.wait_ge(probsT_ready, 6 + 3 * (G + 1))
                pe.wait_ge(v_landed, 16 * NB * NPG)
                b = V.open(pe)
                for b4 in range(4):
                    bb = 4 * G + b4
                    for pg in range(NPG):
                        pe.matmul(b[32 * b4:32 * b4 + 32, 0:P], probsST[:, pg * P + 32 * b4:pg * P + 32 * b4 + 32],
                                  vpages[:, bb * NPG + pg, :], start=(pg == 0), stop=False)
                    mm = pe.matmul(b[32 * b4:32 * b4 + 32, 0:P], probsST[0:NSM, NPG * P + 32 * b4:NPG * P + 32 * b4 + 32],
                                   zbuf[0:NSM, 2, Z_V:Z_V + P], start=False, stop=True)
                V.close(mm)
                v_done[0] = (d_full, V.n)
                pe.wait_ge(orow_ready, 3 + G)
                b = V.open(pe)
                V.close(pe.transpose(b[:, 0:P], orow[:, 0:P], ident))

            pe.wait_ge(tail_ready, 1)
            b = V.open(pe)
            for c in range(CC):
                mm = pe.transpose(b[0:18, c * P:(c + 1) * P], tails[:, c, :], ident)
            V.close(mm)
            pe.wait_ge(oT_ready, 4)
            w = weights(pe, g)
            for j in range(DC):
                b = V.open(pe)
                for k in range(4):
                    mm = pe.matmul(b[:, 0:TOK], w[:, k, j * P:(j + 1) * P], oT[:, k, 0:TOK], start=(k == 0), stop=(k == 3))
                V.close(mm)
            released[g] = (d_full, V.n)
            g += 1
            pe.wait_ge(mix_ready, 1)
            for _ in range(2):
                w = weights(pe, g)
                for j in range(4):
                    b = V.open(pe)
                    for k in range(DC):
                        mm = pe.matmul(b[:, 0:TOK], w[:, k, j * P:(j + 1) * P], mixT[:, k, :], start=(k == 0), stop=(k == DC - 1))
                    V.close(mm)
                released[g] = (d_full, V.n)
                g += 1
            norm_sum([2 + c for c in range(DC)])
            pe.wait_ge(sub_landed, 16)
            for q in range(4):
                b = A.open(pe)
                for j in range(4):
                    mm = pe.transpose(b[:, j * P:(j + 1) * P], subraw[:, 4 * q + j, :], ident)
                A.close(mm)
            pe.wait_ge(h_ready, 2)
            def score_bank(t, q):
                pe.wait_ge(qp_ready, 4 * q + 4)
                b = A.open(pe)
                for j in range(4):
                    hp = 4 * q + j
                    mm = pe.matmul(b[:, j * P:(j + 1) * P], qpT[:, hp, t * P:(t + 1) * P],
                                   subT[:, (hp % 2) * PH + hp // 2, :], start=True, stop=True)
                A.close(mm)

            pe.wait_ge(subT_ready, 4)
            for j in range(16):
                if j % 4 == 0:
                    w = weights(pe, g + j // 4)
                b = A.open(pe)
                for k in range(DC):
                    mm = pe.matmul(b[:, 0:TOK], w[:, k, (j % 4) * P:(j % 4 + 1) * P], hT[:, k, 0:TOK], start=(k == 0), stop=(k == DC - 1))
                A.close(mm)
                released[g + j // 4] = (a_full, A.n)
                if j in SCORE_AFTER:
                    score_bank(0, SCORE_AFTER.index(j))
            g += 4
            score_bank(0, 3)
            for t in range(3):
                for half in range(2):
                    b = A.open(pe)
                    for q in range(4):
                        mm = pe.transpose(b[:, q * P:(q + 1) * P], hT[:, 4 * half + q, t * P:(t + 1) * P], ident)
                    A.close(mm)
            for t in range(3):
                for half in range(2):
                    b = A.open(pe)
                    for q in range(4):
                        mm = pe.transpose(b[0:ROWS[t], q * P:(q + 1) * P], xT[:, 4 * half + q, COLS[t]:COLS[t] + ROWS[t]], ident)
                    A.close(mm)
            pe.wait_ge(gspread_ready, 1)
            for s in range(2):
                for half in range(2):
                    b = A.open(pe)
                    for q in range(4):
                        mm = pe.transpose(b[:, q * P:(q + 1) * P], gspread[:, ((4 * half + q) * 2 + s) * P:((4 * half + q) * 2 + s + 1) * P], ident)
                    A.close(mm)
            for t in range(1, 3):
                for q in range(4):
                    score_bank(t, q)
            pe.wait_ge(d_free, V.n)

            pe.wait_ge(zeros_ready, 1)
            pe.sem_inc(v_used, UR)
            v_round = 0
            for t in range(3):
                acc = bankD[2 * (t % 2):2 * (t % 2) + 2]
                if t == 2:
                    pe.wait_ge(acc_taken, 1)
                for half in range(2):
                    pe.matmul(acc[half][:, :], zeros[:, 0:P], zeros, start=True, stop=False, skip_group_check=True)
                rounds = SLOTS[t] // UR
                with pe.Fori(0, rounds) as i:
                    for r in range(UR):
                        pe.wait_ge(v_in[r], (i + (v_round + 1)) * 16)
                        pe.wait_ge(diag_ready, (i + v_round) * UR + (r + 1))
                        pe.matmul(acc[0][:, :], diag[:, r % NDG, :], vrows[r][:, 0:512], start=False, stop=False,
                                  skip_group_check=True)
                        pe.matmul(acc[1][:, :], diag[:, r % NDG, :], vrows[r][:, 512:D], start=False, stop=False,
                                  skip_group_check=True).then_inc(v_used, 1)
                v_round += rounds
                for half in range(2):
                    mm = pe.matmul(acc[half][:, :], zeros[:, 0:P], zeros, start=False, stop=True, skip_group_check=True)
                mm.then_inc(acc_done, 1)
            pe.wait_ge(y_ready, 3)
            pe.wait_ge(acc_taken, 2)
            for half in range(2):
                mm = pe.matmul(bankD[2 + half][0:NSM, :], cv["sum4"], yout[:, half * 512:(half + 1) * 512],
                               start=True, stop=True)
            mm.then_inc(acc_done, 1)

        @block.sync
        def _(sp):
            small = [(b_ada.rearrange("(j p) -> j p", p=P), 0, 48), (norm1_w.rearrange("(j p) -> j p", p=P), 48, 8),
                     (norm2_w.rearrange("(j p) -> j p", p=P), 56, 8), (conv_w.rearrange("w (j p) -> (w j) p", p=P), 64, 12)]
            sp.dma_start(crow[0:1, :], c_prompt).then_inc(in_small, 16)
            sp.dma_start(crow[1:9, :], c_sample).then_inc(in_small, 16)
            sp.dma_start(ctab[:, :], consts).then_inc(in_const, 16)
            for src, a, n in small:
                sp.dma_start(smallrows[a:a + n, :], src).then_inc(in_small, 16)
            sp.dma_start(qkrow[0:1, 0:HD], q_norm_w.rearrange("(a d) -> a d", a=1)).then_inc(in_small, 16)
            sp.dma_start(qkrow[0:1, HD:P], k_norm_w.rearrange("(a d) -> a d", a=1)).then_inc(in_small, 16)
            sp.dma_start(srow[0:16, :], state_conv.rearrange("b j c -> (b j) c")).then_inc(in_small, 16)
            for t in range(2):
                sp.dma_start(xin[:, t, :], x_prompt[t * P:(t + 1) * P, :]).then_inc(in_x, 16)
            sp.dma_start(xin[0:NSM, 2, :], x_sample).then_inc(in_x, 16)

            for g, (name, what) in enumerate(groups):
                if g >= NW:
                    sp.wait_ge(*released[g - NW])
                if name == "attnout":
                    dst = wring[g % NW].rearrange("p (k n) -> p k n", n=D)
                    for n in range(NKV):
                        sp.dma_start(dst[n * HD:(n + 1) * HD, :, :],
                                     attn_rows[n].rearrange("g d m -> d g m")).then_inc(w_landed[g % NW], 16)
                else:
                    k, n, at = what[0][1], sum(part[2] for part in what), 0
                    dst = wring[g % NW][:, 0:k * n].rearrange("p (k n) -> p k n", n=n)
                    for src, _, width in what:
                        sp.dma_start(dst[:, :, at:at + width], src).then_inc(w_landed[g % NW], 16)
                        at += width
                if name == "attnout":
                    sp.wait_ge(oT_ready, 4)
                    sp.wait_ge(kv_out, 16 * 9)
                    sp.dma_start(subraw, peer_sub_keys.rearrange("q h k d -> k (q h) d")).then_inc(sub_landed, 16)
            sp.wait_ge(tail_row, 1)
            sp.dma_start(conv_prompt, tailrows[0:2, :]).then_inc(conv_out_done, 16)
            sp.dma_start(conv_sample.rearrange("b j c -> (b j) c"), tailrows[2:18, :]).then_inc(conv_out_done, 16)
            for t in range(2):
                sp.wait_ge(y_ready, t + 1)
                sp.dma_start(y_prompt[t * P:(t + 1) * P, :], yout[:, :]).then_inc(y_out, 16)
            sp.wait_ge(y_ready, 4)
            sp.dma_start(y_sample, yout[0:NSM, :]).then_inc(y_out, 16)
            sp.wait_ge(y_out, 16 * 3)
            sp.wait_ge(conv_out_done, 16 * 2)

        @block.gpsimd
        def _(pool):
            lane = Lane(pool, pool_seq)
            pool.dma_start(pages[:, :], page_table.rearrange("(a b) g -> a (b g)", a=1)).then_inc(in_pages, 16)
            pool.memset(ones[:, :], 1.0).then_inc(consts_ready, 1)
            pool.memset(Qs[:, :], 0.0).then_inc(consts_ready, 1)
            pool.memset(QIs[:, :, :], 0.0).then_inc(consts_ready, 1)
            pool.memset(uP[:, :, 0:2], 0.0).then_inc(consts_ready, 1)
            pool.wait_ge(in_pages, 16)

            def fetch(dst, src, done, b):
                with pool.Fori(0, NPG) as g:
                    page = pool.value_load(pages[0:1, bass.ds(g + b * NPG, 1)], min_val=0, max_val=NPHYS - 1)
                    pool.dma_start(dst[:, bass.ds(g, 1), :].rearrange("p a d -> p (a d)"),
                                   src[bass.ds(page * PAGE, PAGE), :]).then_inc(done, 16)
            for b in range(NI):
                fetch(ipages[:, b], cache_kidx, i_landed[b], b)
            for b in range(NB):
                fetch(vpages[:, b * NPG:(b + 1) * NPG], cache_v, v_landed, b)
            for n, (t, k_out, v_out, i_out) in enumerate((
                    (2, k_sample, v_sample, kidx_sample),
                    (0, k_prompt[0:P, :], v_prompt[0:P, :], kidx_prompt[0:P, :]),
                    (1, k_prompt[P:SEQ, :], v_prompt[P:SEQ, :], kidx_prompt[P:SEQ, :]))):
                pool.wait_ge(rope_done, n + 1)
                r = ROWS[t]
                pool.dma_start(k_out, zbuf[0:r, t, Z_K:Z_K + P]).then_inc(kv_out, 16)
                pool.dma_start(v_out, zbuf[0:r, t, Z_V:Z_V + P]).then_inc(kv_out, 16)
                pool.dma_start(i_out, zbuf[0:r, t, Z_KI:Z_KI + HD]).then_inc(kv_out, 16)
            for b in range(NI, NB):
                pool.wait_ge(a_full, turned_i[b - NI])
                fetch(ipages[:, b % NI], cache_kidx, i_landed[b % NI], b)
            for b in range(NB):
                pool.wait_ge(a_full, turned_i[(3, 5, 7)[b]] if b < NK else turned_k[b - NK])
                fetch(kpages[:, (b + 1) % NK], cache_k, k_landed[(b + 1) % NK], b)

            for full, n in released[len(groups) - 1], released[len(groups) - 2], v_done[0]:
                pool.wait_ge(full, n)
            streams = {"u": (urows, ucur, peer_u, u_in, u_used, ucur_done), "v": (vrows, vcur, peer_v, v_in, v_used, vcur_done)}
            done = {"u": 0, "v": 0}
            behind = {}

            def gather(rounds, *parts):
                with pool.Fori(0, rounds // 2) as i:
                    for par in range(2):
                        for kind, t in parts:
                            ring, cur, table, landed, used, cur_done = streams[kind]
                            first = behind.get((kind, t), 0) + par
                            pool.tensor_copy(cur[:, par, :], eidx[:, t, bass.ds(i * (2 * UR) + first * UR, UR)])\
                                .then_inc(cur_done, 1)
                            pool.wait_ge(cur_done, i * 2 + (done[kind] + par + 1))
                            for r in range(UR):
                                pool.wait_ge(used, i * (2 * UR) + ((done[kind] + par) * UR + r + 1))
                                pool.sem_inc(row_asked, 1)
                                pool.indirect_dma_start(ring[r], None, table, bass.IndirectOffsetOnAxis(
                                    ap=cur[:, par, r:r + 1], axis=0)).then_inc(landed[r], 16)
                for kind, t in parts:
                    done[kind] += rounds
                    behind[kind, t] = behind.get((kind, t), 0) + rounds

            step = CHUNK // UR
            pool.wait_ge(rows_ready, 1)
            pool.wait_ge(routed, 1)
            gather(2 * step, ("u", 0))
            gather(2 * step, ("v", 0), ("u", 0))
            pool.wait_ge(routed, 2)
            gather(2 * step, ("v", 0), ("u", 1))
            gather(2 * step, ("v", 1), ("u", 1))
            pool.wait_ge(routed, 3)
            gather(step, ("v", 1), ("u", 2))
            gather(step, ("v", 1))
            gather(step, ("v", 2))

        @block.scalar
        def _(act):
            A = Banks(bankA, a_full, a_free)
            L = Lane(act, act_seq)

            def ada(g):
                b = A.take(act)
                L.tell(act.activation(adarow[:, :], b[:, :], ACT.Copy), adarow_ready)
                act.sem_inc(a_free, 1)
                b = A.take(act)
                L.tell(act.activation(modT[:, 4 * g:4 * g + 4, :].rearrange("p j b -> p (j b)"), b[:, 0:36], ACT.Copy), mod_ready)
                act.sem_inc(a_free, 1)

            act.wait_ge(xT_ready, DC)
            L.tell(act.activation(sq, xT[:, :, :].rearrange("p c t -> p (c t)"), ACT.Square), sq_ready)
            act.wait_ge(var_ready, 1)
            L.tell(act.activation(rstd[:, :], rstd[:, :], ACT.Sqrt), sd_ready)
            for g in range(4):
                ada(g)
            for part in (((0, 512),), ((Z_K, 256), (Z_KI, 72)), ((Z_QI, 512),)):
                width = sum(n for _, n in part)
                if part[0][0] == Z_QI:
                    act.sem_inc(qk_ready, 1)
                    act.wait_ge(qk_var, 1)
                    L.tell(act.activation(stat[:, 0:30], stat[:, 0:30], ACT.Sqrt), qk_sd)
                b = A.take(act)
                L.tell(act.activation(adarow[:, 0:width], b[:, 0:width], ACT.Copy), adarow_ready)
                act.sem_inc(a_free, 1)
                for t in range(3):
                    b, at = A.take(act), 0
                    for a, n in part:
                        L.tell(act.activation(zbuf[0:ROWS[t], t, a:a + n], b[0:ROWS[t], at:at + n], ACT.Copy))
                        at += n
                    act.sem_inc(a_free, 1)
            act.sem_inc(z_ready, 1)

            blocks = iter(range(28))

            def fill(n):
                for _ in range(n):
                    j = next(blocks, None)
                    if j is None:
                        return
                    b = A.take(act)
                    if j < 12:
                        L.tell(act.activation((bufX, bufB, bufC)[j // 4][:, j % 4, :], b[:, 0:TOK], ACT.Copy), conv_in)
                    else:
                        L.tell(act.activation(sig[:, j - 12, :], b[:, 0:TOK], ACT.Copy))
                    act.sem_inc(a_free, 1)

            fill(FILL["start"])
            fill(FILL["T2"])
            for t in range(2):
                W = P * (t + 1)
                for hp in range(4):
                    b = A.take(act)
                    if 4 * t + hp >= 2:
                        act.wait_ge(relu_used, 4 * t + hp - 1)
                    dst = relu[:, 0:2 * W] if hp % 2 == 0 else probs[:, 0:2 * W]
                    L.tell(act.activation(dst, b[:, 0:2 * W], ACT.Relu), relu_ready)
                    act.sem_inc(a_free, 1)
                fill(FILL["select"][t])
                for h in range(NH):
                    act.wait_ge(nmax_ready, NH // 2 * t + h // 2 + 1)
                    src = logit_bank[t, h // 2][:, (h % 2) * W:(h % 2 + 1) * W]
                    L.tell(act.activation(probs[:, h * W:(h + 1) * W], src, ACT.Exp, bias=nmax[:, h:h + 1], scale=QSCALE,
                                          accum_out=rsum[:, t, h:h + 1]), probs_ready)
                fill(FILL["softmax"][t])
                for q in range(2 * (t + 1)):
                    b = A.take(act)
                    L.tell(act.activation(probsT[:, q * 512:(q + 1) * 512], b[:, :], ACT.Copy), probsT_ready)
                    act.sem_inc(a_free, 1)
                fill(FILL["next"][t])
            act.wait_ge(oT_ready, 2)

            def copy_i(bb):
                b = A.take(act)
                if bb >= 2:
                    act.wait_ge(ib_used, bb - 1)
                L.tell(act.activation(ibT[:, bb % 2, :], b[:, :], ACT.Copy), ib_ready)
                act.sem_inc(a_free, 1)

            def copy_k(bb):
                for half in range(2):
                    b = A.take(act)
                    if bb >= KB:
                        act.wait_ge(kb_used, bb - KB + 1)
                    L.tell(act.activation(kbT[:, bb % KB, half * 512:(half + 1) * 512], b[:, :], ACT.Copy), kb_ready)
                    act.sem_inc(a_free, 1)

            copy_i(0)
            for bb in range(NB):
                if bb + 1 < NB:
                    copy_i(bb + 1)
                fill(1)
            fill(28)
            for j in range(DC):
                b = A.take(act)
                L.tell(act.activation((bufX, bufC)[j // 4][:, j % 4, :], b[:, 0:TOK], ACT.Copy), co_ready)
                act.sem_inc(a_free, 1)
            for bb in range(4):
                copy_k(bb)
                ada(4 + 2 * bb)
                ada(5 + 2 * bb)
            L.tell(act.activation(sig[:, :, :].rearrange("p j t -> p (j t)"), sig[:, :, :].rearrange("p j t -> p (j t)"), ACT.Sigmoid),
                   gates_ready)
            for G in range(2):
                if G == 0:
                    copy_k(4)
                    copy_k(5)
                act.wait_ge(nmax_ready, NH + G + 1)
                for i, (a, n) in enumerate(span):
                    src = logit_bank[2, G][i][:, 0:n]
                    L.tell(act.activation(probsS[:, a:a + n], src, ACT.Exp, bias=nmax[:, 0:1], scale=QSCALE,
                                          accum_out=rsum[:, 2, 4 * G + i:4 * G + i + 1]), probs_ready)
                if G == 0:
                    copy_k(6)
                    copy_k(7)
                for half in range(2):
                    b = A.take(act)
                    if G == 1:
                        act.wait_ge(orow_ready, 3)
                    L.tell(act.activation(probsST[:, half * 512:(half + 1) * 512], b[:, :], ACT.Copy), probsT_ready)
                    act.sem_inc(a_free, 1)
                b = A.take(act)
                L.tell(act.activation(probsST[0:NSM, NPG * P:NPG * P + P], b[0:NSM, 0:P], ACT.Copy), probsT_ready)
                act.sem_inc(a_free, 1)
            for c in range(DC):
                act.wait_ge(x1_ready, c + 1)
                L.tell(act.activation(sq[:, c * TOK:(c + 1) * TOK], xT[:, c, :], ACT.Square), sq_ready)
            act.wait_ge(var_ready, 2)
            L.tell(act.activation(rstd[:, :], rstd[:, :], ACT.Sqrt), sd_ready)
            act.wait_ge(sub_landed, 16)
            for q in range(4):
                b = A.take(act)
                L.tell(act.activation(subT[:, 4 * q:4 * q + 4, :].rearrange("p j k -> p (j k)"), b[:, :], ACT.Copy), subT_ready)
                act.sem_inc(a_free, 1)
            act.wait_ge(h_ready, 2)
            def copy_scores():
                b = A.take(act)
                q = L.count.get(id(s_ready), 0) % 4
                L.tell(act.activation(ssb[:, 4 * q:4 * q + 4, :].rearrange("p j k -> p (j k)"), b[:, :], ACT.Copy), s_ready)
                act.sem_inc(a_free, 1)

            for j in range(16):
                b = A.take(act)
                L.tell(act.activation(qpT[:, j, 0:SEQ], b[:, 0:SEQ], ACT.Copy), wait=False)
                L.tell(act.activation(qpT[:, j, SEQ:3 * P].rearrange("p (r t) -> p r t", r=4),
                                      b[:, SEQ:TOK].unsqueeze(1).broadcast_to([P, 4, NSM]), ACT.Copy), qp_ready)
                act.sem_inc(a_free, 1)
                if j in SCORE_AFTER:
                    copy_scores()
            copy_scores()
            act.wait_ge(conv_out_done, 32)
            for t in range(3):
                for half in range(2):
                    b = A.take(act)
                    L.tell(act.activation(h2tok[:, t, half * 512:(half + 1) * 512], b[:, :], ACT.Copy))
                    act.sem_inc(a_free, 1)
            for t in range(3):
                for half in range(2):
                    b = A.take(act)
                    L.tell(act.activation(x1tok[0:ROWS[t], t, half * 512:(half + 1) * 512], b[0:ROWS[t], :], ACT.Copy))
                    act.sem_inc(a_free, 1)
            for s in range(2):
                for half in range(2):
                    b = A.take(act)
                    L.tell(act.activation(g2tok[:, s, half * 512:(half + 1) * 512], b[:, :], ACT.Copy))
                    act.sem_inc(a_free, 1)
            act.sem_inc(rows_ready, 1)
            def scores(t):
                if t:
                    act.wait_ge(s_used, t)
                for q in range(4):
                    copy_scores()

            scores(1)
            def gelus(c):
                t, first = CHUNKS[c]
                act.wait_ge(dots_ready, c + 1)
                if first == 0:
                    L.tell(act.activation(gate[:, t, 0:SLOTS[t]], gate[:, t, 0:SLOTS[t]], ACT.Exp), exp_done)
                chunk = dots[:, t, first:first + CHUNK]
                L.tell(act.activation(chunk, chunk, ACT.Gelu_apprx_tanh), gelu_done)

            def diagonals(c):
                t, first = CHUNKS[c]
                act.wait_ge(w_ready, c + 1)
                with act.Fori(0, CHUNK // UR) as i:
                    for r in range(UR):
                        act.wait_ge(v_used, (i + c * (CHUNK // UR)) * UR + (r + 1 + UR - NDG))
                        act.activation(diag[:, r % NDG, :], ident, ACT.Copy, scale=dots[:, t, bass.ds(i * UR + (first + r), 1)])\
                           .then_inc(diag_ready, 1)

            for c in range(len(CHUNKS)):
                gelus(c)
                if CHUNKS[c] == (0, SLOTS[0] - CHUNK):
                    scores(2)
                if c:
                    diagonals(c - 1)
            diagonals(len(CHUNKS) - 1)

        @block.vector
        def _(dve):
            V = Banks(bankD, d_full, d_free)
            L = Lane(dve, dve_seq)
            tt, ts, cp = dve.tensor_tensor, dve.tensor_scalar, dve.tensor_copy

            def free():
                dve.sem_inc(d_free, 1)

            dve.wait_ge(in_const, 16)
            L.tell(cp(ident_bf[:, :], ident))
            L.tell(cp(rep_bf[:, :], cv["rep"][0:NSM, :]))
            dve.wait_ge(consts_ready, 4)
            L.tell(cp(smallT[:, :], V.take(dve)[:, 0:76])); free()
            L.tell(dve.memset(cT[:, :, :], 0.0))
            L.tell(cp(cT[:, :, 0:9], V.take(dve)[:, 0:72].rearrange("p (c b) -> p c b", b=9)), cT_ready); free()
            L.tell(cp(stateT[:, :, :].rearrange("p c b -> p (c b)"), V.take(dve)[:, 0:64])); free()
            L.tell(cp(qkw[:, :], V.take(dve)[:, 0:P])); free()
            for c in range(DC):
                L.tell(cp(xT[:, c, :], V.take(dve)[:, 0:TOK]), xT_ready); free()

            def bias(a, e):
                dve.wait_ge(mod_ready, e // 4)
                L.tell(tt(modT[:, a:e, :], modT[:, a:e, :], smallT[:, a:e].unsqueeze(2).broadcast_to([P, e - a, 9]), ALU.add))

            def norm_scale(scale, w):
                L.tell(ts(ab[:, :, :], modT[:, scale:scale + DC, :], 1.0, None, ALU.add))
                L.tell(tt(ab[:, :, :], ab[:, :, :], smallT[:, w:w + DC].unsqueeze(2).broadcast_to([P, DC, 9]), ALU.mult))

            def norm_unit(n):
                b = V.take(dve)
                L.tell(ts(rstd[:, :], b[:, 0:TOK], 1.0 / D, EPS, ALU.mult, ALU.add), var_ready); free()
                dve.wait_ge(sd_ready, n)
                L.tell(dve.reciprocal(rstd[:, :], rstd[:, :]))
                L.tell(tt(hT[:, :, 0:TOK], xT[:, :, :], rstd[:, :].unsqueeze(1).broadcast_to([P, DC, TOK]), ALU.mult))

            def norm_shift(shift):
                for c in range(DC):
                    L.tell(ts(hT[:, c, 0:SEQ], hT[:, c, 0:SEQ], ab[:, c, 0:1], modT[:, shift + c, 0:1], ALU.mult, ALU.add),
                           wait=False)
                hs = hT[:, :, SEQ:TOK].rearrange("p c (b s) -> p c b s", s=NS)
                L.tell(tt(hs, hs, ab[:, :, 1:9].unsqueeze(3).broadcast_to([P, DC, NB, NS]), ALU.mult))
                L.tell(tt(hs, hs, modT[:, shift:shift + DC, 1:9].unsqueeze(3).broadcast_to([P, DC, NB, NS]), ALU.add))

            norm_unit(1)
            bias(0, 16)
            norm_scale(8, 48)
            norm_shift(0)
            dve.sem_inc(h_ready, 1)

            L.tell(dve.memset(qTz, 0.0), wait=False)
            L.tell(dve.memset(qiTz, 0.0), wait=False)
            L.tell(dve.memset(stat[:, 0:30], 1.0))

            def rotate(z, a, nh, t, r):
                x1 = z[:, a:a + nh * HD].rearrange("p (h d) -> p h d", d=HD)[:, :, 0:32]
                x2 = z[:, a:a + nh * HD].rearrange("p (h d) -> p h d", d=HD)[:, :, 32:64]
                cs = cv["cos"][0:r, 32 * t:32 * t + 32].unsqueeze(1).broadcast_to([r, nh, 32])
                sn = cv["sin"][0:r, 32 * t:32 * t + 32].unsqueeze(1).broadcast_to([r, nh, 32])
                t1, t2 = (rope[i][0:r, 0:nh * 32].rearrange("p (h d) -> p h d", d=32) for i in range(2))
                L.tell(tt(t1, x2, sn, ALU.mult), wait=False)
                L.tell(tt(t2, x1, sn, ALU.mult))
                L.tell(tt(x1, x1, cs, ALU.mult), wait=False)
                L.tell(tt(x2, x2, cs, ALU.mult))
                L.tell(tt(x1, x1, t1, ALU.subtract), wait=False)
                L.tell(tt(x2, x2, t2, ALU.add))

            def heads(t):
                return zbuf[0:ROWS[t], t, 0:10 * HD].rearrange("p (h d) -> p h d", d=HD), stat[0:ROWS[t], 10 * t:10 * t + 10]

            dve.wait_ge(qk_ready, 1)
            for t in range(3):
                zq, st = heads(t)
                sqv = probs[0:ROWS[t], 0:10 * HD].rearrange("p (h d) -> p h d", d=HD)
                L.tell(tt(sqv, zq, zq, ALU.mult))
                L.tell(dve.tensor_reduce(st, sqv, AX, ALU.add))
            L.tell(ts(stat[:, 0:30], stat[:, 0:30], 1.0 / HD, EPS, ALU.mult, ALU.add), qk_var)
            dve.wait_ge(qk_sd, 1)
            L.tell(dve.reciprocal(stat[:, 0:30], stat[:, 0:30]))
            for t in (2, 0, 1):
                r = ROWS[t]
                zq, st = heads(t)
                L.tell(tt(zq, zq, st.unsqueeze(2).broadcast_to([r, 10, HD]), ALU.mult))
                L.tell(tt(zq[:, 0:8], zq[:, 0:8], qkw[0:r, 0:HD].unsqueeze(1).broadcast_to([r, 8, HD]), ALU.mult), wait=False)
                L.tell(tt(zq[:, 8:10], zq[:, 8:10], qkw[0:r, HD:P].unsqueeze(1).broadcast_to([r, 2, HD]), ALU.mult))
                rotate(zbuf[0:r, t, :], 0, 10, t, r)
            dve.wait_ge(z_ready, 1)
            for n, t in enumerate((2, 0, 1)):
                r, z = ROWS[t], zbuf[0:ROWS[t], t, :]
                rotate(z, Z_QI, 9, t, r)
                L.tell(cp(orow[0:r, :].rearrange("p (g n d) -> p n g d", g=NG, n=NKV),
                          z[:, 0:512].rearrange("p (n g d) -> p n g d", n=NKV, g=NG)), wait=False)
                L.tell(cp(kidup[0:r, 0:HD], z[:, Z_KI:Z_KI + HD]), wait=False)
                L.tell(cp(kidup[0:r, HD:P], z[:, Z_KI:Z_KI + HD]), wait=False)
                L.tell(ts(wis[0:r, t, :], z[:, Z_WI:Z_WI + NH], IDX_SCALE, None, ALU.mult), rope_done)

                b = V.take(dve)
                bq = b[:, 0:NG * r].rearrange("p (g t) -> p g t", t=r)
                if t == 2:
                    for nn in range(NKV):
                        s, e = nn * HD, (nn + 1) * HD
                        dst = Qs[s:e, :].rearrange("p (b h s) -> p b h s", h=NH, s=NS)[:, :, nn * NG:(nn + 1) * NG, :]
                        for gg in range(NG):
                            L.tell(cp(dst[:, :, gg, :], bq[s:e, gg, :].rearrange("p (b s) -> p b s", s=NS)))
                    free()
                else:
                    for nn in range(NKV):
                        s, e = nn * HD, (nn + 1) * HD
                        L.tell(cp(qTz[s:e, nn * NG:(nn + 1) * NG, :], bq[s:e]))
                    free()
                b = V.take(dve)
                bi = b[:, 0:4 * r].rearrange("p (c t) -> p c t", t=r)
                for par in range(2):
                    s, e = par * HD, (par + 1) * HD
                    if t == 2:
                        for v in range(2):
                            dst = QIs[v * HD:(v + 1) * HD, v, :].rearrange("p (b h s) -> p b h s", h=NH, s=NS)
                            for c in range(4):
                                L.tell(cp(dst[:, :, 2 * c + par, :], bi[s:e, c, :].rearrange("p (b s) -> p b s", s=NS)))
                    else:
                        L.tell(cp(qiTz[s:e].rearrange("p (c q) t -> p c q t", q=2)[:, :, par, :], bi[s:e]))
                free()
                b = V.take(dve)
                L.tell(cp(kT[:, COLS[t]:COLS[t] + r], b[:, 0:r]), wait=False)
                L.tell(cp(kiT[:, COLS[t]:COLS[t] + r], b[:, P:P + r]), qT_ready)
                free()
                if t == 2:
                    b = V.take(dve)
                    for G in range(2):
                        L.tell(tt(stat[:, 16:24], b[:, NH * G:NH * G + NH], cv["headsel"], ALU.mult))
                        L.tell(dve.tensor_reduce(wrow[:, G:G + 1], stat[:, 16:24], AX, ALU.add))
                        L.tell(ts(wsel[:, G, :], cv["repT"][:, G * NSM:(G + 1) * NSM], wrow[:, G:G + 1], None, ALU.mult))
                    dve.sem_inc(wsel_ready, 1)
                    free()
                    continue

                W = P * (t + 1)
                L.tell(cp(scP[:, 0:W], cv["causal0"] if t == 0 else cv["causal1"]))
                for hp in range(4):
                    dve.wait_ge(relu_ready, 4 * t + hp + 1)
                    src = relu if hp % 2 == 0 else probs
                    for j in range(2):
                        L.tell(dve.scalar_tensor_tensor(scP[:, 0:W], src[:, j * W:(j + 1) * W],
                                                        wis[:, t, 2 * hp + j:2 * hp + j + 1], scP[:, 0:W], ALU.mult, ALU.add))
                    dve.sem_inc(relu_used, 1)
                src = scP
                for _ in range(TOPK_P // 8):
                    L.tell(dve.max(best[:, :], src[:, 0:W]))
                    L.tell(dve.match_replace(workP[:, 0:W], best[:, :], src[:, 0:W], TAKEN))
                    src = workP
                L.tell(ts(workP[:, 0:W], workP[:, 0:W], -1e35, NEG, ALU.is_gt, ALU.mult))
                L.tell(tt(mbP[:, 0:W], workP[:, 0:W], cv["causal0"] if t == 0 else cv["causal1"], ALU.add), mb_ready)
                for hp in range(4):
                    b = V.take(dve)
                    L.tell(dve.tensor_reduce(stat[:, 32 + 2 * hp:34 + 2 * hp], b[:, 0:2 * W].rearrange("p (h k) -> p h k", k=W),
                                             AX, ALU.max))
                    L.tell(ts(nmax[:, 2 * hp:2 * hp + 2], stat[:, 32 + 2 * hp:34 + 2 * hp], -QSCALE, None, ALU.mult), nmax_ready)
                dve.wait_ge(probs_ready, NH * (t + 1))
                dve.sem_inc(d_free, 4)
                L.tell(dve.reciprocal(rinv[:, :], rsum[:, t, :]))
                b = V.take(dve)
                L.tell(tt(orow.rearrange("p (g n d) -> p n g d", g=NG, n=NKV),
                          b[:, :].rearrange("p (n g d) -> p n g d", n=NKV, g=NG),
                          rinv[:, :].rearrange("p (n g) -> p n g", n=NKV).unsqueeze(3).broadcast_to([P, NKV, NG, HD]), ALU.mult),
                       orow_ready)
                free()
                b = V.take(dve)
                L.tell(cp(oT[:, :, COLS[t]:COLS[t] + P], b[:, :].rearrange("p (g t) -> p g t", t=P)), oT_ready)
                free()

            def conv(c):
                L.tell(tt(uP[:, c, 2:SEQ + 2], bufX[:, c, 0:SEQ], bufC[:, c, 0:SEQ], ALU.mult), wait=False)
                L.tell(cp(uS[:, c, :, 0:2], stateT[:, c, :].rearrange("p (b j) -> p b j", j=2)), wait=False)
                L.tell(tt(uS[:, c, :, 2:6], bufX[:, c, SEQ:TOK].rearrange("p (b s) -> p b s", s=NS),
                          bufC[:, c, SEQ:TOK].rearrange("p (b s) -> p b s", s=NS), ALU.mult))
                L.tell(cp(tails[:, c, 0:2], uP[:, c, SEQ:SEQ + 2]), wait=False)
                L.tell(cp(tails[:, c, 2:18].rearrange("p (b j) -> p b j", j=2), uS[:, c, :, 4:6]), wait=False)
                for u, y, n in ((uP[:, c], bufX[:, c, 0:SEQ], SEQ), (uS[:, c], bufX[:, c, SEQ:TOK].rearrange("p (b s) -> p b s", s=NS), NS)):
                    tap = [u[:, j:j + n] if n == SEQ else u[:, :, j:j + n] for j in range(3)]
                    wc = [smallT[:, 64 + 4 * j + c:65 + 4 * j + c] for j in range(3)]
                    L.tell(ts(y, tap[2], wc[2], None, ALU.mult))
                    L.tell(dve.scalar_tensor_tensor(y, tap[0], wc[0], y, ALU.mult, ALU.add))
                    L.tell(dve.scalar_tensor_tensor(y, tap[1], wc[1], y, ALU.mult, ALU.add))
                L.tell(tt(aT[:, c, :], bufB[:, c, :], bufX[:, c, :], ALU.mult))

            dve.wait_ge(conv_in, 12)
            for G in range(2):
                conv(2 * G)
                conv(2 * G + 1)
                if G == 1:
                    dve.sem_inc(tail_ready, 1)
                    dve.sem_inc(a_ready, 1)
                for i, (a, n) in enumerate(span):
                    b = V.take(dve)
                    L.tell(ts(reluS[:, G, a:a + n], b[:, 0:n], 0.0, None, ALU.max), reluS_ready)
                    free()
            for a, n in span:
                b = V.take(dve)
                if a < 1024:
                    L.tell(cp(scS[0:NSM, a:a + n], b[0:NSM, 0:n]))
                else:
                    L.tell(tt(scS[0:NSM, a:a + n], b[0:NSM, 0:n], cv["newbias"][0:NSM, :], ALU.add))
                free()
            L.tell(dve.max(best[0:NSM, :], scS[0:NSM, :]))
            L.tell(dve.match_replace(scS[0:NSM, :], best[0:NSM, :], scS[0:NSM, :], TAKEN))
            seq0 = L.count[id(dve_seq)]
            with dve.Fori(0, TOPK_S // 8 - 1) as i:
                dve.max(best[0:NSM, :], scS[0:NSM, :]).then_inc(dve_seq, 1)
                dve.wait_ge(dve_seq, i * 2 + (seq0 + 1))
                dve.sem_inc(round_begun, 1)
                dve.match_replace(scS[0:NSM, :], best[0:NSM, :], scS[0:NSM, :], TAKEN).then_inc(dve_seq, 1)
                dve.wait_ge(dve_seq, i * 2 + (seq0 + 2))
            L.count[id(dve_seq)] = seq0 + 2 * (TOPK_S // 8 - 1)
            L.tell(ts(mbS[:, :], scS[0:NSM, :], -1e35, NEG, ALU.is_gt, ALU.mult), mbS_ready)
            dve.wait_ge(gates_ready, 1)
            dve.wait_ge(co_ready, DC)
            for i, src in enumerate((bufX, bufC)):
                L.tell(tt(sig[:, 4 * i:4 * i + 4, :], sig[:, 4 * i:4 * i + 4, :], src, ALU.mult))
            bias(16, 48)

            for G in range(2):
                bs = [V.take(dve) for _ in range(3)]
                for i, (a, n) in enumerate(span):
                    L.tell(dve.tensor_reduce(stat[:, 40 + i:41 + i], bs[i][:, 0:n], AX, ALU.max))
                L.tell(dve.tensor_reduce(stat[:, 43:44], stat[:, 40:43], AX, ALU.max))
                L.tell(ts(nmax[:, 0:1], stat[:, 43:44], -QSCALE, None, ALU.mult), nmax_ready)
                dve.wait_ge(probs_ready, 2 * NH + 3 * (G + 1))
                dve.sem_inc(d_free, 3)
                L.tell(dve.tensor_reduce(stat[:, 44:45], rsum[:, 2, 4 * G:4 * G + 3], AX, ALU.add))
                L.tell(dve.reciprocal(rinv[:, 0:1], stat[:, 44:45]))
                b = V.take(dve)
                L.tell(ts(orow[:, 0:P], b[:, 0:P], rinv[:, 0:1], None, ALU.mult), orow_ready)
                free()
                b = V.take(dve)
                for nn in range(NKV):
                    s, e = nn * HD, (nn + 1) * HD
                    src = b[s:e, 0:P].rearrange("p (b h s) -> p b h s", h=NH, s=NS)[:, :, nn * NG:(nn + 1) * NG, :]
                    for gg in range(NG):
                        L.tell(cp(oT[s:e, gg, SEQ + 16 * G:SEQ + 16 * G + 16].rearrange("p (b s) -> p b s", s=NS), src[:, :, gg, :]))
                free()
                dve.sem_inc(oT_ready, 1)

            b = V.take(dve)
            L.tell(cp(tailrows[:, :], b[0:18, :]), tail_row)
            free()
            for j in range(DC):
                b = V.take(dve)
                L.tell(tt(sig[:, 8 + j, :], sig[:, 8 + j, :], b[:, 0:TOK], ALU.mult))
                free()
                L.tell(tt(mixT[:, j, :], sig[:, j, :], sig[:, 8 + j, :], ALU.add))
            dve.sem_inc(mix_ready, 1)
            for j in range(DC):
                b = V.take(dve)
                xs = xT[:, j, SEQ:TOK].rearrange("p (b s) -> p b s", s=NS)
                tmp = rstd[:, 0:NSM].rearrange("p (b s) -> p b s", s=NS)
                L.tell(dve.scalar_tensor_tensor(xT[:, j, 0:SEQ], b[:, 0:SEQ], modT[:, 16 + j, 0:1], xT[:, j, 0:SEQ], ALU.mult, ALU.add),
                       wait=False)
                L.tell(tt(tmp, b[:, SEQ:TOK].rearrange("p (b s) -> p b s", s=NS),
                          modT[:, 16 + j, 1:9].unsqueeze(2).broadcast_to([P, NB, NS]), ALU.mult))
                L.tell(tt(xs, xs, tmp, ALU.add), x1_ready)
                free()
            norm_scale(32, 56)
            norm_unit(2)
            norm_shift(24)
            L.tell(cp(hT[:, :, TOK:3 * P].rearrange("p c (r t) -> p c r t", t=NSM),
                      hT[:, :, SEQ:TOK].unsqueeze(2).broadcast_to([P, DC, 3, NSM])))
            dve.sem_inc(h_ready, 1)
            dve.wait_ge(*v_done[0])
            gs = gspread.rearrange("p (c s t) -> p c s t", s=2, t=P)
            L.tell(cp(gs[:, :, 0, :], modT[:, 40:48, 0:1].broadcast_to([P, DC, P])), wait=False)
            for r in range(4):
                L.tell(cp(gs[:, :, 1, 32 * r:32 * r + 32].rearrange("p c (b s) -> p c b s", s=NS),
                          modT[:, 40:48, 1:9].unsqueeze(3).broadcast_to([P, DC, NB, NS])), wait=(r == 3))
            dve.sem_inc(gspread_ready, 1)

            def route(t):
                cand, onehot = route_work[min(t, 1)][:, 0], route_work[min(t, 1)][:, 1:3]
                wide = [P, 2, PTOP, PTOP]
                for h in range(0, PH, 2):
                    dve.wait_ge(s_ready, 4 * t + h // 2 + 1)
                    if h == PH - 2 and t == 0:
                        L.tell(dve.memset(zeros, 0.0), zeros_ready)
                    for hp in range(2 * h, 2 * h + 4):
                        s, v, ix = ssb[:, hp, :], topv[:, hp, :], topi[:, hp, :]
                        L.tell(dve.max(v[:, 0:8], s))
                        L.tell(dve.max_index(ix[:, 0:8], v[:, 0:8], s))
                        L.tell(dve.match_replace(s, v[:, 0:8], s, TAKEN))
                        L.tell(dve.max(v[:, 8:16], s))
                        L.tell(dve.max_index(ix[:, 8:16], v[:, 8:16], s))
                    if h == PH - 2:
                        dve.sem_inc(s_used, 1)
                    yield
                    L.tell(cp(topf[:, 2 * h:2 * h + 4, :], topi[:, 2 * h:2 * h + 4, :]), wait=False)
                    tv = topv[:, 2 * h:2 * h + 4, :].rearrange("p (h q) k -> p h q k", q=2)
                    tf = topf[:, 2 * h:2 * h + 4, :].rearrange("p (h q) k -> p h q k", q=2)
                    L.tell(tt(cand, tv[:, :, 0, :].unsqueeze(3).broadcast_to(wide), tv[:, :, 1, :].unsqueeze(2).broadcast_to(wide), ALU.add))
                    for e in range(2):
                        cf, v, ix = cand[:, e].rearrange("p i j -> p (i j)"), tops[:, h + e, :], posu[:, h + e, :]
                        L.tell(dve.max(v[:, 0:8], cf))
                        L.tell(dve.max_index(ix[:, 0:8], v[:, 0:8], cf))
                        L.tell(dve.match_replace(cf, v[:, 0:8], cf, TAKEN))
                        L.tell(dve.max(v[:, 8:16], cf))
                        L.tell(dve.max_index(ix[:, 8:16], v[:, 8:16], cf))
                    for q in range(2):
                        pu, pq, pf = (x[:, h:h + 2, :] for x in (posu, posq, posf))
                        L.tell(ts(pq, pu, 15 if q else 4, None, ALU.bitwise_and if q else ALU.logical_shift_right))
                        L.tell(cp(pf, pq))
                        L.tell(tt(onehot[:, q], pf.unsqueeze(3).broadcast_to(wide),
                                  cv["iota"].unsqueeze(1).unsqueeze(1).broadcast_to(wide), ALU.is_equal))
                        L.tell(tt(onehot[:, q], onehot[:, q], tf[:, :, q, :].unsqueeze(2).broadcast_to(wide), ALU.mult))
                        L.tell(dve.tensor_reduce(pick[:, q, h:h + 2, :], onehot[:, q], AX, ALU.add))
                    if h < PH - 2:
                        yield
                L.tell(cp(gsm[:, 0, :], tops[:, :, 0:1].rearrange("p h k -> p (h k)")))
                L.tell(tt(tops[:, :, :], tops[:, :, :], gsm[:, 0, :].unsqueeze(2).broadcast_to([P, PH, PTOP]), ALU.subtract))
                L.tell(dve.scalar_tensor_tensor(pick[:, 0], pick[:, 0], float(PK), pick[:, 1], ALU.mult, ALU.add))
                ef, gf = pick[:, 0].rearrange("p h k -> p (h k)"), tops[:, :, :].rearrange("p h k -> p (h k)")
                if t < 2:
                    L.tell(cp(eidx[:, t, :], ef), wait=False)
                    L.tell(cp(gate[:, t, :], gf))
                else:
                    for q in range(4):
                        s, e = 32 * q, 32 * q + 32
                        L.tell(cp(eidx[s:e, t, 0:32], ef[s:e, s:e]), wait=False)
                        L.tell(cp(gate[s:e, t, 0:32], gf[s:e, s:e]))
                dve.sem_inc(routed, 1)
                yield

            dve.sem_inc(u_used, UR)
            u_round = 0

            def output(t):
                dve.wait_ge(acc_done, t + 1)
                if t:
                    dve.wait_ge(y_out, 16 * t)
                acc = bankD[2 * (t % 2):2 * (t % 2) + 2]
                for half in range(2):
                    s, e = half * 512, (half + 1) * 512
                    if t < 2:
                        L.tell(tt(yout[:, s:e], acc[half][:, :], g2tok[:, 0, s:e], ALU.mult))
                    else:
                        L.tell(cp(yout[:, s:e], acc[half][:, :]))
                dve.sem_inc(acc_taken, 1)
                if t < 2:
                    L.tell(tt(yout, yout, x1tok[:, t, :], ALU.add))
                dve.sem_inc(y_ready, 1)

            for _ in route(0):
                pass
            for c, (t, first) in enumerate(CHUNKS):
                if first == 0:
                    router = route(t + 1) if t < 2 else iter(())
                for half in range(2):
                    with dve.Fori(0, CHUNK // UR // 2) as i:
                        for r in range(UR):
                            dve.wait_ge(u_in[r], (i + (u_round + 1)) * 16)
                            dve.tensor_tensor_reduce(out=urows[r], in0=urows[r], in1=h2tok[:, t, :], scale=1.0, scalar=0.0,
                                                     op0=ALU.mult, op1=ALU.add, accum_out=dcur[:, r:r + 1]).then_inc(u_used, 1)
                        dve.wait_ge(u_used, (i + (u_round + 2)) * UR)
                        dve.tensor_copy(dots[:, t, bass.ds(i * UR + (first + half * CHUNK // 2), UR)], dcur[:, :])\
                            .then_inc(dcur_copied, 1)
                        dve.wait_ge(dcur_copied, i + (u_round + 1))
                    u_round += CHUNK // UR // 2
                    if half == 1:
                        dve.sem_inc(dots_ready, 1)
                    next(router, None)
                    if first == SLOTS[0] - CHUNK and half == 0:
                        next(router, None)
                if first == 0:
                    dve.wait_ge(exp_done, t + 1)
                    n = SLOTS[t]
                    nh = n // PTOP
                    gv = gate[:, t, 0:n].rearrange("p (h k) -> p h k", k=PTOP)
                    L.tell(dve.tensor_reduce(gsm[:, 1, 0:nh], gv, AX, ALU.add))
                    L.tell(dve.reciprocal(gsm[:, 1, 0:nh], gsm[:, 1, 0:nh]))
                    L.tell(tt(gv, gv, gsm[:, 1, 0:nh].unsqueeze(2).broadcast_to([P, nh, PTOP]), ALU.mult))
                dve.wait_ge(gelu_done, c + 1)
                e = first + CHUNK
                L.tell(tt(dots[:, t, first:e], dots[:, t, first:e], gate[:, t, first:e], ALU.mult), w_ready)
                if c == len(CHUNKS) - 3:
                    output(0)
            output(1)
            output(2)
            dve.wait_ge(acc_done, 4)
            for half in range(2):
                s, e = half * 512, (half + 1) * 512
                L.tell(tt(yout[0:NSM, s:e], bankD[2 + half][0:NSM, :], g2tok[0:NSM, 1, s:e], ALU.mult))
                L.tell(tt(yout[0:NSM, s:e], yout[0:NSM, s:e], x1tok[0:NSM, 2, s:e], ALU.add))
            dve.sem_inc(y_ready, 1)


def kernel(**inputs):
    import concourse.bacc as bacc
    from concourse.bass_utils import run_bass_kernel_spmd

    nc = bacc.Bacc("TRN2", target_bir_lowering=False, num_devices=1)
    arrays = {name: np.ascontiguousarray(inputs[name]) for name in INPUTS}
    arrays["consts"] = const_table()
    ap = {}
    for name, a in arrays.items():
        t = nc.dram_tensor(name, a.shape, mybir.dt.from_np(a.dtype), kind="ExternalInput").ap()
        if name in LAYERED or name in ("x_prompt",):
            t = t[0]
        if name in ("cache_k", "cache_v"):
            t = t.rearrange("g p n d -> (g p) (n d)")
        if name == "cache_kidx":
            t = t.rearrange("g p d -> (g p) d")
        if name == "x_sample":
            t = t.rearrange("b s d -> (b s) d")
        ap[name] = t
    outs = {}
    for name, shape, view in OUTPUTS:
        t = nc.dram_tensor("out_" + name, shape, F32, kind="ExternalOutput").ap()
        outs[name] = t.rearrange(view[0]) if view[0] else t
        if view[1]:
            outs[name] = outs[name][0]
    layer_program(nc, **ap, **outs)
    r = run_bass_kernel_spmd(nc, [arrays], core_ids=[0])
    return tuple(r.results[0]["out_" + name] for name, _, _ in OUTPUTS)
```

```python
from contextlib import ExitStack

import numpy as np

import concourse.bass as bass
from concourse import mybir

F32 = mybir.dt.float32
BF16 = mybir.dt.bfloat16
I32 = mybir.dt.int32
U32 = mybir.dt.uint32
ALU = mybir.AluOpType
ACT = mybir.ActivationFunctionType
AX = mybir.AxisListType.X

P = 128
D = 1024
DC = D // P
SEQ = 256
NB, NS = 8, 4
NSM = NB * NS
TOK = SEQ + NSM
PAST, PAGE = 1024, 128
NPG = PAST // PAGE
NPHYS = 80
CONV = 512
CC = CONV // P
NH, NKV, HD = 8, 2, 64
NG = NH // NKV
TOPK_P, TOPK_S = SEQ // 4, 256
IDX_SCALE = (64 ** -0.5) * (8 ** -0.5)
QSCALE = HD ** -0.5
EPS = 1e-6
NEG = -1e30
TAKEN = -3e38
NKEY = PAST + NSM
PH, PK, PTOP = 8, 128, 16
ROWS = [P, P, NSM]
COLS = [0, P, SEQ]
SLOTS = [PH * PTOP, PH * PTOP, PH * PTOP // 4]

C_XIN, C_ATT, C_Q, C_K, C_V, C_QI, C_KI, C_WI, C_GA = 0, 1536, 1536, 2048, 2176, 2304, 2816, 2880, 2888
ZW = C_GA - C_ATT
Z_K, Z_V, Z_QI, Z_KI, Z_WI = C_K - C_ATT, C_V - C_ATT, C_QI - C_ATT, C_KI - C_ATT, C_WI - C_ATT

CONST_PARTS = [("ident", P), ("cos", 3 * 32), ("sin", 3 * 32), ("causal0", P), ("causal1", 2 * P), ("newbias", NSM),
               ("rep", 2 * P), ("repT", 2 * NSM), ("headsel", NH), ("sum4", NSM), ("iota", PTOP)]


def const_table():
    t = {n: np.zeros((P, w), np.float32) for n, w in CONST_PARTS}
    t["ident"][:] = np.eye(P, dtype=np.float32)
    freq = (np.float32(10000.0) ** (-np.arange(32, dtype=np.float32) / np.float32(32))).astype(np.float32)
    row = np.arange(P)
    for tile, pos in enumerate([row, row + P, PAST + row % NS]):
        ang = pos.astype(np.float32)[:, None] * freq[None, :]
        t["cos"][:, 32 * tile:32 * tile + 32] = np.cos(ang)
        t["sin"][:, 32 * tile:32 * tile + 32] = np.sin(ang)
    key = np.arange(2 * P)
    t["causal0"][:] = np.where(key[None, :P] <= row[:, None], 0.0, NEG)
    t["causal1"][:] = np.where(key[None, :] <= row[:, None] + P, 0.0, NEG)
    tok = np.arange(NSM)
    t["newbias"][:NSM] = np.where((tok[None, :] // NS == tok[:, None] // NS) & (tok[None, :] <= tok[:, None]), 0.0, NEG)
    for g in range(2):
        src = (4 * g + row // 32) * NS + row % NS
        t["rep"][src, P * g + row] = 1.0
        t["repT"][row, NSM * g + src] = 1.0
    t["headsel"][row, (row // NS) % NH] = 1.0
    t["sum4"][row, row % NSM] = 1.0
    t["iota"][:] = np.arange(PTOP)[None, :]
    return np.concatenate([t[n] for n, _ in CONST_PARTS], axis=1)


INPUTS = ["x_prompt", "x_sample", "cache_k", "cache_v", "cache_kidx", "state_conv", "page_table", "c_prompt", "c_sample",
          "w_ada", "b_ada", "norm1_w", "w_in", "conv_w", "q_norm_w", "k_norm_w", "w_conv_out", "w_attn_out", "w_out",
          "norm2_w", "peer_w_q", "peer_sub_keys", "peer_u", "peer_v"]
LAYERED = set(INPUTS) - {"x_prompt", "x_sample", "page_table", "c_prompt", "c_sample"}
OUTPUTS = [("y_prompt", (1, SEQ, D), ("a t d -> (a t) d", False)), ("y_sample", (NB, NS, D), ("b s d -> (b s) d", False)),
           ("k_prompt", (1, 1, SEQ, NKV, HD), ("l b t n d -> (l b t) (n d)", False)),
           ("v_prompt", (1, 1, SEQ, NKV, HD), ("l b t n d -> (l b t) (n d)", False)),
           ("kidx_prompt", (1, 1, SEQ, HD), ("l b t d -> (l b t) d", False)),
           ("conv_prompt", (1, 1, 2, CONV), ("l b t d -> (l b t) d", False)),
           ("k_sample", (1, NB, NS, NKV, HD), ("l b t n d -> (l b t) (n d)", False)),
           ("v_sample", (1, NB, NS, NKV, HD), ("l b t n d -> (l b t) (n d)", False)),
           ("kidx_sample", (1, NB, NS, HD), ("l b t d -> (l b t) d", False)),
           ("conv_sample", (1, NB, 2, CONV), (None, True))]


class Lane:

    def __init__(self, eng, own):
        self.eng, self.own, self.count = eng, own, {}

    def done_but(self, n):
        self.eng.wait_ge(self.own, self.count[id(self.own)] - n)

    def tell(self, ins, sem=None, wait=True):
        sem = self.own if sem is None else sem
        self.count[id(sem)] = self.count.get(id(sem), 0) + 1
        ins.then_inc(sem, 1)
        if wait:
            self.eng.wait_ge(sem, self.count[id(sem)])


class Banks:

    def __init__(self, banks, full, free):
        self.banks, self.full, self.free, self.n = banks, full, free, 0

    def open(self, pe):
        if self.n >= len(self.banks):
            pe.wait_ge(self.free, self.n - len(self.banks) + 1)
        self.n += 1
        return self.banks[(self.n - 1) % len(self.banks)]

    def close(self, mm, n=1):
        mm.then_inc(self.full, n)

    def take(self, eng):
        eng.wait_ge(self.full, self.n + 1)
        self.n += 1
        return self.banks[(self.n - 1) % len(self.banks)]


def layer_program(nc, x_prompt, x_sample, cache_k, cache_v, cache_kidx, state_conv, page_table, c_prompt, c_sample,
                  w_ada, b_ada, norm1_w, w_in, conv_w, q_norm_w, k_norm_w, w_conv_out, w_attn_out, w_out, norm2_w,
                  peer_w_q, peer_sub_keys, peer_u, peer_v, consts,
                  y_prompt, y_sample, k_prompt, v_prompt, kidx_prompt, conv_prompt, k_sample, v_sample, kidx_sample,
                  conv_sample):
    with ExitStack() as ctx:
        def sb(name, shape, dt=F32):
            return ctx.enter_context(nc.sbuf_tensor(name, shape, dt))

        def sem(name):
            return ctx.enter_context(nc.semaphore(name))

        WSLOT = DC * 512
        NW = 2
        UR = 8
        ctab = sb("ctab", [P, sum(w for _, w in CONST_PARTS)])
        cv, at = {}, 0
        for n, w in CONST_PARTS:
            cv[n] = ctab[:, at:at + w]
            at += w
        ident = cv["ident"]
        ident_bf = sb("ident_bf", [P, P], BF16)
        rep_bf = sb("rep_bf", [NSM, 2 * P], BF16)
        ones = sb("ones", [P, P])
        smallT = sb("smallT", [P, 76])
        qkw = sb("qkw", [P, P])
        cT = sb("cT", [P, DC, 32])
        modT = sb("modT", [P, 48, 9])
        ab = sb("ab", [P, DC, 9])
        xT = sb("xT", [P, DC, TOK])
        hT = sb("hT", [P, DC, 3 * P])
        oT = sb("oT", [P, NG, TOK])
        rstd = sb("rstd", [P, TOK])
        stateT = sb("stateT", [P, CC, NB * 2])
        pages = sb("pages", [1, NB * NPG], I32)

        big = sb("big", [P, NB * NPG * P + 2 * NPG * P + 2 * NPG * 64 + NW * WSLOT])
        o = NB * NPG * P
        vpages = big[:, 0:o].rearrange("p (g d) -> p g d", d=P)
        NI, NK = 6, 3
        ipages = big[:, o:o + NI * NPG * 64].rearrange("p (r g d) -> p r g d", r=NI, d=64)
        kpages = big[:, o:o + NK * NPG * P].rearrange("p (r g d) -> p r g d", r=NK, d=P)
        o += NK * NPG * P
        wring = [big[:, o + i * WSLOT:o + (i + 1) * WSLOT] for i in range(NW)]
        wring += [wring[0][:, 0:WSLOT // 2], wring[0][:, WSLOT // 2:WSLOT]]
        urows = [big[:, i * D:(i + 1) * D] for i in range(UR)]
        vrows = [big[:, (UR + i) * D:(UR + i + 1) * D] for i in range(UR)]
        assert 2 * UR * D + PH * 256 <= o + NW * WSLOT
        spare = NB * NPG * P
        gspread = big[:, spare:spare + 16 * P]
        def route_work(early):
            o1 = spare + 16 * P if early else 2 * UR * D + 512
            onehot = big[:, o1:o1 + 1024].rearrange("p (q h i j) -> p q h i j", q=2, h=2, i=PTOP)
            cand = yout[:, 0:512] if early else big[:, 2 * UR * D:2 * UR * D + 512]
            return cand.rearrange("p (h i j) -> p h i j", h=2, i=PTOP), onehot


        zall = sb("zall", [P, 32 * P])
        zbuf = zall[:, 0:3 * ZW].rearrange("p (t z) -> p t z", z=ZW)
        subraw = zall[:, 0:16 * P].rearrange("p (j d) -> p j d", d=P)
        subT = zall[:, 16 * P:32 * P].rearrange("p (j k) -> p j k", k=P)

        r5 = sb("r5", [P, 16 * TOK + 12 * TOK + CC * (SEQ + 2) + CC * NB * 6])
        sig = r5[:, 0:16 * TOK].rearrange("p (j t) -> p j t", t=TOK)
        o = 16 * TOK
        bufX = r5[:, o:o + 4 * TOK].rearrange("p (j t) -> p j t", t=TOK)
        bufB = r5[:, o + 4 * TOK:o + 8 * TOK].rearrange("p (j t) -> p j t", t=TOK)
        bufC = r5[:, o + 8 * TOK:o + 12 * TOK].rearrange("p (j t) -> p j t", t=TOK)
        mixT = r5[:, o + 8 * TOK:o + 16 * TOK].rearrange("p (j t) -> p j t", t=TOK)
        o += 12 * TOK
        uP = r5[:, o:o + CC * (SEQ + 2)].rearrange("p (j t) -> p j t", t=SEQ + 2)
        o += CC * (SEQ + 2)
        uS = r5[:, o:o + CC * NB * 6].rearrange("p (j b t) -> p j b t", b=NB, t=6)
        kpages_last = r5[:, 16 * TOK + 12 * TOK:16 * TOK + 12 * TOK + NPG * P].rearrange("p (g d) -> p g d", d=P)
        ipages_last = r5[:, 8 * TOK:8 * TOK + 2 * NPG * 64].rearrange("p (r g d) -> p r g d", r=2, d=64)
        aT = bufB
        qpT = r5[:, 0:16 * 3 * P].rearrange("p (j t) -> p j t", t=3 * P)
        ssb = r5[:, 48 * P:64 * P].rearrange("p (j k) -> p j k", k=P)
        dots = r5[:, 64 * P:67 * P].rearrange("p (t s) -> p t s", t=3)
        eidx = r5[:, 67 * P:70 * P].bitcast(I32).rearrange("p (t s) -> p t s", t=3)
        tails = sb("tails", [P, CC, 2 + NB * 2])

        R6 = 9 * D
        r6 = sb("r6", [P, R6])
        cut = [0]

        def part(n, start=None):
            if start is not None:
                cut[0] = start
            v = r6[:, cut[0]:cut[0] + n]
            cut[0] += n
            assert cut[0] <= R6, cut[0]
            return v
        xin = part(3 * D, 0).rearrange("p (t d) -> p t d", d=D)
        crow = part(D)
        srow = part(CONV)
        sq = part(DC * TOK)
        smallrows = part(P)[0:76]
        qkrow = part(P)
        qTz = part(NH * P, 0).rearrange("p (h t) -> p h t", t=P)
        qiTz = part(NH * P).rearrange("p (h t) -> p h t", t=P)
        probs = part(NH * 2 * P)
        probsT = part(NH * 2 * P)
        relu = part(2 * 2 * P)
        rope = [part(10 * 32) for _ in range(2)]
        scP = part(2 * P)
        workP = part(2 * P)
        orow = part(4 * P)
        kidup = part(P)
        mbP = part(P).bitcast(BF16)
        adarow = part(512)
        reluS = part(2 * NKEY, 0).rearrange("p (g k) -> p g k", k=NKEY)
        probsS = part(NKEY, 0)
        KB = 4
        kbT = part(KB * PAST).rearrange("p (r k) -> p r k", k=PAST)
        scS = part(NKEY)
        mbS = part(NKEY // 2).bitcast(BF16)[0:NSM]
        ibT = part(2 * 4 * P, cut[0]).rearrange("p (r k) -> p r k", k=4 * P)
        probsST = part(NPG * P + P, cut[0] - 8 * P)
        tailrows = part(CONV, 0)[0:2 + NB * 2]
        x1tok = part(3 * D, 0).rearrange("p (t d) -> p t d", d=D)
        h2tok = part(3 * D).rearrange("p (t d) -> p t d", d=D)
        g2tok = part(2 * D).rearrange("p (t d) -> p t d", d=D)
        yout = part(D)
        kT = sb("kT", [P, TOK])
        kiT = sb("kiT", [P, TOK])
        wis = sb("wis", [P, 3, NH])
        stat = sb("stat", [P, 64])
        best = sb("best", [P, 8])
        nmax = sb("nmax", [P, NH])
        rsum = sb("rsum", [P, 3, NH])
        rinv = sb("rinv", [P, NH])
        QIs = sb("QIs", [P, 2, NB * 32])
        Qs = sb("Qs", [P, NB * 32])
        wrow = sb("wrow", [P, 2])
        wsel = sb("wsel", [P, 2, NSM])
        cuts = [0]

        def small(n):
            cuts[0] += n
            return zall[:, cuts[0] - n:cuts[0]]
        topv = small(16 * PTOP).rearrange("p (j k) -> p j k", k=PTOP)
        topi = small(16 * PTOP).bitcast(U32).rearrange("p (j k) -> p j k", k=PTOP)
        topf = small(16 * PTOP).rearrange("p (j k) -> p j k", k=PTOP)
        tops = small(P).rearrange("p (h k) -> p h k", k=PTOP)
        posu = small(P).bitcast(U32).rearrange("p (h k) -> p h k", k=PTOP)
        posq = small(2 * 2 * PTOP).bitcast(U32).rearrange("p (q h k) -> p q h k", q=2, k=PTOP)
        posf = small(2 * P).rearrange("p (q h k) -> p q h k", q=2, k=PTOP)
        pick = small(2 * P).rearrange("p (q h k) -> p q h k", q=2, k=PTOP)
        gate = small(3 * P).rearrange("p (t s) -> p t s", t=3)
        gsm = sb("gsm", [P, 2, PH])
        dcur = sb("dcur", [P, UR])
        ucur = sb("ucur", [P, 2, UR], I32)
        vcur = sb("vcur", [P, 2, UR], I32)
        NDG = 4
        o = 2 * UR * D + PH * 256
        diag = big[:, o:o + NDG * P].rearrange("p (n k) -> p n k", k=P)
        zeros = big[:, o + NDG * P:o + NDG * P + 512]

        bankA = [ctx.enter_context(nc.psum_tensor(f"bankA{i}", [P, 512], F32)) for i in range(4)]
        bankD = [ctx.enter_context(nc.psum_tensor(f"bankD{i}", [P, 512], F32)) for i in range(4)]

        span = ((0, 512), (512, 512), (1024, NSM))

        in_small, in_x, in_pages, in_const = sem("in_small"), sem("in_x"), sem("in_pages"), sem("in_const")
        w_landed = [sem(f"w_landed{i}") for i in range(NW + 2)]
        kv_out, y_out, conv_out_done = sem("kv_out"), sem("y_out"), sem("conv_out_done")
        gelu_done, row_asked, round_begun = sem("gelu_done"), sem("row_asked"), sem("round_begun")
        sub_landed, exp_done = sem("sub_landed"), sem("exp_done")
        h2_ready = sem("h2_ready")
        v_landed = sem("v_landed")
        k_landed = [sem(f"k_landed{i}") for i in range(NK + 1)]
        i_landed = [sem(f"i_landed{i}") for i in range(NB)]
        adarow_ready, mod_ready, qk_ready, co_ready = (
            sem("adarow_ready"), sem("mod_ready"), sem("qk_ready"), sem("co_ready"))
        a_full, a_free, d_full, d_free = sem("a_full"), sem("a_free"), sem("d_full"), sem("d_free")
        act_seq, dve_seq = sem("act_seq"), sem("dve_seq")
        consts_ready = sem("consts_ready")
        xT_ready, cT_ready, sq_ready, var_ready, sd_ready, h_ready = (
            sem("xT_ready"), sem("cT_ready"), sem("sq_ready"), sem("var_ready"), sem("sd_ready"), sem("h_ready"))
        z_ready, qk_var, qk_sd, rope_done = sem("z_ready"), sem("qk_var"), sem("qk_sd"), sem("rope_done")
        qT_ready, mb_ready = sem("qT_ready"), sem("mb_ready")
        nmax_ready, probs_ready, probsT_ready, orow_ready = (
            sem("nmax_ready"), sem("probs_ready"), sem("probsT_ready"), sem("orow_ready"))
        relu_ready, relu_used = sem("relu_ready"), sem("relu_used")
        gspread_ready = sem("gspread_ready")
        wsel_ready, ib_ready, ib_used, kb_ready, kb_used, reluS_ready = (
            sem("wsel_ready"), sem("ib_ready"), sem("ib_used"), sem("kb_ready"), sem("kb_used"), sem("reluS_ready"))
        mbS_ready, oT_ready, gates_ready, conv_in, a_ready, tail_ready, tail_row = (
            sem("mbS_ready"), sem("oT_ready"), sem("gates_ready"), sem("conv_in"), sem("a_ready"), sem("tail_ready"),
            sem("tail_row"))
        mix_ready, x1_ready, rows_ready, subT_ready, qp_ready, s_ready, s_used = (
            sem("mix_ready"), sem("x1_ready"), sem("rows_ready"), sem("subT_ready"), sem("qp_ready"), sem("s_ready"),
            sem("s_used"))
        routed, zeros_ready = sem("routed"), sem("zeros_ready")
        u_in = [sem(f"u_in{i}") for i in range(UR)]
        v_in = [sem(f"v_in{i}") for i in range(UR)]
        u_used, v_used, dots_ready, w_ready, diag_ready, acc_done, acc_taken, y_ready = (
            sem("u_used"), sem("v_used"), sem("dots_ready"), sem("w_ready"), sem("diag_ready"),
            sem("acc_done"), sem("acc_taken"), sem("y_ready"))
        dcur_copied, ucur_done, vcur_done = sem("dcur_copied"), sem("ucur_done"), sem("vcur_done")

        def cols(w, a, n):
            k = w.shape[0] // P
            return [(w[:, a:a + n].rearrange("(k p) n -> p k n", p=P), k, n)]

        attn_rows = w_attn_out.rearrange("(n g d) m -> n g d m", n=NKV, g=NG)
        groups = ([("ada", cols(w_ada, 512 * i, 512)) for i in range(4)]
                  + [("q", cols(w_in, C_Q, 512)), ("kvw", cols(w_in, C_K, 256) + cols(w_in, C_KI, 72)),
                     ("qi", cols(w_in, C_QI, 512))]
                  + [("conv", cols(w_in, 512 * i, 512)) for i in range(3)]
                  + [x for i in range(8) for x in (("gate", cols(w_in, C_GA + 256 * i, 256)),
                                                   ("ada", cols(w_ada, 512 * (i + 4), 512)))]
                  + [("convout", cols(w_conv_out, 0, D))]
                  + [("attnout", [(None, 4, D)] * 2)]
                  + [("out", cols(w_out, 512 * i, 512)) for i in range(2)]
                  + [("peerq", cols(peer_w_q, 512 * i, 512)) for i in range(4)])
        names = [n for n, _ in groups]
        slot_of = [{"gate": 2 + (g - names.index("gate")) // 2 % 2, "ada": 1}[n]
                   if names.index("gate") <= g < names.index("convout") else g % 2 for g, n in enumerate(names)]
        shares = {0: (0, 2, 3), 1: (1,), 2: (0, 2), 3: (0, 3)}
        assert slot_of[names.index("gate") - 1] == 1 and slot_of[names.index("convout")] == 0

        def weights(eng, g):
            eng.wait_ge(w_landed[slot_of[g]], 16 * sum(len(groups[j][1]) for j in range(g + 1) if slot_of[j] == slot_of[g]))
            k, n = groups[g][1][0][1], sum(part[2] for part in groups[g][1])
            n = D if names[g] == "attnout" else n
            return wring[slot_of[g]][:, 0:k * n].rearrange("p (k n) -> p k n", n=n)

        block = ctx.enter_context(nc.Block())

        released = {}
        turned_i, turned_k = {}, {}
        v_done = {}
        FILL = {"start": 1, "T2": 2, "select": (2, 2), "softmax": (2, 3), "next": (1, 0)}
        CHUNK = 32
        CHUNKS = [(t, first) for t in range(3) for first in range(0, SLOTS[t], CHUNK)]
        CONV_FILL = (1, 2, 2)
        H2_BEFORE = 4
        SCORE_AFTER = [4, 8, 12]

        def index_slot(b):
            return ipages[:, b] if b < NI else ipages_last[:, b - NI]

        def key_slot(b):
            if b == NB - 1:
                return kpages_last, k_landed[NK], 16 * NPG
            r = (b + 1) % NK
            return kpages[:, r], k_landed[r], 16 * NPG * (b // NK + 1)

        logit_bank = {}

        @block.tensor
        def _(pe):
            A, V = Banks(bankA, a_full, a_free), Banks(bankD, d_full, d_free)
            pe.wait_ge(in_const, 16)
            pe.wait_ge(consts_ready, 4)
            pe.wait_ge(in_small, 16 * 9)
            b = V.open(pe)
            V.close(pe.transpose(b[:, 0:76], smallrows[:, :], ident[0:76, 0:76]))
            b = V.open(pe)
            for c in range(DC):
                mm = pe.transpose(b[:, 9 * c:9 * c + 9], crow[0:9, c * P:(c + 1) * P], ident[0:9, 0:9])
            V.close(mm)
            b = V.open(pe)
            for c in range(CC):
                mm = pe.transpose(b[:, 16 * c:16 * c + 16], srow[0:16, c * P:(c + 1) * P], ident[0:16, 0:16])
            V.close(mm)
            b = V.open(pe)
            V.close(pe.matmul(b[:, 0:P], ones[0:1, :], qkrow[0:1, :], start=True, stop=True))
            pe.wait_ge(in_x, 48)
            for c in range(DC):
                b = V.open(pe)
                for t in range(3):
                    mm = pe.transpose(b[:, COLS[t]:COLS[t] + ROWS[t]], xin[0:ROWS[t], t, c * P:(c + 1) * P],
                                      ident[0:ROWS[t], 0:ROWS[t]])
                V.close(mm)

            g = 0
            ada_done = [0]

            def ada(g):
                w = weights(pe, g)
                b = A.open(pe)
                for k in range(DC):
                    q = k % 4
                    mm = pe.matmul(b[32 * q:32 * q + 32, :], cT[:, k, :], w[:, k, :], start=(k < 4), stop=(k >= 4),
                                   skip_group_check=True)
                A.close(mm)
                released[g] = (a_full, A.n)
                ada_done[0] += 1
                pe.wait_ge(adarow_ready, ada_done[0])
                b = A.open(pe)
                for j in range(4):
                    mm = pe.matmul(b[:, 9 * j:9 * j + 9], adarow[:, j * P:(j + 1) * P], cv["sum4"][:, 0:9], start=True, stop=True)
                A.close(mm)

            def norm_sum(n):
                b = V.open(pe)
                for c in range(DC):
                    pe.wait_ge(sq_ready, n[c])
                    mm = pe.matmul(b[:, 0:TOK], ones[:, :], sq[:, c * TOK:(c + 1) * TOK], start=(c == 0), stop=(c == DC - 1))
                V.close(mm)

            norm_sum([1] * DC)
            pe.wait_ge(cT_ready, 1)
            for _ in range(4):
                ada(g)
                g += 1

            for name in ("q", "kvw", "qi"):
                w = weights(pe, g)
                width = w.shape[2]
                b = A.open(pe)
                for k in range(DC):
                    q = k % 4
                    pe.wait_ge(h_ready, k + 1)
                    mm = pe.matmul(b[32 * q:32 * q + 32, 0:width], hT[:, k, SEQ:TOK], w[:, k, :], start=(k < 4), stop=(k >= 4),
                                   skip_group_check=True)
                A.close(mm)
                for t in range(2):
                    b = A.open(pe)
                    for k in range(DC):
                        mm = pe.matmul(b[:, 0:width], hT[:, k, COLS[t]:COLS[t] + P], w[:, k, :], start=(k == 0), stop=(k == DC - 1))
                    A.close(mm)
                released[g] = (a_full, A.n)
                g += 1
                ada_done[0] += 1
                pe.wait_ge(adarow_ready, ada_done[0])
                b = A.open(pe)
                A.close(pe.matmul(b[0:NSM, 0:width], cv["sum4"], adarow[:, 0:width], start=True, stop=True))

            blocks = iter([(gg, j) for gg, name in enumerate(names) if name in ("conv", "gate")
                           for j in range(groups[gg][1][0][2] // P)])

            def fill(n):
                for _ in range(n):
                    gg, j = next(blocks, (None, None))
                    if gg is None:
                        return
                    if j == 0:
                        slot[0] = weights(pe, gg)
                    w, b = slot[0], A.open(pe)
                    for k in range(DC):
                        mm = pe.matmul(b[:, 0:TOK], w[:, k, j * P:(j + 1) * P], hT[:, k, 0:TOK], start=(k == 0), stop=(k == DC - 1))
                    A.close(mm)
                    released[gg] = (a_full, A.n)

            slot = [None]
            def turn_tile(t, n):
                r, z = ROWS[t], zbuf[0:ROWS[t], t, :]
                idt = ident[0:r, 0:r]
                pe.wait_ge(rope_done, n)
                b = V.open(pe)
                for gg in range(NG):
                    mm = pe.transpose(b[:, gg * r:gg * r + r], orow[0:r, gg * P:(gg + 1) * P], idt)
                V.close(mm)
                b = V.open(pe)
                for c in range(4):
                    mm = pe.transpose(b[:, c * r:c * r + r], z[:, Z_QI + c * P:Z_QI + (c + 1) * P], idt)
                V.close(mm)
                b = V.open(pe)
                pe.transpose(b[:, 0:r], z[:, Z_K:Z_K + P], idt)
                V.close(pe.transpose(b[:, P:P + r], kidup[0:r, :], idt))

            fill(FILL["start"])
            turn_tile(2, 1)
            b = V.open(pe)
            for gg in range(2):
                mm = pe.matmul(b[:, NH * gg:NH * gg + NH], cv["rep"][0:NSM, gg * P:(gg + 1) * P], wis[0:NSM, 2, :],
                               start=True, stop=True)
            V.close(mm)

            fill(FILL["T2"])
            for t in range(2):
                W = P * (t + 1)
                turn_tile(t, 2 + t)
                pe.wait_ge(qT_ready, t + 2)
                for hp in range(NH // 2):
                    b = A.open(pe)
                    for j in range(2):
                        mm = pe.matmul(b[:, j * W:(j + 1) * W], qiTz[:, 2 * hp + j, :], kiT[:, 0:W], start=True, stop=True)
                    A.close(mm)
                fill(FILL["select"][t])
                pe.wait_ge(mb_ready, t + 1)
                for hp in range(NH // 2):
                    b = V.open(pe)
                    logit_bank[t, hp] = b
                    for j in range(2):
                        pe.matmul(b[:, j * W:(j + 1) * W], qTz[:, 2 * hp + j, :], kT[:, 0:W], start=True, stop=False)
                        mm = pe.matmul(b[:, j * W:(j + 1) * W], ident_bf[:, :], mbP[:, 0:W], start=False, stop=True)
                    V.close(mm)
                fill(FILL["softmax"][t])
                pe.wait_ge(probs_ready, NH * (t + 1))
                per = t + 1
                for q in range(NH * per // 4):
                    b = A.open(pe)
                    for j in range(4):
                        mm = pe.transpose(b[:, j * P:(j + 1) * P], probs[:, (4 * q + j) * P:(4 * q + j + 1) * P], ident)
                    A.close(mm)
                pe.wait_ge(probsT_ready, 2 if t == 0 else 6)
                b = V.open(pe)
                for h in range(NH):
                    for c in range(per):
                        kv = zbuf[:, c, Z_V + (h // NG) * HD:Z_V + (h // NG + 1) * HD]
                        mm = pe.matmul(b[:, h * HD:(h + 1) * HD], probsT[:, (h * per + c) * P:(h * per + c + 1) * P], kv,
                                       start=(c == 0), stop=(c == per - 1))
                V.close(mm)
                pe.wait_ge(orow_ready, t + 1)
                b = V.open(pe)
                for gg in range(NG):
                    mm = pe.transpose(b[:, gg * P:(gg + 1) * P], orow[:, gg * P:(gg + 1) * P], ident)
                V.close(mm)
                fill(FILL["next"][t])
            pe.wait_ge(oT_ready, 2)
            def turn_i(bb):
                pe.wait_ge(i_landed[bb], 16 * NPG)
                b = A.open(pe)
                for q in range(4):
                    mm = pe.transpose(b[:, q * P:(q + 1) * P],
                                      index_slot(bb)[:, 2 * q:2 * q + 2, :].rearrange("p g d -> p (g d)"), ident)
                A.close(mm)
                turned_i[bb] = A.n

            turn_i(0)
            for G in range(2):
                sbank = [V.open(pe) for _ in range(3)]
                for bb in range(4 * G, 4 * G + 4):
                    b4 = bb % 4
                    if bb + 1 < NB:
                        turn_i(bb + 1)
                    pe.wait_ge(ib_ready, bb + 1)
                    for pg in range(NPG):
                        mm = pe.matmul(sbank[pg // 4][32 * b4:32 * b4 + 32, (pg % 4) * P:(pg % 4 + 1) * P],
                                       QIs[:, pg % 2, bb * 32:(bb + 1) * 32], ibT[:, bb % 2, (pg // 2) * P:(pg // 2 + 1) * P],
                                       start=True, stop=True)
                    mm.then_inc(ib_used, 1)
                mm = pe.matmul(sbank[2][:, 0:NSM], QIs[:, 0, G * P:(G + 1) * P], kiT[:, SEQ:TOK], start=True, stop=True)
                V.close(mm, 3)
            pe.wait_ge(reluS_ready, 6)
            pe.wait_ge(wsel_ready, 1)
            for a, n in span:
                b = V.open(pe)
                for G in range(2):
                    mm = pe.matmul(b[0:NSM, 0:n], wsel[:, G, :], reluS[:, G, a:a + n], start=(G == 0), stop=(G == 1))
                V.close(mm)

            def turn_k(bb):
                pages_k, landed, n = key_slot(bb)
                pe.wait_ge(landed, n)
                for half in range(2):
                    b = A.open(pe)
                    for q in range(4):
                        mm = pe.transpose(b[:, q * P:(q + 1) * P], pages_k[:, 4 * half + q, :], ident)
                    A.close(mm)
                turned_k[bb] = A.n

            rest = [gg for gg, name in enumerate(names) if name == "ada"][4:]
            for bb in range(4):
                turn_k(bb)
                fill(2 if bb else 1)
                ada(rest[2 * bb])
                fill(2)
                ada(rest[2 * bb + 1])

            g = names.index("convout")
            conv_blocks = iter(range(DC))

            def conv_out(n):
                for j in [next(conv_blocks) for _ in range(n)]:
                    if j == 0:
                        pe.wait_ge(a_ready, 1)
                        slot[0] = weights(pe, g)
                    b = A.open(pe)
                    for k in range(4):
                        mm = pe.matmul(b[:, 0:TOK], slot[0][:, k, j * P:(j + 1) * P], aT[:, k, 0:TOK], start=(k == 0), stop=(k == 3))
                    A.close(mm)
                released[g] = (a_full, A.n)

            conv_out(CONV_FILL[0])
            pe.wait_ge(mbS_ready, 1)
            for G in range(2):
                sbank = [V.open(pe) for _ in range(3)]
                logit_bank[2, G] = sbank
                for i, (a, n) in enumerate(span):
                    pe.matmul(sbank[i][:, 0:n], rep_bf[:, G * P:(G + 1) * P], mbS[:, a:a + n], start=True, stop=False,
                              skip_group_check=True)
                for b4 in range(4):
                    bb = 4 * G + b4
                    pe.wait_ge(kb_ready, 2 * bb + 2)
                    for half in range(2):
                        mm = pe.matmul(sbank[half][32 * b4:32 * b4 + 32, :], Qs[:, bb * 32:(bb + 1) * 32],
                                       kbT[:, bb % KB, half * 512:(half + 1) * 512], start=False, stop=(b4 == 3),
                                       skip_group_check=True)
                    mm.then_inc(kb_used, 1)
                mm = pe.matmul(sbank[2][:, 0:NSM], Qs[:, G * P:(G + 1) * P], kT[:, SEQ:TOK], start=False, stop=True,
                               skip_group_check=True)
                V.close(mm, 3)
                if G == 0:
                    for bb in range(4, NB):
                        turn_k(bb)
                conv_out(CONV_FILL[G + 1])
                pe.wait_ge(probs_ready, 2 * NH + 3 * (G + 1))
                for half in range(2):
                    b = A.open(pe)
                    for q in range(4):
                        pg = 4 * half + q
                        mm = pe.transpose(b[:, q * P:(q + 1) * P], probsS[:, pg * P:(pg + 1) * P], ident)
                    A.close(mm)
                b = A.open(pe)
                A.close(pe.transpose(b[0:NSM, 0:P], probsS[:, PAST:NKEY], ident))
                pe.wait_ge(probsT_ready, 6 + 3 * (G + 1))
                pe.wait_ge(v_landed, 16 * NB * NPG)
                b = V.open(pe)
                for b4 in range(4):
                    bb = 4 * G + b4
                    for pg in range(NPG):
                        pe.matmul(b[32 * b4:32 * b4 + 32, 0:P], probsST[:, pg * P + 32 * b4:pg * P + 32 * b4 + 32],
                                  vpages[:, bb * NPG + pg, :], start=(pg == 0), stop=False)
                    mm = pe.matmul(b[32 * b4:32 * b4 + 32, 0:P], probsST[0:NSM, NPG * P + 32 * b4:NPG * P + 32 * b4 + 32],
                                   zbuf[0:NSM, 2, Z_V:Z_V + P], start=False, stop=True)
                V.close(mm)
                v_done[0] = (d_full, V.n)
                pe.wait_ge(orow_ready, 3 + G)
                b = V.open(pe)
                V.close(pe.transpose(b[:, 0:P], orow[:, 0:P], ident))

            conv_out(DC - sum(CONV_FILL))
            g += 1
            pe.wait_ge(tail_ready, 1)
            b = V.open(pe)
            for c in range(CC):
                mm = pe.transpose(b[0:18, c * P:(c + 1) * P], tails[:, c, :], ident)
            V.close(mm)
            pe.wait_ge(oT_ready, 4)
            w = weights(pe, g)
            for j in range(DC):
                b = V.open(pe)
                for k in range(4):
                    mm = pe.matmul(b[:, 0:TOK], w[:, k, j * P:(j + 1) * P], oT[:, k, 0:TOK], start=(k == 0), stop=(k == 3))
                V.close(mm)
            released[g] = (d_full, V.n)
            g += 1
            pe.wait_ge(mix_ready, 1)
            for _ in range(2):
                w = weights(pe, g)
                for j in range(4):
                    b = V.open(pe)
                    for k in range(DC):
                        mm = pe.matmul(b[:, 0:TOK], w[:, k, j * P:(j + 1) * P], mixT[:, k, :], start=(k == 0), stop=(k == DC - 1))
                    V.close(mm)
                released[g] = (d_full, V.n)
                g += 1
            norm_sum([2 + c for c in range(DC)])
            pe.wait_ge(sub_landed, 16)
            for q in range(4):
                b = A.open(pe)
                for j in range(4):
                    mm = pe.transpose(b[:, j * P:(j + 1) * P], subraw[:, 4 * q + j, :], ident)
                A.close(mm)
            def score_bank(t, q):
                pe.wait_ge(qp_ready, 4 * q + 4)
                b = A.open(pe)
                for j in range(4):
                    hp = 4 * q + j
                    mm = pe.matmul(b[:, j * P:(j + 1) * P], qpT[:, hp, t * P:(t + 1) * P],
                                   subT[:, (hp % 2) * PH + hp // 2, :], start=True, stop=True)
                A.close(mm)

            def turn_h2(t):
                pe.wait_ge(h_ready, 2 * DC + 1)
                for half in range(2):
                    b = A.open(pe)
                    for q in range(4):
                        mm = pe.transpose(b[:, q * P:(q + 1) * P], hT[:, 4 * half + q, t * P:(t + 1) * P], ident)
                    A.close(mm)

            pe.wait_ge(subT_ready, 4)
            for j in range(16):
                if j == H2_BEFORE:
                    turn_h2(0)
                if j % 4 == 0:
                    w = weights(pe, g + j // 4)
                b = A.open(pe)
                for k in range(DC):
                    pe.wait_ge(h_ready, DC + k + 1)
                    mm = pe.matmul(b[:, 0:TOK], w[:, k, (j % 4) * P:(j % 4 + 1) * P], hT[:, k, 0:TOK], start=(k == 0), stop=(k == DC - 1))
                A.close(mm)
                released[g + j // 4] = (a_full, A.n)
                if j in SCORE_AFTER:
                    score_bank(0, SCORE_AFTER.index(j))
            g += 4
            score_bank(0, 3)
            turn_h2(1)
            turn_h2(2)
            for t in range(3):
                for half in range(2):
                    b = A.open(pe)
                    for q in range(4):
                        mm = pe.transpose(b[0:ROWS[t], q * P:(q + 1) * P], xT[:, 4 * half + q, COLS[t]:COLS[t] + ROWS[t]], ident)
                    A.close(mm)
            pe.wait_ge(gspread_ready, 1)
            for s in range(2):
                for half in range(2):
                    b = A.open(pe)
                    for q in range(4):
                        mm = pe.transpose(b[:, q * P:(q + 1) * P], gspread[:, ((4 * half + q) * 2 + s) * P:((4 * half + q) * 2 + s + 1) * P], ident)
                    A.close(mm)
            for q in range(4):
                score_bank(1, q)
            pe.wait_ge(d_free, V.n)

            pe.wait_ge(zeros_ready, 1)
            pe.sem_inc(v_used, UR)
            v_round = 0
            for t in range(3):
                acc = bankD[2 * (t % 2):2 * (t % 2) + 2]
                if t == 2:
                    pe.wait_ge(acc_taken, 1)
                for half in range(2):
                    pe.matmul(acc[half][:, :], zeros[:, 0:P], zeros, start=True, stop=False, skip_group_check=True)
                for rounds in ((SLOTS[0] - CHUNK) // UR, CHUNK // UR) if t == 0 else (SLOTS[t] // UR,):
                    with pe.Fori(0, rounds) as i:
                        for r in range(UR):
                            pe.wait_ge(v_in[r], (i + (v_round + 1)) * 16)
                            pe.wait_ge(diag_ready, (i + v_round) * UR + (r + 1))
                            pe.matmul(acc[0][:, :], diag[:, r % NDG, :], vrows[r][:, 0:512], start=False, stop=False,
                                      skip_group_check=True)
                            pe.matmul(acc[1][:, :], diag[:, r % NDG, :], vrows[r][:, 512:D], start=False, stop=False,
                                      skip_group_check=True).then_inc(v_used, 1)
                    if v_round == 0:
                        for q in range(4):
                            score_bank(2, q)
                    v_round += rounds
                for half in range(2):
                    mm = pe.matmul(acc[half][:, :], zeros[:, 0:P], zeros, start=False, stop=True, skip_group_check=True)
                mm.then_inc(acc_done, 1)
            pe.wait_ge(y_ready, 3)
            pe.wait_ge(acc_taken, 2)
            for half in range(2):
                mm = pe.matmul(bankD[2 + half][0:NSM, :], cv["sum4"], yout[:, half * 512:(half + 1) * 512],
                               start=True, stop=True)
            mm.then_inc(acc_done, 1)

        @block.sync
        def _(sp):
            small = [(b_ada.rearrange("(j p) -> j p", p=P), 0, 48), (norm1_w.rearrange("(j p) -> j p", p=P), 48, 8),
                     (norm2_w.rearrange("(j p) -> j p", p=P), 56, 8), (conv_w.rearrange("w (j p) -> (w j) p", p=P), 64, 12)]
            sp.dma_start(crow[0:1, :], c_prompt).then_inc(in_small, 16)
            sp.dma_start(crow[1:9, :], c_sample).then_inc(in_small, 16)
            sp.dma_start(ctab[:, :], consts).then_inc(in_const, 16)
            for src, a, n in small:
                sp.dma_start(smallrows[a:a + n, :], src).then_inc(in_small, 16)
            sp.dma_start(qkrow[0:1, 0:HD], q_norm_w.rearrange("(a d) -> a d", a=1)).then_inc(in_small, 16)
            sp.dma_start(qkrow[0:1, HD:P], k_norm_w.rearrange("(a d) -> a d", a=1)).then_inc(in_small, 16)
            sp.dma_start(srow[0:16, :], state_conv.rearrange("b j c -> (b j) c")).then_inc(in_small, 16)
            for t in range(2):
                sp.dma_start(xin[:, t, :], x_prompt[t * P:(t + 1) * P, :]).then_inc(in_x, 16)
            sp.dma_start(xin[0:NSM, 2, :], x_sample).then_inc(in_x, 16)

            for g, (name, what) in enumerate(groups):
                for slot in shares[slot_of[g]]:
                    before = [j for j in range(g) if slot_of[j] == slot]
                    if before:
                        sp.wait_ge(*released[before[-1]])
                if name == "attnout":
                    dst = wring[slot_of[g]].rearrange("p (k n) -> p k n", n=D)
                    for n in range(NKV):
                        sp.dma_start(dst[n * HD:(n + 1) * HD, :, :],
                                     attn_rows[n].rearrange("g d m -> d g m")).then_inc(w_landed[slot_of[g]], 16)
                else:
                    k, n, at = what[0][1], sum(part[2] for part in what), 0
                    dst = wring[slot_of[g]][:, 0:k * n].rearrange("p (k n) -> p k n", n=n)
                    for src, _, width in what:
                        sp.dma_start(dst[:, :, at:at + width], src).then_inc(w_landed[slot_of[g]], 16)
                        at += width
                if name == "attnout":
                    sp.wait_ge(oT_ready, 4)
                    sp.wait_ge(kv_out, 16 * 9)
                    sp.dma_start(subraw, peer_sub_keys.rearrange("q h k d -> k (q h) d")).then_inc(sub_landed, 16)
            sp.wait_ge(tail_row, 1)
            sp.dma_start(conv_prompt, tailrows[0:2, :]).then_inc(conv_out_done, 16)
            sp.dma_start(conv_sample.rearrange("b j c -> (b j) c"), tailrows[2:18, :]).then_inc(conv_out_done, 16)
            for t in range(2):
                sp.wait_ge(y_ready, t + 1)
                sp.dma_start(y_prompt[t * P:(t + 1) * P, :], yout[:, :]).then_inc(y_out, 16)
            sp.wait_ge(y_ready, 4)
            sp.dma_start(y_sample, yout[0:NSM, :]).then_inc(y_out, 16)
            sp.wait_ge(y_out, 16 * 3)
            sp.wait_ge(conv_out_done, 16 * 2)

        @block.gpsimd
        def _(pool):
            pool.dma_start(pages[:, :], page_table.rearrange("(a b) g -> a (b g)", a=1)).then_inc(in_pages, 16)
            pool.memset(ones[:, :], 1.0).then_inc(consts_ready, 1)
            pool.memset(Qs[:, :], 0.0).then_inc(consts_ready, 1)
            pool.memset(QIs[:, :, :], 0.0).then_inc(consts_ready, 1)
            pool.memset(uP[:, :, 0:2], 0.0).then_inc(consts_ready, 1)
            pool.wait_ge(in_pages, 16)

            def fetch(dst, src, done, b):
                with pool.Fori(0, NPG) as g:
                    page = pool.value_load(pages[0:1, bass.ds(g + b * NPG, 1)], min_val=0, max_val=NPHYS - 1)
                    pool.dma_start(dst[:, bass.ds(g, 1), :].rearrange("p a d -> p (a d)"),
                                   src[bass.ds(page * PAGE, PAGE), :]).then_inc(done, 16)
            for b in range(NB):
                fetch(index_slot(b), cache_kidx, i_landed[b], b)
            for b in range(NB):
                fetch(vpages[:, b * NPG:(b + 1) * NPG], cache_v, v_landed, b)
            for n, (t, k_out, v_out, i_out) in enumerate((
                    (2, k_sample, v_sample, kidx_sample),
                    (0, k_prompt[0:P, :], v_prompt[0:P, :], kidx_prompt[0:P, :]),
                    (1, k_prompt[P:SEQ, :], v_prompt[P:SEQ, :], kidx_prompt[P:SEQ, :]))):
                pool.wait_ge(rope_done, n + 1)
                r = ROWS[t]
                pool.dma_start(k_out, zbuf[0:r, t, Z_K:Z_K + P]).then_inc(kv_out, 16)
                pool.dma_start(v_out, zbuf[0:r, t, Z_V:Z_V + P]).then_inc(kv_out, 16)
                pool.dma_start(i_out, zbuf[0:r, t, Z_KI:Z_KI + HD]).then_inc(kv_out, 16)
            for b in (0, 1, 2, NB - 1, *range(3, NB - 1)):
                if b == NB - 1:
                    pool.wait_ge(a_ready, 1)
                else:
                    pool.wait_ge(a_full, turned_i[(3, 5, 1)[b]] if b < NK else turned_k[b - NK])
                pages_k, landed, _ = key_slot(b)
                fetch(pages_k, cache_k, landed, b)

            streams = {"u": (urows, ucur, peer_u, u_in, u_used, ucur_done), "v": (vrows, vcur, peer_v, v_in, v_used, vcur_done)}
            done = {"u": 0, "v": 0}
            behind = {}

            def gather(rounds, *parts):
                with pool.Fori(0, rounds // 2) as i:
                    for par in range(2):
                        for kind, t in parts:
                            ring, cur, table, landed, used, cur_done = streams[kind]
                            first = behind.get((kind, t), 0) + par
                            pool.tensor_copy(cur[:, par, :], eidx[:, t, bass.ds(i * (2 * UR) + first * UR, UR)])\
                                .then_inc(cur_done, 1)
                            pool.wait_ge(cur_done, i * 2 + (done[kind] + par + 1))
                            for r in range(UR):
                                pool.wait_ge(used, i * (2 * UR) + ((done[kind] + par) * UR + r + 1))
                                pool.sem_inc(row_asked, 1)
                                pool.indirect_dma_start(ring[r], None, table, bass.IndirectOffsetOnAxis(
                                    ap=cur[:, par, r:r + 1], axis=0)).then_inc(landed[r], 16)
                for kind, t in parts:
                    done[kind] += rounds
                    behind[kind, t] = behind.get((kind, t), 0) + rounds

            step = CHUNK // UR
            pool.wait_ge(*v_done[0])
            pool.wait_ge(routed, 1)
            gather(step, ("u", 0))
            for full, n in released[len(groups) - 1], released[len(groups) - 2]:
                pool.wait_ge(full, n)
            pool.wait_ge(rows_ready, 1)
            pool.wait_ge(routed, 2)
            gather(step, ("v", 0), ("u", 0))
            for n in (3, 4):
                pool.wait_ge(routed, n)
                gather(step, ("v", 0), ("u", 0))
            pool.wait_ge(routed, 5)
            gather(step, ("v", 0), ("u", 1))
            pool.wait_ge(routed, 8)
            gather(3 * step, ("v", 1), ("u", 1))
            pool.wait_ge(routed, 12)
            gather(step, ("v", 1), ("u", 2))
            gather(step, ("v", 2))

        @block.scalar
        def _(act):
            A = Banks(bankA, a_full, a_free)
            L = Lane(act, act_seq)

            def ada(g):
                b = A.take(act)
                L.tell(act.activation(adarow[:, :], b[:, :], ACT.Copy), adarow_ready)
                act.sem_inc(a_free, 1)
                b = A.take(act)
                L.tell(act.activation(modT[:, 4 * g:4 * g + 4, :].rearrange("p j b -> p (j b)"), b[:, 0:36], ACT.Copy), mod_ready)
                act.sem_inc(a_free, 1)

            act.wait_ge(xT_ready, DC)
            L.tell(act.activation(sq, xT[:, :, :].rearrange("p c t -> p (c t)"), ACT.Square), sq_ready)
            act.wait_ge(var_ready, 1)
            L.tell(act.activation(rstd[:, :], rstd[:, :], ACT.Sqrt), sd_ready)
            for g in range(4):
                ada(g)
            for part in (((0, 512),), ((Z_K, 256), (Z_KI, 72)), ((Z_QI, 512),)):
                width = sum(n for _, n in part)
                if part[0][0] == Z_QI:
                    act.sem_inc(qk_ready, 1)
                    act.wait_ge(qk_var, 1)
                    L.tell(act.activation(stat[:, 0:30], stat[:, 0:30], ACT.Sqrt), qk_sd)
                b = A.take(act)
                L.tell(act.activation(adarow[:, 0:width], b[:, 0:width], ACT.Copy), adarow_ready)
                act.sem_inc(a_free, 1)
                for t in range(3):
                    b, at = A.take(act), 0
                    for a, n in part:
                        L.tell(act.activation(zbuf[0:ROWS[t], t, a:a + n], b[0:ROWS[t], at:at + n], ACT.Copy))
                        at += n
                    act.sem_inc(a_free, 1)
            act.sem_inc(z_ready, 1)

            blocks = iter(range(28))

            def fill(n):
                for _ in range(n):
                    j = next(blocks, None)
                    if j is None:
                        return
                    b = A.take(act)
                    if j < 12:
                        L.tell(act.activation((bufX, bufB, bufC)[j // 4][:, j % 4, :], b[:, 0:TOK], ACT.Copy), conv_in)
                    else:
                        L.tell(act.activation(sig[:, j - 12, :], b[:, 0:TOK], ACT.Copy))
                    act.sem_inc(a_free, 1)

            fill(FILL["start"])
            fill(FILL["T2"])
            for t in range(2):
                W = P * (t + 1)
                for hp in range(4):
                    b = A.take(act)
                    if 4 * t + hp >= 2:
                        act.wait_ge(relu_used, 4 * t + hp - 1)
                    dst = relu[:, 0:2 * W] if hp % 2 == 0 else probs[:, 0:2 * W]
                    L.tell(act.activation(dst, b[:, 0:2 * W], ACT.Relu), relu_ready)
                    act.sem_inc(a_free, 1)
                fill(FILL["select"][t])
                for h in range(NH):
                    act.wait_ge(nmax_ready, NH // 2 * t + h // 2 + 1)
                    src = logit_bank[t, h // 2][:, (h % 2) * W:(h % 2 + 1) * W]
                    L.tell(act.activation(probs[:, h * W:(h + 1) * W], src, ACT.Exp, bias=nmax[:, h:h + 1], scale=QSCALE,
                                          accum_out=rsum[:, t, h:h + 1]), probs_ready)
                fill(FILL["softmax"][t])
                for q in range(2 * (t + 1)):
                    b = A.take(act)
                    L.tell(act.activation(probsT[:, q * 512:(q + 1) * 512], b[:, :], ACT.Copy), probsT_ready)
                    act.sem_inc(a_free, 1)
                fill(FILL["next"][t])
            act.wait_ge(oT_ready, 2)

            def copy_i(bb):
                b = A.take(act)
                if bb >= 2:
                    act.wait_ge(ib_used, bb - 1)
                L.tell(act.activation(ibT[:, bb % 2, :], b[:, :], ACT.Copy), ib_ready)
                act.sem_inc(a_free, 1)

            def copy_k(bb):
                for half in range(2):
                    b = A.take(act)
                    if bb >= KB:
                        act.wait_ge(kb_used, bb - KB + 1)
                    L.tell(act.activation(kbT[:, bb % KB, half * 512:(half + 1) * 512], b[:, :], ACT.Copy), kb_ready)
                    act.sem_inc(a_free, 1)

            conv_blocks = iter(range(DC))

            def conv_out(n):
                for j in [next(conv_blocks) for _ in range(n)]:
                    b = A.take(act)
                    L.tell(act.activation((bufX, bufC)[j // 4][:, j % 4, :], b[:, 0:TOK], ACT.Copy), co_ready)
                    act.sem_inc(a_free, 1)

            copy_i(0)
            for bb in range(NB):
                if bb + 1 < NB:
                    copy_i(bb + 1)
            for bb in range(4):
                copy_k(bb)
                fill(2 if bb else 1)
                ada(4 + 2 * bb)
                fill(2)
                ada(5 + 2 * bb)
            L.tell(act.activation(sig[:, :, :].rearrange("p j t -> p (j t)"), sig[:, :, :].rearrange("p j t -> p (j t)"), ACT.Sigmoid),
                   gates_ready)
            conv_out(CONV_FILL[0])
            for G in range(2):
                if G == 0:
                    copy_k(4)
                    copy_k(5)
                act.wait_ge(nmax_ready, NH + G + 1)
                for i, (a, n) in enumerate(span):
                    src = logit_bank[2, G][i][:, 0:n]
                    L.tell(act.activation(probsS[:, a:a + n], src, ACT.Exp, bias=nmax[:, 0:1], scale=QSCALE,
                                          accum_out=rsum[:, 2, 4 * G + i:4 * G + i + 1]), probs_ready)
                if G == 0:
                    copy_k(6)
                    copy_k(7)
                conv_out(CONV_FILL[G + 1])
                for half in range(2):
                    b = A.take(act)
                    if G == 1:
                        act.wait_ge(orow_ready, 3)
                    L.tell(act.activation(probsST[:, half * 512:(half + 1) * 512], b[:, :], ACT.Copy), probsT_ready)
                    act.sem_inc(a_free, 1)
                b = A.take(act)
                L.tell(act.activation(probsST[0:NSM, NPG * P:NPG * P + P], b[0:NSM, 0:P], ACT.Copy), probsT_ready)
                act.sem_inc(a_free, 1)
            conv_out(DC - sum(CONV_FILL))
            for c in range(DC):
                act.wait_ge(x1_ready, c + 1)
                L.tell(act.activation(sq[:, c * TOK:(c + 1) * TOK], xT[:, c, :], ACT.Square), sq_ready)
            act.wait_ge(var_ready, 2)
            L.tell(act.activation(rstd[:, :], rstd[:, :], ACT.Sqrt), sd_ready)
            act.wait_ge(sub_landed, 16)
            for q in range(4):
                b = A.take(act)
                L.tell(act.activation(subT[:, 4 * q:4 * q + 4, :].rearrange("p j k -> p (j k)"), b[:, :], ACT.Copy), subT_ready)
                act.sem_inc(a_free, 1)
            def copy_scores():
                b = A.take(act)
                q = L.count.get(id(s_ready), 0) % 4
                L.tell(act.activation(ssb[:, 4 * q:4 * q + 4, :].rearrange("p j k -> p (j k)"), b[:, :], ACT.Copy), s_ready)
                act.sem_inc(a_free, 1)

            def copy_h2(t):
                for half in range(2):
                    b = A.take(act)
                    L.tell(act.activation(h2tok[:, t, half * 512:(half + 1) * 512], b[:, :], ACT.Copy), h2_ready)
                    act.sem_inc(a_free, 1)

            for j in range(16):
                if j == H2_BEFORE:
                    copy_h2(0)
                b = A.take(act)
                L.tell(act.activation(qpT[:, j, 0:SEQ], b[:, 0:SEQ], ACT.Copy), wait=False)
                L.tell(act.activation(qpT[:, j, SEQ:3 * P].rearrange("p (r t) -> p r t", r=4),
                                      b[:, SEQ:TOK].unsqueeze(1).broadcast_to([P, 4, NSM]), ACT.Copy), qp_ready)
                act.sem_inc(a_free, 1)
                if j in SCORE_AFTER:
                    copy_scores()
            copy_scores()
            copy_h2(1)
            copy_h2(2)
            act.wait_ge(conv_out_done, 32)
            for t in range(3):
                for half in range(2):
                    b = A.take(act)
                    L.tell(act.activation(x1tok[0:ROWS[t], t, half * 512:(half + 1) * 512], b[0:ROWS[t], :], ACT.Copy))
                    act.sem_inc(a_free, 1)
            for s in range(2):
                for half in range(2):
                    b = A.take(act)
                    L.tell(act.activation(g2tok[:, s, half * 512:(half + 1) * 512], b[:, :], ACT.Copy))
                    act.sem_inc(a_free, 1)
            act.sem_inc(rows_ready, 1)
            def scores(t):
                if t:
                    act.wait_ge(s_used, t)
                for q in range(4):
                    copy_scores()

            def gelus(c):
                t, first = CHUNKS[c]
                act.wait_ge(dots_ready, c + 1)
                L.tell(act.activation(gate[:, t, first:first + CHUNK], gate[:, t, first:first + CHUNK], ACT.Exp), exp_done)
                chunk = dots[:, t, first:first + CHUNK]
                L.tell(act.activation(chunk, chunk, ACT.Gelu_apprx_tanh), gelu_done)

            def diagonals(c):
                t, first = CHUNKS[c]
                act.wait_ge(w_ready, c + 1)
                with act.Fori(0, CHUNK // UR) as i:
                    for r in range(UR):
                        act.wait_ge(v_used, (i + c * (CHUNK // UR)) * UR + (r + 1 + UR - NDG))
                        act.activation(diag[:, r % NDG, :], ident, ACT.Copy, scale=dots[:, t, bass.ds(i * UR + (first + r), 1)])\
                           .then_inc(diag_ready, 1)

            for c in range(len(CHUNKS)):
                gelus(c)
                if CHUNKS[c] == (0, SLOTS[0] - CHUNK):
                    scores(2)
                diagonals(c)
                if c == 0:
                    scores(1)

        @block.vector
        def _(dve):
            V = Banks(bankD, d_full, d_free)
            L = Lane(dve, dve_seq)
            tt, ts, cp = dve.tensor_tensor, dve.tensor_scalar, dve.tensor_copy

            def free():
                dve.sem_inc(d_free, 1)

            dve.wait_ge(in_const, 16)
            L.tell(cp(ident_bf[:, :], ident))
            L.tell(cp(rep_bf[:, :], cv["rep"][0:NSM, :]))
            dve.wait_ge(consts_ready, 4)
            L.tell(cp(smallT[:, :], V.take(dve)[:, 0:76])); free()
            L.tell(dve.memset(cT[:, :, :], 0.0))
            L.tell(cp(cT[:, :, 0:9], V.take(dve)[:, 0:72].rearrange("p (c b) -> p c b", b=9)), cT_ready); free()
            L.tell(cp(stateT[:, :, :].rearrange("p c b -> p (c b)"), V.take(dve)[:, 0:64])); free()
            L.tell(cp(qkw[:, :], V.take(dve)[:, 0:P])); free()
            for c in range(DC):
                L.tell(cp(xT[:, c, :], V.take(dve)[:, 0:TOK]), xT_ready); free()

            def bias(a, e):
                dve.wait_ge(mod_ready, e // 4)
                L.tell(tt(modT[:, a:e, :], modT[:, a:e, :], smallT[:, a:e].unsqueeze(2).broadcast_to([P, e - a, 9]), ALU.add))

            def norm_scale(scale, w):
                L.tell(ts(ab[:, :, :], modT[:, scale:scale + DC, :], 1.0, None, ALU.add))
                L.tell(tt(ab[:, :, :], ab[:, :, :], smallT[:, w:w + DC].unsqueeze(2).broadcast_to([P, DC, 9]), ALU.mult))

            def norm_unit(n):
                b = V.take(dve)
                L.tell(ts(rstd[:, :], b[:, 0:TOK], 1.0 / D, EPS, ALU.mult, ALU.add), var_ready); free()
                dve.wait_ge(sd_ready, n)
                L.tell(dve.reciprocal(rstd[:, :], rstd[:, :]))
                L.tell(tt(hT[:, :, 0:TOK], xT[:, :, :], rstd[:, :].unsqueeze(1).broadcast_to([P, DC, TOK]), ALU.mult))

            def norm_shift(shift):
                hs = hT[:, :, SEQ:TOK].rearrange("p c (b s) -> p c b s", s=NS)
                L.tell(tt(hs, hs, ab[:, :, 1:9].unsqueeze(3).broadcast_to([P, DC, NB, NS]), ALU.mult))
                L.tell(tt(hs, hs, modT[:, shift:shift + DC, 1:9].unsqueeze(3).broadcast_to([P, DC, NB, NS]), ALU.add))
                for c in range(DC):
                    L.tell(ts(hT[:, c, 0:SEQ], hT[:, c, 0:SEQ], ab[:, c, 0:1], modT[:, shift + c, 0:1], ALU.mult, ALU.add),
                           h_ready, wait=False)

            norm_unit(1)
            bias(0, 16)
            norm_scale(8, 48)
            norm_shift(0)

            L.tell(dve.memset(qTz, 0.0), wait=False)
            L.tell(dve.memset(qiTz, 0.0), wait=False)
            L.tell(dve.memset(stat[:, 0:30], 1.0))
            def conv(c):
                dve.wait_ge(conv_in, 9 + c)
                L.tell(tt(uP[:, c, 2:SEQ + 2], bufX[:, c, 0:SEQ], bufC[:, c, 0:SEQ], ALU.mult), wait=False)
                L.tell(cp(uS[:, c, :, 0:2], stateT[:, c, :].rearrange("p (b j) -> p b j", j=2)), wait=False)
                L.tell(tt(uS[:, c, :, 2:6], bufX[:, c, SEQ:TOK].rearrange("p (b s) -> p b s", s=NS),
                          bufC[:, c, SEQ:TOK].rearrange("p (b s) -> p b s", s=NS), ALU.mult))
                L.tell(cp(tails[:, c, 0:2], uP[:, c, SEQ:SEQ + 2]), wait=False)
                L.tell(cp(tails[:, c, 2:18].rearrange("p (b j) -> p b j", j=2), uS[:, c, :, 4:6]), wait=False)
                for u, y, n in ((uP[:, c], bufX[:, c, 0:SEQ], SEQ), (uS[:, c], bufX[:, c, SEQ:TOK].rearrange("p (b s) -> p b s", s=NS), NS)):
                    tap = [u[:, j:j + n] if n == SEQ else u[:, :, j:j + n] for j in range(3)]
                    wc = [smallT[:, 64 + 4 * j + c:65 + 4 * j + c] for j in range(3)]
                    L.tell(ts(y, tap[2], wc[2], None, ALU.mult))
                    L.tell(dve.scalar_tensor_tensor(y, tap[0], wc[0], y, ALU.mult, ALU.add))
                    L.tell(dve.scalar_tensor_tensor(y, tap[1], wc[1], y, ALU.mult, ALU.add))
                L.tell(tt(aT[:, c, :], bufB[:, c, :], bufX[:, c, :], ALU.mult))


            def rotate(z, a, nh, t, r):
                x1 = z[:, a:a + nh * HD].rearrange("p (h d) -> p h d", d=HD)[:, :, 0:32]
                x2 = z[:, a:a + nh * HD].rearrange("p (h d) -> p h d", d=HD)[:, :, 32:64]
                cs = cv["cos"][0:r, 32 * t:32 * t + 32].unsqueeze(1).broadcast_to([r, nh, 32])
                sn = cv["sin"][0:r, 32 * t:32 * t + 32].unsqueeze(1).broadcast_to([r, nh, 32])
                t1, t2 = (rope[i][0:r, 0:nh * 32].rearrange("p (h d) -> p h d", d=32) for i in range(2))
                L.tell(tt(t1, x2, sn, ALU.mult), wait=False)
                L.tell(tt(t2, x1, sn, ALU.mult))
                L.tell(tt(x1, x1, cs, ALU.mult), wait=False)
                L.tell(tt(x2, x2, cs, ALU.mult))
                L.tell(tt(x1, x1, t1, ALU.subtract), wait=False)
                L.tell(tt(x2, x2, t2, ALU.add))

            def heads(t):
                return zbuf[0:ROWS[t], t, 0:10 * HD].rearrange("p (h d) -> p h d", d=HD), stat[0:ROWS[t], 10 * t:10 * t + 10]

            dve.wait_ge(qk_ready, 1)
            for t in range(3):
                zq, st = heads(t)
                sqv = probs[0:ROWS[t], 0:10 * HD].rearrange("p (h d) -> p h d", d=HD)
                L.tell(tt(sqv, zq, zq, ALU.mult))
                L.tell(dve.tensor_reduce(st, sqv, AX, ALU.add))
            L.tell(ts(stat[:, 0:30], stat[:, 0:30], 1.0 / HD, EPS, ALU.mult, ALU.add), qk_var)
            dve.wait_ge(qk_sd, 1)
            L.tell(dve.reciprocal(stat[:, 0:30], stat[:, 0:30]))
            for t in (2, 0, 1):
                r = ROWS[t]
                zq, st = heads(t)
                L.tell(tt(zq, zq, st.unsqueeze(2).broadcast_to([r, 10, HD]), ALU.mult))
                L.tell(tt(zq[:, 0:8], zq[:, 0:8], qkw[0:r, 0:HD].unsqueeze(1).broadcast_to([r, 8, HD]), ALU.mult), wait=False)
                L.tell(tt(zq[:, 8:10], zq[:, 8:10], qkw[0:r, HD:P].unsqueeze(1).broadcast_to([r, 2, HD]), ALU.mult))
                rotate(zbuf[0:r, t, :], 0, 10, t, r)
            dve.wait_ge(z_ready, 1)
            for n, t in enumerate((2, 0, 1)):
                r, z = ROWS[t], zbuf[0:ROWS[t], t, :]
                rotate(z, Z_QI, 9, t, r)
                L.tell(cp(orow[0:r, :].rearrange("p (g n d) -> p n g d", g=NG, n=NKV),
                          z[:, 0:512].rearrange("p (n g d) -> p n g d", n=NKV, g=NG)), wait=False)
                L.tell(cp(kidup[0:r, 0:HD], z[:, Z_KI:Z_KI + HD]), wait=False)
                L.tell(cp(kidup[0:r, HD:P], z[:, Z_KI:Z_KI + HD]), wait=False)
                L.tell(ts(wis[0:r, t, :], z[:, Z_WI:Z_WI + NH], IDX_SCALE, None, ALU.mult), rope_done)

                b = V.take(dve)
                bq = b[:, 0:NG * r].rearrange("p (g t) -> p g t", t=r)
                if t == 2:
                    for nn in range(NKV):
                        s, e = nn * HD, (nn + 1) * HD
                        dst = Qs[s:e, :].rearrange("p (b h s) -> p b h s", h=NH, s=NS)[:, :, nn * NG:(nn + 1) * NG, :]
                        for gg in range(NG):
                            L.tell(cp(dst[:, :, gg, :], bq[s:e, gg, :].rearrange("p (b s) -> p b s", s=NS)))
                    free()
                else:
                    for nn in range(NKV):
                        s, e = nn * HD, (nn + 1) * HD
                        L.tell(cp(qTz[s:e, nn * NG:(nn + 1) * NG, :], bq[s:e]))
                    free()
                b = V.take(dve)
                bi = b[:, 0:4 * r].rearrange("p (c t) -> p c t", t=r)
                for par in range(2):
                    s, e = par * HD, (par + 1) * HD
                    if t == 2:
                        for v in range(2):
                            dst = QIs[v * HD:(v + 1) * HD, v, :].rearrange("p (b h s) -> p b h s", h=NH, s=NS)
                            for c in range(4):
                                L.tell(cp(dst[:, :, 2 * c + par, :], bi[s:e, c, :].rearrange("p (b s) -> p b s", s=NS)))
                    else:
                        L.tell(cp(qiTz[s:e].rearrange("p (c q) t -> p c q t", q=2)[:, :, par, :], bi[s:e]))
                free()
                b = V.take(dve)
                L.tell(cp(kT[:, COLS[t]:COLS[t] + r], b[:, 0:r]), wait=False)
                L.tell(cp(kiT[:, COLS[t]:COLS[t] + r], b[:, P:P + r]), qT_ready)
                free()
                if t == 2:
                    b = V.take(dve)
                    for G in range(2):
                        L.tell(tt(stat[:, 16:24], b[:, NH * G:NH * G + NH], cv["headsel"], ALU.mult))
                        L.tell(dve.tensor_reduce(wrow[:, G:G + 1], stat[:, 16:24], AX, ALU.add))
                        L.tell(ts(wsel[:, G, :], cv["repT"][:, G * NSM:(G + 1) * NSM], wrow[:, G:G + 1], None, ALU.mult))
                    dve.sem_inc(wsel_ready, 1)
                    free()
                    continue

                W = P * (t + 1)
                L.tell(cp(scP[:, 0:W], cv["causal0"] if t == 0 else cv["causal1"]))
                for hp in range(4):
                    dve.wait_ge(relu_ready, 4 * t + hp + 1)
                    src = relu if hp % 2 == 0 else probs
                    for j in range(2):
                        L.tell(dve.scalar_tensor_tensor(scP[:, 0:W], src[:, j * W:(j + 1) * W],
                                                        wis[:, t, 2 * hp + j:2 * hp + j + 1], scP[:, 0:W], ALU.mult, ALU.add))
                    dve.sem_inc(relu_used, 1)
                src = scP
                for _ in range(TOPK_P // 8):
                    L.tell(dve.max(best[:, :], src[:, 0:W]))
                    L.tell(dve.match_replace(workP[:, 0:W], best[:, :], src[:, 0:W], TAKEN))
                    src = workP
                L.tell(ts(workP[:, 0:W], workP[:, 0:W], -1e35, NEG, ALU.is_gt, ALU.mult))
                L.tell(tt(mbP[:, 0:W], workP[:, 0:W], cv["causal0"] if t == 0 else cv["causal1"], ALU.add), mb_ready)
                for hp in range(4):
                    b = V.take(dve)
                    L.tell(dve.tensor_reduce(stat[:, 32 + 2 * hp:34 + 2 * hp], b[:, 0:2 * W].rearrange("p (h k) -> p h k", k=W),
                                             AX, ALU.max))
                    L.tell(ts(nmax[:, 2 * hp:2 * hp + 2], stat[:, 32 + 2 * hp:34 + 2 * hp], -QSCALE, None, ALU.mult), nmax_ready)
                if t == 1:
                    conv(0)
                    conv(1)
                dve.wait_ge(probs_ready, NH * (t + 1))
                dve.sem_inc(d_free, 4)
                L.tell(dve.reciprocal(rinv[:, :], rsum[:, t, :]))
                b = V.take(dve)
                L.tell(tt(orow.rearrange("p (g n d) -> p n g d", g=NG, n=NKV),
                          b[:, :].rearrange("p (n g d) -> p n g d", n=NKV, g=NG),
                          rinv[:, :].rearrange("p (n g) -> p n g", n=NKV).unsqueeze(3).broadcast_to([P, NKV, NG, HD]), ALU.mult),
                       orow_ready)
                free()
                b = V.take(dve)
                L.tell(cp(oT[:, :, COLS[t]:COLS[t] + P], b[:, :].rearrange("p (g t) -> p g t", t=P)), oT_ready)
                free()

            for G in range(2):
                conv(2 + G)
                if G == 1:
                    dve.sem_inc(tail_ready, 1)
                    dve.sem_inc(a_ready, 1)
                for i, (a, n) in enumerate(span):
                    b = V.take(dve)
                    L.tell(ts(reluS[:, G, a:a + n], b[:, 0:n], 0.0, None, ALU.max), reluS_ready)
                    free()
            for a, n in span:
                b = V.take(dve)
                if a < 1024:
                    L.tell(cp(scS[0:NSM, a:a + n], b[0:NSM, 0:n]))
                else:
                    L.tell(tt(scS[0:NSM, a:a + n], b[0:NSM, 0:n], cv["newbias"][0:NSM, :], ALU.add))
                free()
            seq0, per_step = L.count[id(dve_seq)], 8
            with dve.Fori(0, TOPK_S // 8 // per_step) as i:
                for n in range(per_step):
                    if n:
                        dve.wait_ge(dve_seq, i * (2 * per_step) + (seq0 + 2 * n))
                        dve.sem_inc(round_begun, 1)
                    dve.max(best[0:NSM, :], scS[0:NSM, :]).then_inc(dve_seq, 1)
                    dve.wait_ge(dve_seq, i * (2 * per_step) + (seq0 + 2 * n + 1))
                    dve.sem_inc(round_begun, 1)
                    dve.match_replace(scS[0:NSM, :], best[0:NSM, :], scS[0:NSM, :], TAKEN).then_inc(dve_seq, 1)
                dve.wait_ge(dve_seq, i * (2 * per_step) + (seq0 + 2 * per_step))
            L.count[id(dve_seq)] = seq0 + 2 * (TOPK_S // 8)
            L.tell(ts(mbS[:, :], scS[0:NSM, :], -1e35, NEG, ALU.is_gt, ALU.mult), mbS_ready)
            bias(16, 48)

            for G in range(2):
                bs = [V.take(dve) for _ in range(3)]
                for i, (a, n) in enumerate(span):
                    L.tell(dve.tensor_reduce(stat[:, 40 + i:41 + i], bs[i][:, 0:n], AX, ALU.max))
                L.tell(dve.tensor_reduce(stat[:, 43:44], stat[:, 40:43], AX, ALU.max))
                L.tell(ts(nmax[:, 0:1], stat[:, 43:44], -QSCALE, None, ALU.mult), nmax_ready)
                dve.wait_ge(probs_ready, 2 * NH + 3 * (G + 1))
                dve.sem_inc(d_free, 3)
                L.tell(dve.tensor_reduce(stat[:, 44:45], rsum[:, 2, 4 * G:4 * G + 3], AX, ALU.add))
                L.tell(dve.reciprocal(rinv[:, 0:1], stat[:, 44:45]))
                b = V.take(dve)
                L.tell(ts(orow[:, 0:P], b[:, 0:P], rinv[:, 0:1], None, ALU.mult), orow_ready)
                free()
                b = V.take(dve)
                for nn in range(NKV):
                    s, e = nn * HD, (nn + 1) * HD
                    src = b[s:e, 0:P].rearrange("p (b h s) -> p b h s", h=NH, s=NS)[:, :, nn * NG:(nn + 1) * NG, :]
                    for gg in range(NG):
                        L.tell(cp(oT[s:e, gg, SEQ + 16 * G:SEQ + 16 * G + 16].rearrange("p (b s) -> p b s", s=NS), src[:, :, gg, :]))
                free()
                dve.sem_inc(oT_ready, 1)

            b = V.take(dve)
            L.tell(cp(tailrows[:, :], b[0:18, :]), tail_row)
            free()
            dve.wait_ge(gates_ready, 1)
            dve.wait_ge(co_ready, DC)
            for i, src in enumerate((bufX, bufC)):
                L.tell(tt(sig[:, 4 * i:4 * i + 4, :], sig[:, 4 * i:4 * i + 4, :], src, ALU.mult))
            for j in range(DC):
                b = V.take(dve)
                L.tell(tt(sig[:, 8 + j, :], sig[:, 8 + j, :], b[:, 0:TOK], ALU.mult))
                free()
                L.tell(tt(mixT[:, j, :], sig[:, j, :], sig[:, 8 + j, :], ALU.add))
            dve.sem_inc(mix_ready, 1)
            for j in range(DC):
                b = V.take(dve)
                xs = xT[:, j, SEQ:TOK].rearrange("p (b s) -> p b s", s=NS)
                tmp = rstd[:, 0:NSM].rearrange("p (b s) -> p b s", s=NS)
                L.tell(dve.scalar_tensor_tensor(xT[:, j, 0:SEQ], b[:, 0:SEQ], modT[:, 16 + j, 0:1], xT[:, j, 0:SEQ], ALU.mult, ALU.add),
                       wait=False)
                L.tell(tt(tmp, b[:, SEQ:TOK].rearrange("p (b s) -> p b s", s=NS),
                          modT[:, 16 + j, 1:9].unsqueeze(2).broadcast_to([P, NB, NS]), ALU.mult))
                L.tell(tt(xs, xs, tmp, ALU.add), x1_ready)
                free()
            norm_scale(32, 56)
            norm_unit(2)
            norm_shift(24)
            L.tell(cp(hT[:, :, TOK:3 * P].rearrange("p c (r t) -> p c r t", t=NSM),
                      hT[:, :, SEQ:TOK].unsqueeze(2).broadcast_to([P, DC, 3, NSM])), h_ready)
            dve.wait_ge(*v_done[0])
            gs = gspread.rearrange("p (c s t) -> p c s t", s=2, t=P)
            L.tell(cp(gs[:, :, 0, :], modT[:, 40:48, 0:1].broadcast_to([P, DC, P])), wait=False)
            for r in range(4):
                L.tell(cp(gs[:, :, 1, 32 * r:32 * r + 32].rearrange("p c (b s) -> p c b s", s=NS),
                          modT[:, 40:48, 1:9].unsqueeze(3).broadcast_to([P, DC, NB, NS])), wait=(r == 3))
            dve.sem_inc(gspread_ready, 1)

            def top16(n, values, best, place):
                for i in range(n):
                    L.tell(dve.max(best[i][:, 0:8], values[i]), wait=False)
                for i in range(n):
                    L.done_but(n - 1)
                    L.tell(dve.max_index(place[i][:, 0:8], best[i][:, 0:8], values[i]), wait=False)
                for i in range(n):
                    L.done_but(n - 1)
                    L.tell(dve.match_replace(values[i], best[i][:, 0:8], values[i], TAKEN), wait=False)
                for i in range(n):
                    L.done_but(n - 1)
                    L.tell(dve.max(best[i][:, 8:16], values[i]), wait=False)
                for i in range(n):
                    L.done_but(n - 1)
                    L.tell(dve.max_index(place[i][:, 8:16], best[i][:, 8:16], values[i]), wait=False)
                L.done_but(0)

            def route(t):
                wide = [P, 2, PTOP, PTOP]
                for h in range(0, PH, 2):
                    cand, onehot = route_work(early=(t == 0 and h < 4))
                    dve.wait_ge(s_ready, 4 * t + h // 2 + 1)
                    four = range(2 * h, 2 * h + 4)
                    top16(4, [ssb[:, hp, :] for hp in four], [topv[:, hp, :] for hp in four], [topi[:, hp, :] for hp in four])
                    if h == PH - 2:
                        dve.sem_inc(s_used, 1)
                    yield
                    L.tell(cp(topf[:, 2 * h:2 * h + 4, :], topi[:, 2 * h:2 * h + 4, :]), wait=False)
                    tv = topv[:, 2 * h:2 * h + 4, :].rearrange("p (h q) k -> p h q k", q=2)
                    tf = topf[:, 2 * h:2 * h + 4, :].rearrange("p (h q) k -> p h q k", q=2)
                    L.tell(tt(cand, tv[:, :, 0, :].unsqueeze(3).broadcast_to(wide), tv[:, :, 1, :].unsqueeze(2).broadcast_to(wide), ALU.add))
                    top16(2, [cand[:, e].rearrange("p i j -> p (i j)") for e in range(2)],
                          [tops[:, h + e, :] for e in range(2)], [posu[:, h + e, :] for e in range(2)])
                    pu, pf = posu[:, h:h + 2, :], posf[:, :, h:h + 2, :]
                    L.tell(ts(posq[:, 0], pu, 4, None, ALU.logical_shift_right), wait=False)
                    L.tell(ts(posq[:, 1], pu, 15, None, ALU.bitwise_and), wait=False)
                    for q in range(2):
                        L.done_but(1)
                        L.tell(cp(pf[:, q], posq[:, q]), wait=False)
                    for q in range(2):
                        L.done_but(1)
                        L.tell(tt(onehot[:, q], pf[:, q].unsqueeze(3).broadcast_to(wide),
                                  cv["iota"].unsqueeze(1).unsqueeze(1).broadcast_to(wide), ALU.is_equal), wait=False)
                    for q in range(2):
                        L.done_but(1)
                        L.tell(tt(onehot[:, q], onehot[:, q], tf[:, :, q, :].unsqueeze(2).broadcast_to(wide), ALU.mult), wait=False)
                    for q in range(2):
                        L.done_but(1)
                        L.tell(dve.tensor_reduce(pick[:, q, h:h + 2, :], onehot[:, q], AX, ALU.add), wait=False)
                    L.done_but(0)
                    L.tell(cp(gsm[:, 0, h:h + 2], tops[:, h:h + 2, 0:1].rearrange("p h k -> p (h k)")), wait=False)
                    L.tell(dve.scalar_tensor_tensor(pick[:, 0, h:h + 2], pick[:, 0, h:h + 2], float(PK), pick[:, 1, h:h + 2],
                                                    ALU.mult, ALU.add))
                    L.tell(tt(tops[:, h:h + 2, :], tops[:, h:h + 2, :],
                              gsm[:, 0, h:h + 2].unsqueeze(2).broadcast_to([P, 2, PTOP]), ALU.subtract), wait=False)
                    s, e, at = (0, P, h * PTOP) if t < 2 else (16 * h, 16 * h + 32, 0)
                    L.tell(cp(eidx[s:e, t, at:at + 32], pick[s:e, 0, h:h + 2].rearrange("p h k -> p (h k)")))
                    L.tell(cp(gate[s:e, t, at:at + 32], tops[s:e, h:h + 2, :].rearrange("p h k -> p (h k)")))
                    dve.sem_inc(routed, 1)
                    yield

            dve.sem_inc(u_used, UR)
            u_round = 0

            def output(t):
                dve.wait_ge(acc_done, t + 1)
                if t:
                    dve.wait_ge(y_out, 16 * t)
                acc = bankD[2 * (t % 2):2 * (t % 2) + 2]
                for half in range(2):
                    s, e = half * 512, (half + 1) * 512
                    if t < 2:
                        L.tell(tt(yout[:, s:e], acc[half][:, :], g2tok[:, 0, s:e], ALU.mult))
                    else:
                        L.tell(cp(yout[:, s:e], acc[half][:, :]))
                dve.sem_inc(acc_taken, 1)
                if t < 2:
                    L.tell(tt(yout, yout, x1tok[:, t, :], ALU.add))
                dve.sem_inc(y_ready, 1)

            def dot_rounds(t, slot, rounds):
                nonlocal u_round
                with dve.Fori(0, rounds) as i:
                    for r in range(UR):
                        dve.wait_ge(u_in[r], (i + (u_round + 1)) * 16)
                        dve.tensor_tensor_reduce(out=urows[r], in0=urows[r], in1=h2tok[:, t, :], scale=1.0, scalar=0.0,
                                                 op0=ALU.mult, op1=ALU.add, accum_out=dcur[:, r:r + 1]).then_inc(u_used, 1)
                    dve.wait_ge(u_used, (i + (u_round + 2)) * UR)
                    dve.tensor_copy(dots[:, t, bass.ds(i * UR + slot, UR)], dcur[:, :]).then_inc(dcur_copied, 1)
                    dve.wait_ge(dcur_copied, i + (u_round + 1))
                u_round += rounds

            router = route(0)
            next(router)
            next(router)
            dve.wait_ge(h2_ready, 2)
            dot_rounds(0, 0, 1)
            next(router)
            next(router)
            dot_rounds(0, UR, 1)
            dot_rounds(0, 2 * UR, 2)
            for full, n in released[len(groups) - 1], released[len(groups) - 2]:
                dve.wait_ge(full, n)
            L.tell(dve.memset(zeros, 0.0), zeros_ready)
            for c, (t, first) in enumerate(CHUNKS):
                if first == 0:
                    dve.wait_ge(h2_ready, 2 * t + 2)
                if (t, first) in ((0, 2 * CHUNK), (1, 0)):
                    router = route(t + 1)
                for half in range(2):
                    if c:
                        dot_rounds(t, first + half * CHUNK // 2, CHUNK // UR // 2)
                    if half == 1:
                        dve.sem_inc(dots_ready, 1)
                    if c:
                        next(router, None)
                        next(router, None)
                dve.wait_ge(exp_done, c + 1)
                gv = gate[:, t, first:first + CHUNK].rearrange("p (h k) -> p h k", k=PTOP)
                L.tell(dve.tensor_reduce(gsm[:, 1, 0:2], gv, AX, ALU.add))
                L.tell(dve.reciprocal(gsm[:, 1, 0:2], gsm[:, 1, 0:2]))
                L.tell(tt(gv, gv, gsm[:, 1, 0:2].unsqueeze(2).broadcast_to([P, 2, PTOP]), ALU.mult))
                dve.wait_ge(gelu_done, c + 1)
                e = first + CHUNK
                L.tell(tt(dots[:, t, first:e], dots[:, t, first:e], gate[:, t, first:e], ALU.mult), w_ready)
                if c == len(CHUNKS) - 3:
                    output(0)
            output(1)
            output(2)
            dve.wait_ge(acc_done, 4)
            for half in range(2):
                s, e = half * 512, (half + 1) * 512
                L.tell(tt(yout[0:NSM, s:e], bankD[2 + half][0:NSM, :], g2tok[0:NSM, 1, s:e], ALU.mult))
                L.tell(tt(yout[0:NSM, s:e], yout[0:NSM, s:e], x1tok[0:NSM, 2, s:e], ALU.add))
            dve.sem_inc(y_ready, 1)


def kernel(**inputs):
    import concourse.bacc as bacc
    from concourse.bass_utils import run_bass_kernel_spmd

    nc = bacc.Bacc("TRN2", target_bir_lowering=False, num_devices=1)
    arrays = {name: np.ascontiguousarray(inputs[name]) for name in INPUTS}
    arrays["consts"] = const_table()
    ap = {}
    for name, a in arrays.items():
        t = nc.dram_tensor(name, a.shape, mybir.dt.from_np(a.dtype), kind="ExternalInput").ap()
        if name in LAYERED or name in ("x_prompt",):
            t = t[0]
        if name in ("cache_k", "cache_v"):
            t = t.rearrange("g p n d -> (g p) (n d)")
        if name == "cache_kidx":
            t = t.rearrange("g p d -> (g p) d")
        if name == "x_sample":
            t = t.rearrange("b s d -> (b s) d")
        ap[name] = t
    outs = {}
    for name, shape, view in OUTPUTS:
        t = nc.dram_tensor("out_" + name, shape, F32, kind="ExternalOutput").ap()
        outs[name] = t.rearrange(view[0]) if view[0] else t
        if view[1]:
            outs[name] = outs[name][0]
    layer_program(nc, **ap, **outs)
    r = run_bass_kernel_spmd(nc, [arrays], core_ids=[0])
    return tuple(r.results[0]["out_" + name] for name, _, _ in OUTPUTS)
```
